# Optimizing a Trainium2 kernel written in Bass

```python
import math
import jax
import jax.numpy as jnp
from jax import lax
import numpy as np

D_MODEL = 1024
BATCH = 1
SEQ = 512
DEPTH = 2

GRID_W = 64
CTX_LEN = 256
HEAD_DIM = 64
N_Q_HEADS = 8
N_KV_HEADS = 2
GQA_GROUP = N_Q_HEADS // N_KV_HEADS
ROPE_THETA = 10000.0
Q_BLOCK = 128
DN_HEADS = 4
DN_HEAD_DIM = 64
CONV_K = 5
HG_HEADS = 4
HG_HEAD_DIM = 64
CHUNK = 64
N_EXPERTS = 16
D_EXPERT = 1408
CAPACITY_FACTOR = 2
MOD_INIT = 0.5
ATTN_Q_W = N_Q_HEADS * HEAD_DIM
ATTN_KV_W = N_KV_HEADS * HEAD_DIM
DN_W = DN_HEADS * DN_HEAD_DIM
HG_W = HG_HEADS * HG_HEAD_DIM
IN_COLS = ATTN_Q_W + 2 * ATTN_KV_W + 4 * DN_W + 4 * DN_HEADS + 5 * HG_W

kernel_name = 'hybrid_prefix_dit_trunk'

def _split_cols(p):
    names = ('attn_q', 'attn_k', 'attn_v', 'dn_qkv', 'dn_z', 'dn_beta', 'dn_a',
             'hg_q', 'hg_f', 'hg_i', 'hg_g')
    sizes = (ATTN_Q_W, ATTN_KV_W, ATTN_KV_W, 3 * DN_W, DN_W, 2 * DN_HEADS, 2 * DN_HEADS,
             HG_W, 2 * HG_W, HG_W, HG_W)
    out = {}
    off = 0
    for n, s in zip(names, sizes):
        out[n] = p[..., off:off + s]
        off += s
    return out

def _rms(x, eps=1e-6):
    xf = x.astype(jnp.float32)
    return (xf * lax.rsqrt(jnp.mean(xf * xf, axis=-1, keepdims=True) + eps)).astype(x.dtype)

def _l2norm(x, eps=1e-6):
    return x * lax.rsqrt(jnp.sum(x * x, axis=-1, keepdims=True) + eps)

def _modulate(x, shift, scale):
    return _rms(x) * (1 + scale) + shift

def _heads(t, n):
    b, s, w = t.shape
    return t.reshape(b, s, n, w // n).transpose(0, 2, 1, 3)

def _merge_heads(t):
    b, h, s, d = t.shape
    return t.transpose(0, 2, 1, 3).reshape(b, s, h * d)

def _rope_tables(n_tokens, dtype):
    rows = n_tokens // GRID_W
    row = jnp.repeat(jnp.arange(rows, dtype=jnp.float32), GRID_W)
    col = jnp.tile(jnp.arange(GRID_W, dtype=jnp.float32), rows)
    n_freq = HEAD_DIM // 4
    inv_freq = ROPE_THETA ** (-jnp.arange(n_freq, dtype=jnp.float32) / n_freq)
    ang_r = row[:, None] * inv_freq
    ang_c = col[:, None] * inv_freq
    return (jnp.cos(ang_r).astype(dtype), jnp.sin(ang_r).astype(dtype),
            jnp.cos(ang_c).astype(dtype), jnp.sin(ang_c).astype(dtype))

def _rope_axis(x, cos, sin):
    x1, x2 = jnp.split(x, 2, axis=-1)
    return jnp.concatenate([x1 * cos - x2 * sin, x1 * sin + x2 * cos], axis=-1)

def _rope2d(x, rope):
    cr, sr, cc, sc = rope
    xr, xc = jnp.split(x, 2, axis=-1)
    return jnp.concatenate([_rope_axis(xr, cr, sr), _rope_axis(xc, cc, sc)], axis=-1)

def _attend(q, k, v):
    s = jnp.einsum('bngqd,bntd->bngqt', q, k).astype(jnp.float32)
    p = jax.nn.softmax(s, axis=-1).astype(v.dtype)
    return jnp.einsum('bngqt,bntd->bngqd', p, v)

def _attention_group(cl, cc, q_norm, k_norm, rope, ctx_out):
    def q_heads(cols, rotate):
        q = _rms(_heads(cols['attn_q'], N_Q_HEADS)) * q_norm
        if rotate:
            q = _rope2d(q, rope)
        b, _, t, _ = q.shape
        return (q * HEAD_DIM ** -0.5).reshape(b, N_KV_HEADS, GQA_GROUP, t, HEAD_DIM)

    def kv_heads(cols, rotate):
        k = _rms(_heads(cols['attn_k'], N_KV_HEADS)) * k_norm
        if rotate:
            k = _rope2d(k, rope)
        return k, _heads(cols['attn_v'], N_KV_HEADS)

    ql = q_heads(cl, True)
    kl, vl = kv_heads(cl, True)
    kc, vc = kv_heads(cc, False)
    k_all = jnp.concatenate([kc, kl], axis=2)
    v_all = jnp.concatenate([vc, vl], axis=2)
    b, _, _, s, _ = ql.shape
    nb = s // Q_BLOCK
    qb = jnp.moveaxis(ql.reshape(b, N_KV_HEADS, GQA_GROUP, nb, Q_BLOCK, HEAD_DIM), 3, 0)
    ob = lax.map(lambda qq: _attend(qq, k_all, v_all), qb)
    o_lat = jnp.moveaxis(ob, 0, 3).reshape(b, N_Q_HEADS, s, HEAD_DIM)
    out_lat = _merge_heads(o_lat)
    out_ctx = None
    if ctx_out:
        qc = q_heads(cc, False)
        oc = _attend(qc, kc, vc).reshape(b, N_Q_HEADS, -1, HEAD_DIM)
        out_ctx = _merge_heads(oc)
    return out_lat, out_ctx

def _short_conv(t, w):
    k, ch = w.shape
    y = lax.conv_general_dilated(t, w.astype(t.dtype)[:, None, :], window_strides=(1,),
                                 padding=[(k // 2, k // 2)],
                                 dimension_numbers=('NWC', 'WIO', 'NWC'),
                                 feature_group_count=ch)
    return jax.nn.silu(y)

def _to_chunks(t):
    b, h, s = t.shape[:3]
    t = t.reshape((b, h, s // CHUNK, CHUNK) + t.shape[3:])
    return jnp.moveaxis(t, 2, 0)

def _chunk_scan(step, xs, s0):
    s_final, o = lax.scan(step, s0, tuple(_to_chunks(t) for t in xs))
    n, b, h, c, d = o.shape
    return jnp.moveaxis(o, 0, 2).reshape(b, h, n * c, d), s_final

def _flip_time(xs):
    return tuple(jnp.flip(t, axis=2) for t in xs)

def _bidirectional(step, ctx_f, lat_f, ctx_b, lat_b, s0):
    o_cf, s_f = _chunk_scan(step, ctx_f, s0)
    o_lf, _ = _chunk_scan(step, lat_f, s_f)
    o_cb, s_b = _chunk_scan(step, _flip_time(ctx_b), s0)
    o_lb, _ = _chunk_scan(step, _flip_time(lat_b), s_b)
    return o_lf + jnp.flip(o_lb, axis=2), o_cf + jnp.flip(o_cb, axis=2)

def _gated_delta_chunk(state, xs):
    q, k, v, g, beta = xs
    c = q.shape[2]
    cum = jnp.cumsum(g, axis=-1)
    causal = jnp.tril(jnp.ones((c, c), dtype=bool))
    strict = jnp.tril(jnp.ones((c, c), dtype=bool), -1)
    decay = jnp.exp(jnp.where(causal, cum[..., :, None] - cum[..., None, :], -jnp.inf))
    kb = k * beta[..., None]
    m = jnp.where(strict, jnp.einsum('bhtd,bhsd->bhts', kb, k) * decay, 0.0)
    rhs = jnp.concatenate([v * beta[..., None], kb * jnp.exp(cum)[..., None]], axis=-1)
    sol = lax.linalg.triangular_solve(m, rhs, left_side=True, lower=True, unit_diagonal=True)
    dv = v.shape[-1]
    u, w = sol[..., :dv], sol[..., dv:]
    v_new = u - jnp.einsum('bhtk,bhkv->bhtv', w, state)
    attn = jnp.einsum('bhtk,bhsk->bhts', q, k) * decay
    out = (jnp.einsum('bhtk,bhkv->bhtv', q * jnp.exp(cum)[..., None], state)
           + jnp.einsum('bhts,bhsv->bhtv', attn, v_new))
    c_last = cum[..., -1]
    new_state = (state * jnp.exp(c_last)[..., None, None]
                 + jnp.einsum('bhsk,bhsv->bhkv', k * jnp.exp(c_last[..., None] - cum)[..., None], v_new))
    return new_state, out

def _hgrn2_chunk(state, xs):
    q, k, v, g = xs
    c = q.shape[2]
    cum = jnp.cumsum(g, axis=2)
    causal = jnp.tril(jnp.ones((c, c), dtype=bool))[:, :, None]
    decay = jnp.exp(jnp.where(causal, cum[:, :, :, None, :] - cum[:, :, None, :, :], -jnp.inf))
    attn = jnp.einsum('bhtk,bhsk,bhtsk->bhts', q, k, decay)
    out = (jnp.einsum('bhtk,bhkv->bhtv', q * jnp.exp(cum), state)
           + jnp.einsum('bhts,bhsv->bhtv', attn, v))
    c_last = cum[:, :, -1]
    new_state = (state * jnp.exp(c_last)[..., None]
                 + jnp.einsum('bhsk,bhsv->bhkv', k * jnp.exp(c_last[:, :, None] - cum), v))
    return new_state, out

def _gated_out(o, z, norm_w, n_heads):
    y = _rms(o) * norm_w.astype(jnp.float32) * jax.nn.silu(_heads(z, n_heads).astype(jnp.float32))
    return _merge_heads(y).astype(z.dtype)

def _deltanet_group(cl, cc, conv_w, a_log, dt_bias, norm_w, ctx_out):
    f32 = jnp.float32

    def prep(cols):
        qkv = _short_conv(cols['dn_qkv'], conv_w)
        b, t, _ = qkv.shape
        q, k, v = jnp.split(qkv.astype(f32), 3, axis=-1)
        q = _l2norm(_heads(q, DN_HEADS)) * DN_HEAD_DIM ** -0.5
        k = _l2norm(_heads(k, DN_HEADS))
        v = _heads(v, DN_HEADS)
        beta = jax.nn.sigmoid(cols['dn_beta'].astype(f32)).reshape(b, t, 2, DN_HEADS)
        a = cols['dn_a'].astype(f32).reshape(b, t, 2, DN_HEADS)
        g = -jnp.exp(a_log.astype(f32)) * jax.nn.softplus(a + dt_bias.astype(f32))
        beta = beta.transpose(2, 0, 3, 1)
        g = g.transpose(2, 0, 3, 1)
        return (q, k, v, g[0], beta[0]), (q, k, v, g[1], beta[1])

    lat_f, lat_b = prep(cl)
    ctx_f, ctx_b = prep(cc)
    b = cl['dn_qkv'].shape[0]
    s0 = jnp.zeros((b, DN_HEADS, DN_HEAD_DIM, DN_HEAD_DIM), f32)
    o_lat, o_ctx = _bidirectional(_gated_delta_chunk, ctx_f, lat_f, ctx_b, lat_b, s0)
    y_lat = _gated_out(o_lat, cl['dn_z'], norm_w, DN_HEADS)
    y_ctx = _gated_out(o_ctx, cc['dn_z'], norm_w, DN_HEADS) if ctx_out else None
    return y_lat, y_ctx

def _hgrn2_group(cl, cc, lb, norm_w, ctx_out):
    f32 = jnp.float32

    def prep(cols):
        b, t, _ = cols['hg_q'].shape
        q = _heads(jax.nn.silu(cols['hg_q'].astype(f32)), HG_HEADS)
        i = _heads(cols['hg_i'].astype(f32), HG_HEADS)
        f = lb + (1.0 - lb) * jax.nn.sigmoid(cols['hg_f'].astype(f32).reshape(b, t, 2, HG_W))
        f = f.reshape(b, t, 2, HG_HEADS, HG_HEAD_DIM).transpose(2, 0, 3, 1, 4)
        k = 1.0 - f
        g = jnp.log(f)
        return (q, k[0], i, g[0]), (q, k[1], i, g[1])

    lat_f, lat_b = prep(cl)
    ctx_f, ctx_b = prep(cc)
    b = cl['hg_q'].shape[0]
    s0 = jnp.zeros((b, HG_HEADS, HG_HEAD_DIM, HG_HEAD_DIM), f32)
    o_lat, o_ctx = _bidirectional(_hgrn2_chunk, ctx_f, lat_f, ctx_b, lat_b, s0)
    y_lat = _gated_out(o_lat, cl['hg_g'], norm_w, HG_HEADS)
    y_ctx = _gated_out(o_ctx, cc['hg_g'], norm_w, HG_HEADS) if ctx_out else None
    return y_lat, y_ctx

def _token_mixing(h_lat, h_ctx, w_in, w_out, q_norm, k_norm, dn_conv, dn_a_log, dn_dt_bias,
                  dn_norm, hg_lb, hg_norm, rope, ctx_out):
    cl = _split_cols(h_lat @ w_in)
    cc = _split_cols(h_ctx @ w_in)
    a_lat, a_ctx = _attention_group(cl, cc, q_norm, k_norm, rope, ctx_out)
    d_lat, d_ctx = _deltanet_group(cl, cc, dn_conv, dn_a_log, dn_dt_bias, dn_norm, ctx_out)
    g_lat, g_ctx = _hgrn2_group(cl, cc, hg_lb, hg_norm, ctx_out)
    y_lat = jnp.concatenate([a_lat, d_lat, g_lat], axis=-1) @ w_out
    y_ctx = None
    if ctx_out:
        y_ctx = jnp.concatenate([a_ctx, d_ctx, g_ctx], axis=-1) @ w_out
    return y_lat, y_ctx

def _expert_choice_ffn(h, router, w_gate, w_up, w_down):
    b, t, _ = h.shape
    cap = CAPACITY_FACTOR * t // N_EXPERTS
    aff = jax.nn.softmax(jnp.einsum('btd,de->bte', h, router).astype(jnp.float32), axis=-1)
    top_w, top_i = lax.top_k(jnp.swapaxes(aff, 1, 2), cap)
    bidx = jnp.arange(b)[:, None, None]
    xe = h[bidx, top_i]
    a = jnp.einsum('becd,edf->becf', xe, w_gate)
    u = jnp.einsum('becd,edf->becf', xe, w_up)
    y = jnp.einsum('becf,efd->becd', jax.nn.silu(a) * u, w_down) * top_w[..., None].astype(h.dtype)
    return jnp.zeros_like(h).at[bidx, top_i].add(y)

def setup_inputs(seed: int = 0) -> dict:
    key = jax.random.key(seed)
    ks = jax.random.split(key, 20)
    f32 = jnp.float32

    def nrm(k, shape, scale):
        return jax.random.normal(k, shape, f32) * scale

    dt = jnp.exp(jax.random.uniform(ks[12], (DEPTH, 2, DN_HEADS), f32, math.log(1e-3), math.log(1e-1)))
    return {
        'x': nrm(ks[0], (BATCH, SEQ, D_MODEL), 1.0),
        'c': nrm(ks[1], (BATCH, D_MODEL), 1.0),
        'ctx': nrm(ks[2], (BATCH, CTX_LEN, D_MODEL), 1.0),
        'c_ctx': nrm(ks[3], (D_MODEL,), 1.0),
        'w_mod': nrm(ks[4], (DEPTH, D_MODEL, 6 * D_MODEL), MOD_INIT * D_MODEL ** -0.5),
        'b_mod': nrm(ks[5], (DEPTH, 6 * D_MODEL), 0.01),
        'w_in': nrm(ks[6], (DEPTH, D_MODEL, IN_COLS), D_MODEL ** -0.5),
        'w_out': nrm(ks[7], (DEPTH, D_MODEL, D_MODEL), D_MODEL ** -0.5),
        'attn_q_norm': 1.0 + nrm(ks[8], (DEPTH, HEAD_DIM), 0.1),
        'attn_k_norm': 1.0 + nrm(ks[9], (DEPTH, HEAD_DIM), 0.1),
        'dn_conv': nrm(ks[10], (DEPTH, CONV_K, 3 * DN_W), CONV_K ** -0.5),
        'dn_a_log': jnp.log(jax.random.uniform(ks[11], (DEPTH, 2, DN_HEADS), f32, 1.0, 16.0)),
        'dn_dt_bias': dt + jnp.log(-jnp.expm1(-dt)),
        'dn_norm': 1.0 + nrm(ks[13], (DEPTH, DN_HEAD_DIM), 0.1),
        'hg_lower_bounds': nrm(ks[14], (DEPTH, 2, HG_W), 0.1),
        'hg_norm': 1.0 + nrm(ks[15], (DEPTH, HG_HEAD_DIM), 0.1),
        'moe_router': nrm(ks[16], (DEPTH, D_MODEL, N_EXPERTS), D_MODEL ** -0.5),
        'moe_w_gate': nrm(ks[17], (DEPTH, N_EXPERTS, D_MODEL, D_EXPERT), D_MODEL ** -0.5),
        'moe_w_up': nrm(ks[18], (DEPTH, N_EXPERTS, D_MODEL, D_EXPERT), D_MODEL ** -0.5),
        'moe_w_down': nrm(ks[19], (DEPTH, N_EXPERTS, D_EXPERT, D_MODEL), D_EXPERT ** -0.5),
    }

def reference(x, c, ctx, c_ctx, w_mod, b_mod, w_in, w_out, attn_q_norm, attn_k_norm, dn_conv,
              dn_a_log, dn_dt_bias, dn_norm, hg_lower_bounds, hg_norm, moe_router, moe_w_gate,
              moe_w_up, moe_w_down):
    rope = _rope_tables(x.shape[1], x.dtype)
    lb_w = jax.nn.softmax(hg_lower_bounds.astype(jnp.float32), axis=0)
    hg_lb = jnp.cumsum(lb_w, axis=0) - lb_w[0]
    cond_lat = jax.nn.silu(c)[:, None, :]
    cond_ctx = jax.nn.silu(c_ctx)[None, None, :]
    x_lat, x_ctx = x, ctx
    for l in range(DEPTH):
        ctx_out = l < DEPTH - 1
        m_lat = jnp.split(cond_lat @ w_mod[l] + b_mod[l], 6, axis=-1)
        m_ctx = jnp.split(cond_ctx @ w_mod[l] + b_mod[l], 6, axis=-1)
        y_lat, y_ctx = _token_mixing(
            _modulate(x_lat, m_lat[0], m_lat[1]), _modulate(x_ctx, m_ctx[0], m_ctx[1]),
            w_in[l], w_out[l], attn_q_norm[l], attn_k_norm[l], dn_conv[l], dn_a_log[l],
            dn_dt_bias[l], dn_norm[l], hg_lb[l], hg_norm[l], rope, ctx_out)
        x_lat = x_lat + m_lat[2] * y_lat
        x_lat = x_lat + m_lat[5] * _expert_choice_ffn(
            _modulate(x_lat, m_lat[3], m_lat[4]), moe_router[l], moe_w_gate[l], moe_w_up[l], moe_w_down[l])
        if ctx_out:
            x_ctx = x_ctx + m_ctx[2] * y_ctx
            x_ctx = x_ctx + m_ctx[5] * _expert_choice_ffn(
                _modulate(x_ctx, m_ctx[3], m_ctx[4]), moe_router[l], moe_w_gate[l], moe_w_up[l], moe_w_down[l])
    return x_lat


_drawn_inputs = setup_inputs


def setup_inputs(seed=0):
    import zlib

    import numpy as np

    out = dict(_drawn_inputs(seed))
    spreads = {}
    factors = {'ctx': 2.798,
     'b_mod': 4.637,
     'attn_q_norm': 8.0,
     'attn_k_norm': 8.0,
     'dn_norm': 3.743,
     'hg_lower_bounds': 8.0,
     'hg_norm': 3.715}
    for name, (base, spread) in spreads.items():
        noise = np.random.default_rng([zlib.crc32(name.encode()), seed]).standard_normal(out[name].shape)
        drawn = base * np.exp(spread * noise) if base else spread * noise
        out[name] = jnp.asarray(drawn.astype(out[name].dtype))
    for name, factor in factors.items():
        out[name] = (out[name] * factor).astype(out[name].dtype)
    return out
```

```python
from contextlib import ExitStack

import concourse.bass as bass
from concourse import mybir
import numpy as np

F32 = mybir.dt.float32
I32 = mybir.dt.int32
ACT = mybir.ActivationFunctionType
ALU = mybir.AluOpType
AX = mybir.AxisListType.X

P = 128
DEPTH, D = 2, 1024
CTX, LAT = 256, 512
TOK = CTX + LAT
NT, NT_CTX, NT_LAT = TOK // P, CTX // P, LAT // P
KT = D // P
HD = 64
NQ, NKV = 8, 2
DNH = 4
CHUNK = 64
NCH = TOK // CHUNK
NCH_CTX = CTX // CHUNK
LEVELS = 6
CONV_K = 5
IN_COLS = 3088
NE, FF = 16, 1408
FT = FF // P
CAP_L, CAP_C = 2 * LAT // NE, 2 * CTX // NE
CAP = CAP_L + CAP_C
EPS = 1e-6
GRID_W = 64
ROPE_THETA = 10000.0

GROUPS = [(0, 512, "T"), (512, 256, "T"), (768, 384, "C"), (1152, 384, "C"),
          (1536, 272, "T"), (1808, 512, "C"), (2320, 256, "C"), (2576, 512, "T")]
N_MOD = 6 * D // 512
N_IN = 7 + 7 * DEPTH
LOADS = N_MOD + len(GROUPS) + 2
WRING = 2
CHOOSE_STEPS = 1 + 2 * NT + (NT_CTX - 1) * 2 + (NT_LAT - 1) * 2 + 1

CONST = {}


def _layout():
    at = 0
    for name, n in (("ident", 128), ("lvl0", 7 * 64), ("lvl1", 7 * 64), ("strict0", 128), ("strict1", 128),
                    ("incl0", 128), ("incl1", 128), ("chunkind", 256), ("causal0", 64), ("causal1", 64),
                    ("iota", 64), ("before", 128), ("after", 128), ("ident64", 64), ("cc", 256), ("ss", 256)):
        CONST[name] = (at, n)
        at += n
    return at


N_CONST = _layout()


def constants():
    p = np.arange(P)[:, None]
    c = np.arange(P)[None, :]
    t64 = np.arange(64)[None, :]
    s64 = p % 64
    same = (p // 64) == (c // 64)
    out = np.zeros((P, N_CONST), np.float32)

    def put(name, a):
        at, n = CONST[name]
        out[:, at:at + n] = np.broadcast_to(a, (P, n))

    put("ident", p == c)
    lv = []
    for level in range(LEVELS):
        h = 1 << level
        lv.append((s64 // (2 * h) == t64 // (2 * h)) & (s64 % (2 * h) < h) & (t64 % (2 * h) >= h))
    lv.append(s64 == t64)
    put("lvl0", np.concatenate(lv, 1))
    lv = []
    for level in range(LEVELS):
        h = 1 << level
        lv.append((s64 // (2 * h) == t64 // (2 * h)) & (s64 % (2 * h) >= h) & (t64 % (2 * h) < h))
    lv.append(s64 == t64)
    put("lvl1", np.concatenate(lv, 1))
    put("strict0", same & (p > c))
    put("strict1", same & (p < c))
    put("incl0", same & (p <= c))
    put("incl1", same & (p >= c))
    put("chunkind", np.concatenate([np.broadcast_to(p // 64 == h, (P, P)) for h in range(2)], 1))
    put("causal0", s64 <= t64)
    put("causal1", s64 >= t64)
    put("iota", t64)
    put("before", c < p)
    put("after", c > p)
    put("ident64", s64 == t64)
    n_freq = HD // 4
    inv = (np.float32(ROPE_THETA) ** (-np.arange(n_freq, dtype=np.float32) / np.float32(n_freq))).astype(np.float32)
    t = np.arange(LAT)
    row, col = (t // GRID_W).astype(np.float32), (t % GRID_W).astype(np.float32)
    ar, ac = row[:, None] * inv, col[:, None] * inv
    cc = np.concatenate([np.cos(ar), np.cos(ar), np.cos(ac), np.cos(ac)], 1)
    ss = np.concatenate([-np.sin(ar), np.sin(ar), -np.sin(ac), np.sin(ac)], 1)
    put("cc", cc.reshape(NT_LAT, P, HD).transpose(1, 0, 2).reshape(P, -1))
    put("ss", ss.reshape(NT_LAT, P, HD).transpose(1, 0, 2).reshape(P, -1))
    return out


class Signal:

    def __init__(self, sem, per_layer):
        self.sem, self.per_layer = sem, per_layer

    def n(self, layer, count):
        return layer * self.per_layer + count


def trunk_program(nc, t):
    ctx = ExitStack()
    with ctx:
        def sb(name, shape, dt=F32):
            return ctx.enter_context(nc.sbuf_tensor(name, shape, dt))

        def sem(name, per_layer=0):
            return Signal(ctx.enter_context(nc.semaphore(name)), per_layer)

        x = sb("x", [P, NT, D])
        const = sb("const", [P, N_CONST])
        rows = sb("rows", [84, P])
        rowsT = sb("rowsT", [P, 84])
        condT = sb("condT", [P, 2 * KT])
        small = sb("small", [P, DEPTH, 4 * HD + 16])
        modC = sb("modC", [P, 4, KT, 2])
        gates = sb("gates", [2, 2, D])
        lbT = sb("lbT", [P, DEPTH, 4])
        omlT = sb("omlT", [P, DEPTH, 4])
        lbw = sb("lbw", [P, 6, 4])
        sel2 = sb("sel2", [2, 2, P])
        ones16 = sb("ones16", [16, P])
        ss = sb("ss", [P, 64])
        ss2 = sb("ss2", [P, 64])
        rs = sb("rs", [P, 64])
        nmax = sb("nmax", [P, 48])
        rsum = sb("rsum", [P, 48])
        rinv = sb("rinv", [P, 48])
        bt = sb("bt", [P, NT, 8])
        gg = sb("gg", [P, NT, 8])
        ga = sb("ga", [P, NT, 8])
        gb = sb("gb", [P, NT, 8])
        ealog = sb("ealog", [P, 8])
        sc = sb("sc", [P, 96])
        eb = sb("eb", [P, NT, DNH])
        ec = sb("ec", [P, 2, NCH])
        rw = sb("rw", [P, DEPTH, KT, NE])
        aff = sb("aff", [P, NT, NE + 1])
        affe = sb("affe", [P, NT])
        rk = sb("rk", [P, NT, 4])
        rank = sb("rank", [P, NT])
        lmax = sb("lmax", [P, NT])
        selM = sb("selM", [2, CAP])
        arena = sb("arena", [P, 43000])
        ps = ctx.enter_context(nc.psum_tensor("ps", [P, 8, 512], F32))

        def view(at, *dims):
            n = int(np.prod(dims))
            v = arena[:, at:at + n]
            if len(dims) == 1:
                return v
            names = "abcde"[:len(dims)]
            return v.rearrange(f"p ({' '.join(names)}) -> p {' '.join(names)}", **dict(zip(names, dims)))

        def cst(name):
            at, n = CONST[name]
            return const[:, at:at + n]

        ident = cst("ident")
        lvl = [cst(f"lvl{d}").rearrange("p (l t) -> p l t", l=7) for d in range(2)]
        lvl_i = [cst(f"lvl{d}").bitcast(I32).rearrange("p (l t) -> p l t", l=7) for d in range(2)]
        hT = view(0, KT, TOK)
        wst = [view(6144 + 4096 * i, KT, 512) for i in range(WRING)]
        qk = view(14336, NT, 640)
        vtok = view(18176, NT, 128)
        convin = view(18944, 6, 776)
        dz = view(23600, NT, 272)
        hgc = view(25232, 6, TOK)
        hgt = view(29840, NT, 512)
        ycat = view(32912, NT, D)
        modrow = view(18944, 6144)
        xn = ycat
        extra = 39056
        sq = view(32912, 3840)
        qn = view(32912, NT, 640)
        rope2 = view(extra, 640)
        qkT = view(0, 5, TOK)
        prob = [view(3840 + TOK * i, TOK) for i in range(2)]
        probT = [view(5376 + TOK * i, TOK) for i in range(2)]
        convout = view(10752, 6, 772)
        dt = view(0, NT, 768)
        sq_dn = view(10752, NT, 512)
        kqT = view(4608, 2, NCH, 2, HD)
        Uc = view(7680, NCH, 2, HD)
        vnew = view(7680, NT, DNH, HD)
        S = view(9216, NCH, 2, HD)
        AT = view(10752, NT, DNH, HD)
        TR = view(12288, NT, 2, DNH, HD)
        vke = view(15360, NT, DNH, 2 * HD)
        NTm = view(18944, NT, DNH, HD)
        NL = view(20480, NT, DNH, HD)
        ysol = view(18944, NT, DNH, 2 * HD)
        kbe = view(22016, NT, DNH, HD)
        Dm = view(extra, NT, DNH, HD)
        Um = view(extra, NT, DNH, HD)
        G = view(extra, NCH, 2, HD)
        otmp = view(extra, NT, DNH, HD)
        sqg = view(extra, NT, 256)
        ykT = dt[:, :, 0:256].rearrange("p i (b c t) -> p i b c t", b=2, c=2)

        gpad = view(0, 2, NCH, CHUNK + 1)
        Cc = view(1560, 2, NCH, CHUNK + 1)
        kk = view(3120, 2, TOK)
        Z = [view(4656 + TOK * i, TOK) for i in range(4)]
        Ah = view(7728, DNH, NT, HD)
        ED = view(9264, 2, TOK)
        ER = view(10800, 2, TOK)
        ket = view(12336, NT, 256)
        Uh = view(13872, NCH, 2, HD)
        Sh = view(15408, NCH, 2, HD)
        reset = view(16944, NCH, CHUNK + 1)
        yT = view(0, KT, TOK)
        gbc = view(14336, 2, D)
        otmp2 = [view(extra + 512 * i, 512) for i in range(2)]
        gu = [view(2 * FF * i, 2, FF) for i in range(4)]
        down = view(11264, FT, D)
        hT2 = view(11264, KT, TOK)
        xn2 = view(22528, NT, D)
        xeT = view(28672, KT, CAP)
        sg = view(30208, FF)
        hh = view(31616, FF)
        hTm = view(33024, FT, CAP)
        ye = view(34080, D)
        WT = view(35104, NT, P)
        Gm = view(36640, NT, CAP_L)
        Wm = view(37024, NT, CAP)
        affm = view(37600, TOK)
        affT = view(38368, TOK)
        gateM = view(39136, D)
        rjunk = view(40160, 512)

        s_in = sem("s_in")
        s_rowsT = sem("s_rowsT")
        s_cond = sem("s_cond")
        s_setup = sem("s_setup")
        wload = [sem(f"wload{i}") for i in range(WRING)]
        wfree = sem("wfree", LOADS)
        bmod = sem("bmod", 32)
        modmm = sem("modmm", N_MOD)
        modadd = sem("modadd", N_MOD)
        modT = sem("modT", 1)
        modcol = sem("modcol", 1)
        sumsq = sem("sumsq", 12)
        rstd = sem("rstd", 2)
        act_rs = sem("act_rs", 2)
        normed = sem("normed", 12)
        normT = sem("normT", 16)
        hT_a = sem("hT_a", 8)
        hT_v = sem("hT_v", 8)
        proj = sem("proj", 48)
        projev = sem("projev", 48)
        qk_ss = sem("qk_ss", 1)
        qk_rs = sem("qk_rs", 1)
        qk_ready = sem("qk_ready", 1)
        qkt = sem("qkt", 5)
        qktev = sem("qktev", 5)
        score = sem("score", 48)
        smax = sem("smax", 48)
        expd = sem("expd", 48)
        ptt = sem("ptt", 48)
        pt_a = sem("pt_a", 48)
        pt_v = sem("pt_v", 48)
        pv = sem("pv", 48)
        attn_y = sem("attn_y", 48)
        conv = sem("conv", 30)
        convact = sem("convact", 6)
        dtt = sem("dtt", 6)
        dtev = sem("dtev", 6)
        dn_ss = sem("dn_ss", 1)
        dn_rs = sem("dn_rs", 1)
        dn_norm = sem("dn_norm", 6)
        kqt = sem("kqt", 6)
        kqtev = sem("kqtev", 6)
        gate_v = sem("gate_v", 1)
        gate_a = sem("gate_a", 4)
        gbr = sem("gbr", 12)
        decay = sem("decay", 12)
        dexp = sem("dexp", 14)
        gram = sem("gram", 12)
        pairs = sem("pairs", 12)
        vke_v = sem("vke_v", 2)
        kev = sem("kev", 2)
        nl = sem("nl", 72)
        umm = sem("umm", 72)
        uev = sem("uev", 60)
        trm = sem("trm", 60)
        tru = sem("tru", 72)
        ymm = sem("ymm", 12)
        yev = sem("yev", 12)
        gmm = sem("gmm", 12)
        gev_a = sem("gev_a", 12)
        gev_v = sem("gev_v", 12)
        step = sem("step", 22)
        stepv = sem("stepv", 24)
        zmm = sem("zmm", 12)
        vnw = sem("vnw", 12)
        avm = sem("avm", 12)
        outv = sem("outv", 12)
        go_ss = sem("go_ss", 2)
        go_rs = sem("go_rs", 2)
        f_a = sem("f_a", 2)
        f_v = sem("f_v", 2)
        g_a = sem("g_a", 2)
        zsub = sem("zsub", 24)
        zexp = sem("zexp", 24)
        zmul = sem("zmul", 24)
        hgram = sem("hgram", 28)
        hpred = sem("hpred", 28)
        er_v = sem("er_v", 2)
        er_a = sem("er_a", 2)
        qe_v = sem("qe_v", 2)
        kett = sem("kett", 12)
        ketev = sem("ketev", 12)
        umh = sem("umh", 12)
        uhev = sem("uhev", 12)
        hstate = sem("hstate", 2)
        hout = sem("hout", 12)
        houtv = sem("houtv", 12)
        mixed = sem("mixed", 1)
        yt = sem("yt", 8)
        yt_a = sem("yt_a", 4)
        yt_v = sem("yt_v", 4)
        gbmm = sem("gbmm", 4)
        gbev = sem("gbev", 4)
        wo = sem("wo", 12)
        wov = sem("wov", 12)
        logit = sem("logit", 1)
        aff_v = sem("aff_v", 1)
        aff_a = sem("aff_a", 1)
        affr = sem("affr", 1)
        affTm = sem("affTm", 1)
        affTv = sem("affTv", 1)
        gm_mm = sem("gm_mm", 1)
        gm_v = sem("gm_v", 1)
        affm_v = sem("affm_v", 17)
        bc_mm = sem("bc_mm", 17)
        picked = sem("picked", 17)
        gath = sem("gath", 17)
        xe_a = sem("xe_a", 17)
        xe_v = sem("xe_v", 17)
        wtm = sem("wtm", 17)
        wta = sem("wta", 17)
        guld = [sem(f"guld{i}", 64 * 16) for i in range(4)]
        dld = [sem(f"dld{i}", 16 * 16) for i in range(3)]
        gufree = sem("gufree", 128)
        dfree = sem("dfree", 48)
        h_a = sem("h_a", 48)
        h_v = sem("h_v", 48)
        htm = sem("htm", 48)
        hta = sem("hta", 48)
        ymm2 = sem("ymm2", 32)
        ye_v = sem("ye_v", 32)
        scm = sem("scm", 192)
        scv = sem("scv", 192)
        cstep = sem("cstep")
        act_step = sem("act_step")
        dve_step = sem("dve_step")
        s_out = sem("s_out")
        counts = {"act": 0, "dve": 0}

        def link_act(ins):
            counts["act"] += 1
            ins.then_inc(act_step.sem, 1)
            nc.scalar.wait_ge(act_step.sem, counts["act"])

        def link(ins):
            counts["dve"] += 1
            ins.then_inc(dve_step.sem, 1)
            nc.vector.wait_ge(dve_step.sem, counts["dve"])

        def loads(layer):
            w_mod, w_in, w_out = t["w_mod"], t["w_in"], t["w_out"]
            for g in range(N_MOD):
                yield w_mod[layer][:, g * 512:(g + 1) * 512], 512
            for c0, n, _ in GROUPS:
                yield w_in[layer][:, c0:c0 + n], n
            for g in range(2):
                yield w_out[layer][:, g * 512:(g + 1) * 512], 512

        def staged(eng, layer, g):
            n = layer * LOADS + g
            eng.wait_ge(wload[n % WRING].sem, 16 * (n // WRING + 1))
            return wst[n % WRING]

        def proj_units():
            for g, (c0, n, kind) in enumerate(GROUPS):
                if kind == "T":
                    for i in range(NT):
                        yield g, kind, i, 0, n
                else:
                    for c in range(n // P):
                        for seg in range(2):
                            yield g, kind, c, seg, (CTX, LAT)[seg]

        def sync_program(sp):
            for layer in range(DEPTH):
                for g, (src, n) in enumerate(loads(layer)):
                    k = layer * LOADS + g
                    if k >= WRING:
                        sp.wait_ge(wfree.sem, k - WRING + 1)
                    if g == N_MOD + len(GROUPS):
                        sp.wait_ge(mixed.sem, mixed.n(layer, 1))
                    if g == 0:
                        if layer:
                            sp.wait_ge(scv.sem, scv.n(layer - 1, 192))
                        for r in range(2):
                            sp.dma_start(modrow[r:r + 1, :], t["b_mod"][layer:layer + 1, :]).then_inc(bmod.sem, 16)
                    sp.dma_start(wst[k % WRING][:, :, 0:n], src.rearrange("(f p) n -> p f n", p=P)) \
                        .then_inc(wload[k % WRING].sem, 16)
                sp_experts(sp, layer)
            sp.wait_ge(scv.sem, scv.n(DEPTH - 1, 192))
            sp.dma_start(t["out"][0].rearrange("(i p) d -> p i d", p=P), x[:, NT_CTX:NT, :]).then_inc(s_out.sem, 16)
            sp.wait_ge(s_out.sem, 16)

        def scalar_program(act):
            lat = t["x"][0].rearrange("(i p) d -> p i d", p=P)
            cx = t["ctx"][0].rearrange("(i p) d -> p i d", p=P)
            ins = [(const[:, :], t["consts"]),
                   (rows[0:60, :], t["dn_conv"].rearrange("l k (j p) -> (l k j) p", p=P)),
                   (rows[60:68, :], t["hg_lower_bounds"].rearrange("l r (j p) -> (l r j) p", p=P)),
                   (rows[68:76, :], t["c"].rearrange("b (f p) -> (b f) p", p=P)),
                   (rows[76:84, :], t["c_ctx"].rearrange("(f p) -> f p", p=P)),
                   (x[:, 0:NT_CTX, :], cx), (x[:, NT_CTX:NT, :], lat)]
            for layer in range(DEPTH):
                for j, name in enumerate(("attn_q_norm", "attn_k_norm", "dn_norm", "hg_norm")):
                    ins.append((small[:, layer, j * HD:(j + 1) * HD], t[name][layer].partition_broadcast(P)))
                for j, name in enumerate(("dn_a_log", "dn_dt_bias")):
                    ins.append((small[:, layer, 4 * HD + 8 * j:4 * HD + 8 * j + 8],
                                t[name][layer].rearrange("r h -> (r h)").partition_broadcast(P)))
                ins.append((rw[:, layer], t["moe_router"][layer].rearrange("(f p) e -> p f e", p=P)))
            assert len(ins) == N_IN
            for dst, src in ins:
                act.dma_start(dst, src).then_inc(s_in.sem, 16)
            act.wait_ge(s_rowsT.sem, 1)
            nc.scalar.activation(rowsT[:, :], ps[:, 7, 0:84], ACT.Copy).then_inc(s_cond.sem, 1)
            nc.scalar.activation(condT[:, :], ps[:, 7, 68:84], ACT.Silu).then_inc(s_cond.sem, 1)
            act.wait_ge(s_setup.sem, 1)
            nc.scalar.activation(lbw[:, 1:3, :], lbw[:, 1:3, :], ACT.Exp).then_inc(s_setup.sem, 1)
            for layer in range(DEPTH):
                act_norm(act, layer, 0)
                act_proj(act, layer)
                act_attention(act, layer)
                act_deltanet(act, layer)
                act_hgrn(act, layer)
                act_out(act, layer)
                act_norm(act, layer, 1)
                act_experts(act, layer)

        def act_norm(act, layer, which):
            act.wait_ge(s_in.sem, 16 * N_IN)
            if which == 1:
                act.wait_ge(wov.sem, wov.n(layer, 12))
            elif layer:
                act.wait_ge(scv.sem, scv.n(layer - 1, 192))
                act.wait_ge(wta.sem, wta.n(layer - 1, NE + 1))
            for i in range(NT):
                nc.scalar.activation((xn if which == 0 else xn2)[:, i, :], x[:, i, :], ACT.Square, accum_out=ss[:, i:i + 1]) \
                    .then_inc(sumsq.sem, 1)
            act.wait_ge(rstd.sem, rstd.n(layer, which + 1))
            link_act(nc.scalar.activation(rs[:, 0:NT], ss2[:, 0:NT], ACT.Ln))
            nc.scalar.activation(rs[:, 0:NT], rs[:, 0:NT], ACT.Exp, scale=-0.5).then_inc(act_rs.sem, 1)
            for f in range(0, KT, 2):
                act.wait_ge(normT.sem, normT.n(layer, 8 * which + f + 1))
                if f == 0:
                    act.wait_ge(modcol.sem, modcol.n(layer, 1))
                b = 2 * (f % 3)
                for v, (bank, c0, n) in enumerate(((b + 1, CTX, LAT), (b, 0, CTX))):
                    ins = nc.scalar.activation((hT if which == 0 else hT2)[:, f, c0:c0 + n], ps[:, bank, 0:n], ACT.Identity,
                                               scale=modC[:, 2 * which + 1, f, v:v + 1],
                                               bias=modC[:, 2 * which, f, v:v + 1])
                ins.then_inc(hT_a.sem, 1)

        def act_proj(act, layer):
            for u, (g, kind, a, seg, n) in enumerate(proj_units()):
                act.wait_ge(proj.sem, proj.n(layer, u + 1))
                src = ps[:, u % 6, 0:n]
                c0 = GROUPS[g][0]
                if g == 0:
                    todo = [(qk[:, a, 0:512], src, ACT.Copy)]
                elif g == 1:
                    todo = [(qk[:, a, 512:640], src[:, 0:128], ACT.Copy), (vtok[:, a, :], src[:, 128:256], ACT.Copy)]
                elif g in (2, 3):
                    j = (c0 - 768) // P + a
                    todo = [(convin[:, j, (2, 262)[seg]:(2, 262)[seg] + n], src, ACT.Copy)]
                elif g == 4:
                    todo = [(dz[:, a, 0:256], src[:, 0:256], ACT.Silu), (dz[:, a, 256:272], src[:, 256:272], ACT.Copy)]
                elif g in (5, 6):
                    j = (c0 - 1808) // P + a
                    todo = [(hgc[:, j, (0, CTX)[seg]:(0, CTX)[seg] + n], src, ACT.Silu if j < 2 else ACT.Copy)]
                else:
                    todo = [(hgt[:, a, 0:256], src[:, 0:256], ACT.Copy), (hgt[:, a, 256:512], src[:, 256:512], ACT.Silu)]
                for dst, s, fn in todo:
                    ins = nc.scalar.activation(dst, s, fn)
                ins.then_inc(projev.sem, 1)

        def tensor_program(pe):
            pe.wait_ge(s_in.sem, 16 * N_IN)
            nc.tensor.transpose(ps[:, 7, 0:84], rows[:, :], ident[0:84, 0:84]).then_inc(s_rowsT.sem, 1)
            pe.wait_ge(s_cond.sem, 2)
            for layer in range(DEPTH):
                pe_mod(pe, layer)
                pe_norm(pe, layer, 0)
                pe_proj(pe, layer)
                pe_attention(pe, layer)
                pe_deltanet(pe, layer)
                pe_hgrn(pe, layer)
                pe_out(pe, layer)
                pe_norm(pe, layer, 1)
                pe_experts(pe, layer)

        def pe_mod(pe, layer):
            cT = condT[:, :].rearrange("p (v f) -> p f v", v=2)
            if layer:
                pe.wait_ge(wta.sem, wta.n(layer - 1, NE + 1))
                pe.wait_ge(scv.sem, scv.n(layer - 1, 192))
            for g in range(N_MOD):
                w = staged(pe, layer, g)
                if g >= 2:
                    pe.wait_ge(modadd.sem, modadd.n(layer, g - 1))
                for f in range(KT):
                    ins = nc.tensor.matmul(ps[0:2, g % 2, :], lhsT=cT[:, f, :], rhs=w[:, f, :],
                                           start=(f == 0), stop=(f == KT - 1))
                ins.then_inc(modmm.sem, 1)
                pe.wait_ge(modmm.sem, modmm.n(layer, g + 1))
                pe.sem_inc(wfree.sem, 1)
            pe.wait_ge(modadd.sem, modadd.n(layer, N_MOD))
            for m, part in enumerate((0, 1, 3, 4)):
                for f in range(KT):
                    c0 = part * D + f * P
                    at = 2 * (m * KT + f)
                    ins = nc.tensor.transpose(ps[:, 6, at:at + 2], modrow[0:2, c0:c0 + P], ident[0:2, 0:2])
            ins.then_inc(modT.sem, 1)

        def pe_norm(pe, layer, which):
            for f in range(KT):
                if f == 0:
                    pe.wait_ge(normed.sem, normed.n(layer, 6 * which + 6))
                if f >= 3:
                    evacuated = (hT_a, hT_v)[(f - 3) % 2]
                    pe.wait_ge(evacuated.sem, evacuated.n(layer, 4 * which + (f - 3) // 2 + 1))
                b = 2 * (f % 3)
                for i in range(NT):
                    bank, c0 = (b, i * P) if i < NT_CTX else (b + 1, (i - NT_CTX) * P)
                    src = (xn if which == 0 else xn2)[:, i, f * P:(f + 1) * P]
                    ins = nc.tensor.transpose(ps[:, bank, c0:c0 + P], src, ident)
                ins.then_inc(normT.sem, 1)

        def pe_proj(pe, layer):
            pe.wait_ge(hT_a.sem, hT_a.n(layer, 4))
            pe.wait_ge(hT_v.sem, hT_v.n(layer, 4))
            last_g, w = -1, None
            units = list(proj_units())
            for u, (g, kind, a, seg, n) in enumerate(units):
                if g != last_g:
                    w, last_g = staged(pe, layer, N_MOD + g), g
                if u >= 6:
                    pe.wait_ge(projev.sem, projev.n(layer, u - 5))
                for f in range(KT):
                    out = ps[:, u % 6, 0:n]
                    if kind == "T":
                        lhs, rhs = hT[:, f, a * P:(a + 1) * P], w[:, f, 0:n]
                    else:
                        c0 = (0, CTX)[seg]
                        lhs, rhs = w[:, f, a * P:(a + 1) * P], hT[:, f, c0:c0 + n]
                    ins = nc.tensor.matmul(out, lhsT=lhs, rhs=rhs, start=(f == 0), stop=(f == KT - 1))
                ins.then_inc(proj.sem, 1)
                if u + 1 == len(units) or units[u + 1][0] != g:
                    pe.wait_ge(proj.sem, proj.n(layer, u + 1))
                    pe.sem_inc(wfree.sem, 1)

        def vector_program(dve):
            nc.vector.memset(ones16[:, :], 1.0)
            dve.wait_ge(s_in.sem, 16 * N_IN)
            nc.vector.tensor_copy(sel2[:, :, :], ident[0:2, 0:2].unsqueeze(2).broadcast_to([2, 2, P]))
            nc.vector.tensor_copy(selM[:, 0:CAP_L], ident[0:2, 0:1].broadcast_to([2, CAP_L]))
            nc.vector.tensor_copy(selM[:, CAP_L:CAP], ident[0:2, 1:2].broadcast_to([2, CAP_C]))
            dve.wait_ge(s_cond.sem, 2)
            b0, b1 = rowsT[:, 60:64], rowsT[:, 64:68]
            link(nc.vector.tensor_tensor(lbw[:, 0, :], b0, b1, ALU.max))
            nc.vector.tensor_tensor(lbw[:, 1, :], b0, lbw[:, 0, :], ALU.subtract)
            nc.vector.tensor_tensor(lbw[:, 2, :], b1, lbw[:, 0, :], ALU.subtract).then_inc(s_setup.sem, 1)
            dve.wait_ge(s_setup.sem, 2)
            link(nc.vector.tensor_tensor(lbw[:, 3, :], lbw[:, 1, :], lbw[:, 2, :], ALU.add))
            link(nc.vector.reciprocal(lbw[:, 3, :], lbw[:, 3, :]))
            nc.vector.tensor_tensor(lbw[:, 4, :], lbw[:, 1, :], lbw[:, 3, :], ALU.mult)
            link(nc.vector.tensor_tensor(lbw[:, 5, :], lbw[:, 2, :], lbw[:, 3, :], ALU.mult))
            link(nc.vector.tensor_tensor(lbw[:, 5, :], lbw[:, 4, :], lbw[:, 5, :], ALU.add))
            nc.vector.tensor_tensor(lbT[:, 0, :], lbw[:, 4, :], lbw[:, 4, :], ALU.subtract)
            link(nc.vector.tensor_tensor(lbT[:, 1, :], lbw[:, 5, :], lbw[:, 4, :], ALU.subtract))
            nc.vector.tensor_scalar(omlT[:, :, :], lbT[:, :, :], -1.0, 1.0, ALU.mult, ALU.add)
            for layer in range(DEPTH):
                dve_mod(dve, layer)
                dve_norm(dve, layer, 0)
                dve_attention(dve, layer)
                dve_deltanet(dve, layer)
                dve_hgrn(dve, layer)
                dve_out(dve, layer)
                dve_norm(dve, layer, 1)
                dve_experts(dve, layer)

        def dve_mod(dve, layer):
            dve.wait_ge(bmod.sem, bmod.n(layer, 32))
            for g in range(N_MOD):
                dve.wait_ge(modmm.sem, modmm.n(layer, g + 1))
                row = modrow[0:2, g * 512:(g + 1) * 512]
                part = g // 2
                if part in (2, 5):
                    dst = gates[:, part // 3, (g % 2) * 512:(g % 2) * 512 + 512]
                else:
                    dst = row
                nc.vector.tensor_tensor(dst, ps[0:2, g % 2, :], row, ALU.add).then_inc(modadd.sem, 1)
            dve.wait_ge(modT.sem, modT.n(layer, 1))
            for m in range(4):
                src = ps[:, 6, 16 * m:16 * m + 16].rearrange("p (f v) -> p f v", v=2)
                ins = nc.vector.tensor_scalar(modC[:, m, :, :], src, float(m % 2), None, ALU.add)
            ins.then_inc(modcol.sem, 1)

        def dve_norm(dve, layer, which):
            dve.wait_ge(sumsq.sem, sumsq.n(layer, 6 * which + 6))
            nc.vector.tensor_scalar(ss2[:, 0:NT], ss[:, 0:NT], 1.0 / D, EPS, ALU.mult, ALU.add) \
                .then_inc(rstd.sem, 1)
            dve.wait_ge(act_rs.sem, act_rs.n(layer, which + 1))
            for i in range(NT):
                nc.vector.tensor_scalar((xn if which == 0 else xn2)[:, i, :], x[:, i, :], rs[:, i:i + 1], None,
                                        ALU.mult).then_inc(normed.sem, 1)
            dve.wait_ge(modcol.sem, modcol.n(layer, 1))
            for f in range(1, KT, 2):
                dve.wait_ge(normT.sem, normT.n(layer, 8 * which + f + 1))
                b = 2 * (f % 3)
                for v, (bank, c0, n) in enumerate(((b + 1, CTX, LAT), (b, 0, CTX))):
                    ins = nc.vector.tensor_scalar((hT if which == 0 else hT2)[:, f, c0:c0 + n], ps[:, bank, 0:n],
                                                  modC[:, 2 * which + 1, f, v:v + 1],
                                                  modC[:, 2 * which, f, v:v + 1], ALU.mult, ALU.add)
                ins.then_inc(hT_v.sem, 1)


        def attn_unit(u):
            qt, h = divmod(u, NQ)
            return qt, h, h // 4, h % 4, (NT_CTX if qt < NT_CTX else NT)

        def dve_attention(dve, layer):
            dve.wait_ge(projev.sem, projev.n(layer, 12))
            flat = qk.rearrange("p i c -> p (i c)")
            dve.wait_ge(normT.sem, normT.n(layer, 8))
            link(nc.vector.tensor_tensor(sq, flat, flat, ALU.mult))
            link(nc.vector.tensor_reduce(ss[:, 0:60], sq.rearrange("p (h d) -> p h d", d=HD), AX, ALU.add))
            nc.vector.tensor_scalar(ss2[:, 0:60], ss[:, 0:60], 1.0 / HD, EPS, ALU.mult, ALU.add) \
                .then_inc(qk_ss.sem, 1)
            dve.wait_ge(qk_rs.sem, qk_rs.n(layer, 1))
            rq = rs[:, 0:60].rearrange("p (i h) -> p i h", h=10)[:, :, 0:NQ]
            link(nc.vector.tensor_scalar(rq, rq, HD ** -0.5, None, ALU.mult))
            qh = qk.rearrange("p i (h d) -> p (i h) d", d=HD)
            link(nc.vector.tensor_tensor(qh, qh, rs[:, 0:60].unsqueeze(2).broadcast_to([P, 60, HD]), ALU.mult))
            for i in range(NT):
                src = qk[:, i, 0:512].rearrange("p (k j d) -> p k j d", k=2, d=HD)
                dst = qn[:, i, 0:512].rearrange("p (j k d) -> p k j d", k=2, d=HD)
                w = small[:, layer, 0:HD].unsqueeze(1).unsqueeze(1).broadcast_to([P, 2, 4, HD])
                nc.vector.tensor_tensor(dst, src, w, ALU.mult)
                src = qk[:, i, 512:640].rearrange("p (k d) -> p k d", d=HD)
                dst = qn[:, i, 512:640].rearrange("p (k d) -> p k d", d=HD)
                w = small[:, layer, HD:2 * HD].unsqueeze(1).broadcast_to([P, 2, HD])
                ins = nc.vector.tensor_tensor(dst, src, w, ALU.mult)
            link(ins)
            cc = cst("cc").rearrange("p (i d) -> p i d", d=HD)
            s_ = cst("ss").rearrange("p (i b h d) -> p i b h d", b=2, h=2, d=16)
            for i in range(NT_LAT):
                q = qn[:, NT_CTX + i, :]
                t1 = qk[:, NT_CTX + i, :]
                nc.vector.tensor_tensor(t1.rearrange("p (h d) -> p h d", d=HD), q.rearrange("p (h d) -> p h d", d=HD),
                                        cc[:, i, :].unsqueeze(1).broadcast_to([P, 10, HD]), ALU.mult)
                for half in range(2):
                    src = q.rearrange("p (a b h d) -> p a b h d", b=2, h=2, d=16)[:, :, :, 1 - half, :]
                    dst = rope2.rearrange("p (a b h d) -> p a b h d", b=2, h=2, d=16)[:, :, :, half, :]
                    tab = s_[:, i, :, half, :].unsqueeze(1).broadcast_to([P, 10, 2, 16])
                    ins = nc.vector.tensor_tensor(dst, src, tab, ALU.mult)
                link(ins)
                link(nc.vector.tensor_tensor(q, t1, rope2, ALU.add))
            nc.vector.memset(ss[:, 60:61], 0.0).then_inc(qk_ready.sem, 1)

            def row_max(u):
                nk = attn_unit(u)[4]
                dve.wait_ge(score.sem, score.n(layer, u + 1))
                b = 2 * (u % 2)
                nc.vector.tensor_reduce(nmax[:, u:u + 1], ps[:, b:b + 2, :].rearrange("p b n -> p (b n)")[:, 0:nk * P],
                                        AX, ALU.max, negate=True).then_inc(smax.sem, 1)

            def evacuate(u):
                nk = attn_unit(u)[4]
                na = 2 * nk // 3
                dve.wait_ge(ptt.sem, ptt.n(layer, u + 1))
                if u >= 2:
                    dve.wait_ge(pv.sem, pv.n(layer, u - 1))
                nc.vector.tensor_copy(probT[u % 2][:, na * P:nk * P], ps[:, 5, 0:(nk - na) * P]).then_inc(pt_v.sem, 1)

            def finish(u):
                qt, h, _, _, _ = attn_unit(u)
                dve.wait_ge(expd.sem, expd.n(layer, u + 1))
                link(nc.vector.reciprocal(rinv[:, u:u + 1], rsum[:, u:u + 1]))
                dve.wait_ge(pv.sem, pv.n(layer, u + 1))
                nc.vector.tensor_scalar(ycat[:, qt, h * HD:(h + 1) * HD], ps[:, 6 + u % 2, 0:HD], rinv[:, u:u + 1],
                                        None, ALU.mult).then_inc(attn_y.sem, 1)

            row_max(0)
            for u in range(48):
                if u + 1 < 48:
                    row_max(u + 1)
                evacuate(u)
                if u >= 1:
                    finish(u - 1)
            finish(47)

        def act_attention(act, layer):
            act.wait_ge(qk_ss.sem, qk_ss.n(layer, 1))
            link_act(nc.scalar.activation(rs[:, 0:60], ss2[:, 0:60], ACT.Ln))
            nc.scalar.activation(rs[:, 0:60], rs[:, 0:60], ACT.Exp, scale=-0.5).then_inc(qk_rs.sem, 1)
            for p in range(5):
                act.wait_ge(qkt.sem, qkt.n(layer, p + 1))
                b = 2 * (p % 3)
                nc.scalar.activation(qkT[:, p, 0:512], ps[:, b, :], ACT.Copy)
                nc.scalar.activation(qkT[:, p, 512:768], ps[:, b + 1, 0:256], ACT.Copy).then_inc(qktev.sem, 1)

            def exps(u):
                nk = attn_unit(u)[4]
                act.wait_ge(smax.sem, smax.n(layer, u + 1))
                if u >= 2:
                    act.wait_ge(ptt.sem, ptt.n(layer, u - 1))
                b = 2 * (u % 2)
                nc.scalar.activation(prob[u % 2][:, 0:nk * P],
                                     ps[:, b:b + 2, :].rearrange("p b n -> p (b n)")[:, 0:nk * P], ACT.Exp,
                                     bias=nmax[:, u:u + 1], accum_out=rsum[:, u:u + 1]).then_inc(expd.sem, 1)

            exps(0)
            for u in range(48):
                if u + 1 < 48:
                    exps(u + 1)
                nk = attn_unit(u)[4]
                na = 2 * nk // 3
                act.wait_ge(ptt.sem, ptt.n(layer, u + 1))
                if u >= 2:
                    act.wait_ge(pv.sem, pv.n(layer, u - 1))
                nc.scalar.activation(probT[u % 2][:, 0:na * P], ps[:, 4, 0:na * P], ACT.Copy).then_inc(pt_a.sem, 1)

        def pe_attention(pe, layer):
            pe.wait_ge(qk_ready.sem, qk_ready.n(layer, 1))
            pe.wait_ge(projev.sem, projev.n(layer, 48))
            for p in range(5):
                if p >= 3:
                    pe.wait_ge(qktev.sem, qktev.n(layer, p - 2))
                b = 2 * (p % 3)
                for i in range(NT):
                    ins = nc.tensor.transpose(ps[:, b + i // 4, (i % 4) * P:(i % 4 + 1) * P],
                                              qn[:, i, p * P:(p + 1) * P], ident)
                ins.then_inc(qkt.sem, 1)
            pe.wait_ge(qktev.sem, qktev.n(layer, 5))

            def scores(u):
                qt, h, kv, j, nk = attn_unit(u)
                if u >= 2:
                    pe.wait_ge(expd.sem, expd.n(layer, u - 1))
                b = 2 * (u % 2)
                part = slice(kv * HD, (kv + 1) * HD)
                for n0 in range(0, nk * P, 512):
                    n = min(512, nk * P - n0)
                    ins = nc.tensor.matmul(ps[:, b + n0 // 512, 0:n], lhsT=qkT[part, j, qt * P:(qt + 1) * P],
                                           rhs=qkT[part, 4, n0:n0 + n], start=True, stop=True)
                ins.then_inc(score.sem, 1)

            def turn(u):
                nk = attn_unit(u)[4]
                na = 2 * nk // 3
                pe.wait_ge(expd.sem, expd.n(layer, u + 1))
                if u >= 1:
                    pe.wait_ge(pt_a.sem, pt_a.n(layer, u))
                    pe.wait_ge(pt_v.sem, pt_v.n(layer, u))
                for kt in range(nk):
                    out = ps[:, 4, kt * P:(kt + 1) * P] if kt < na else ps[:, 5, (kt - na) * P:(kt - na + 1) * P]
                    ins = nc.tensor.transpose(out, prob[u % 2][:, kt * P:(kt + 1) * P], ident)
                ins.then_inc(ptt.sem, 1)

            def values(u):
                qt, h, kv, j, nk = attn_unit(u)
                pe.wait_ge(pt_a.sem, pt_a.n(layer, u + 1))
                pe.wait_ge(pt_v.sem, pt_v.n(layer, u + 1))
                if u >= 2:
                    pe.wait_ge(attn_y.sem, attn_y.n(layer, u - 1))
                for kt in range(nk):
                    ins = nc.tensor.matmul(ps[:, 6 + u % 2, 0:HD], lhsT=probT[u % 2][:, kt * P:(kt + 1) * P],
                                           rhs=vtok[:, kt, kv * HD:(kv + 1) * HD], start=(kt == 0), stop=(kt == nk - 1))
                ins.then_inc(pv.sem, 1)

            scores(0)
            for u in range(48):
                if u + 1 < 48:
                    scores(u + 1)
                turn(u)
                if u >= 1:
                    values(u - 1)
            values(47)

        def order(d):
            c, l = list(range(NCH_CTX)), list(range(NCH_CTX, NCH))
            return c + l if d == 0 else c[::-1] + l[::-1]

        HB = [slice(0, 64), slice(64, 128)]

        def head_bc(v):
            return v.unsqueeze(2).broadcast_to([P, DNH, HD])

        def mask_bc(v):
            return v.unsqueeze(1).broadcast_to([P, DNH, HD])

        def dve_deltanet(dve, layer):
            nc.vector.memset(convin[:, :, 0:2], 0.0)
            nc.vector.memset(convin[:, :, 258:262], 0.0)
            link(nc.vector.memset(convin[:, :, 774:776], 0.0))
            dve.wait_ge(projev.sem, projev.n(layer, 48))
            dve.wait_ge(attn_y.sem, attn_y.n(layer, 48))
            for k in range(CONV_K):
                for j in range(6):
                    w = rowsT[:, layer * 30 + k * 6 + j:layer * 30 + k * 6 + j + 1]
                    if k == 0:
                        ins = nc.vector.tensor_scalar(convout[:, j, :], convin[:, j, 0:772], w, None, ALU.mult)
                    else:
                        dve.wait_ge(conv.sem, conv.n(layer, (k - 1) * 6 + j + 1))
                        ins = nc.vector.scalar_tensor_tensor(convout[:, j, :], convin[:, j, k:k + 772], w,
                                                             convout[:, j, :], ALU.mult, ALU.add)
                    ins.then_inc(conv.sem, 1)
            alog, dtb = small[:, layer, 256:264], small[:, layer, 264:272]
            link(nc.vector.tensor_tensor(ga[:, :, :], dz[:, :, 264:272], dtb.unsqueeze(1).broadcast_to([P, NT, 8]),
                                         ALU.add))
            link(nc.vector.tensor_scalar(gb[:, :, :], ga[:, :, :], -1.0, None, ALU.mult))
            nc.vector.tensor_tensor(gb[:, :, :], gb[:, :, :], ga[:, :, :], ALU.min).then_inc(gate_v.sem, 1)
            dve.wait_ge(gate_a.sem, gate_a.n(layer, 4))
            link(nc.vector.tensor_scalar(bt[:, :, :], bt[:, :, :], 1.0, None, ALU.add))
            nc.vector.reciprocal(bt[:, :, :], bt[:, :, :])
            link(nc.vector.scalar_tensor_tensor(gg[:, :, :], ga[:, :, :], 0.0, gb[:, :, :], ALU.max, ALU.add))
            link(nc.vector.scalar_tensor_tensor(gg[:, :, :], gg[:, :, :], -1.0,
                                                ealog[:, :].unsqueeze(1).broadcast_to([P, NT, 8]), ALU.mult, ALU.mult))
            dve.wait_ge(dtev.sem, dtev.n(layer, 6))
            link(nc.vector.tensor_tensor(sq_dn, dt[:, :, 0:512], dt[:, :, 0:512], ALU.mult))
            link(nc.vector.tensor_reduce(ss[:, 0:48], sq_dn.rearrange("p i (h d) -> p (i h) d", d=HD), AX, ALU.add))
            nc.vector.tensor_scalar(ss2[:, 0:48], ss[:, 0:48], EPS, None, ALU.add).then_inc(dn_ss.sem, 1)
            dve.wait_ge(dn_rs.sem, dn_rs.n(layer, 1))
            rq = rs[:, 0:48].rearrange("p (i h) -> p i h", h=8)[:, :, 0:DNH]
            link(nc.vector.tensor_scalar(rq, rq, HD ** -0.5, None, ALU.mult))
            for i in range(NT):
                v = dt[:, i, 0:512].rearrange("p (h d) -> p h d", d=HD)
                nc.vector.tensor_tensor(v, v, rs[:, 8 * i:8 * i + 8].unsqueeze(2).broadcast_to([P, 8, HD]),
                                        ALU.mult).then_inc(dn_norm.sem, 1)
            dve.wait_ge(kqtev.sem, kqtev.n(layer, 6))
            for d in range(2):
                base = 6 * d
                causal = cst(f"causal{d}")
                for i in range(NT):
                    nc.vector.tensor_tensor(NL[:, i], mask_bc(causal), head_bc(gg[:, i, 4 * d:4 * d + 4]),
                                            ALU.mult).then_inc(gbr.sem, 1)
                dve.wait_ge(dexp.sem, dexp.n(layer, 7 * d + 7))
                link(nc.vector.tensor_tensor(eb[:, :, :], sc[:, 24:48].rearrange("p (i h) -> p i h", h=4),
                                             bt[:, :, 4 * d:4 * d + 4], ALU.mult))
                for i in range(NT):
                    k_ = dt[:, i, 256:512].rearrange("p (h d) -> p h d", d=HD)
                    nc.vector.tensor_tensor(vke[:, i, :, HD:2 * HD], k_, head_bc(sc[:, 4 * i:4 * i + 4]), ALU.mult)
                    ins = nc.vector.tensor_tensor(kbe[:, i], k_, head_bc(eb[:, i, :]), ALU.mult)
                ins.then_inc(kev.sem, 1)
                for i in range(NT):
                    link(nc.vector.tensor_tensor(Dm[:, i], Dm[:, i], mask_bc(causal), ALU.mult))
                    dve.wait_ge(gram.sem, gram.n(layer, base + i + 1))
                    for hb in range(2):
                        bank = 2 * (i % 3) + hb
                        src = ps[:, bank, 0:256].rearrange("p (b k t) -> p b k t", b=2, k=2)
                        hs = Dm[:, i].rearrange("p (b h) t -> p b h t", h=2)[:, :, hb, :]
                        nc.vector.tensor_tensor(AT[:, i].rearrange("p (b h) t -> p b h t", h=2)[:, :, hb, :], hs,
                                                src[:, :, 1, :], ALU.mult)
                        ins = nc.vector.tensor_tensor(NTm[:, i].rearrange("p (b h) t -> p b h t", h=2)[:, :, hb, :], hs,
                                                      src[:, :, 0, :], ALU.mult)
                    link(ins)
                    nc.vector.tensor_tensor(NTm[:, i], NTm[:, i], head_bc(bt[:, i, 4 * d:4 * d + 4]), ALU.mult) \
                        .then_inc(pairs.sem, 1)
                for level in range(LEVELS):
                    m = mask_bc(lvl[d][:, level, :])
                    first = 36 * d + 6 * level
                    for i in range(NT):
                        if level == 0:
                            dve.wait_ge(pairs.sem, pairs.n(layer, base + i + 1))
                        else:
                            dve.wait_ge(umm.sem, umm.n(layer, first - 6 + i + 1))
                            if level == 1:
                                dve.wait_ge(tru.sem, tru.n(layer, first - 6 + i + 1))
                        ins = nc.vector.tensor_tensor(NL[:, i], NTm[:, i], m, ALU.mult)
                        ins.then_inc(nl.sem, 1)
                    for i in range(NT):
                        i64 = mask_bc(cst("ident64"))
                        if level == 0:
                            dve.wait_ge(nl.sem, nl.n(layer, first + i + 1))
                            nc.vector.tensor_tensor(TR[:, i, 1], i64, NL[:, i], ALU.subtract)
                            dve.wait_ge(umm.sem, umm.n(layer, first + i + 1))
                            ins = nc.vector.tensor_tensor(TR[:, i, 0], i64,
                                                          ps[:, 6 + i % 2, 0:256].rearrange("p (h t) -> p h t", h=4),
                                                          ALU.subtract)
                        else:
                            dve.wait_ge(trm.sem, trm.n(layer, 30 * d + 6 * (level - 1) + i + 1))
                            if level < LEVELS - 1:
                                v = TR[:, i].rearrange("p a h t -> p (a h t)")
                                src = ps[:, i, :]
                            else:
                                v = TR[:, i, 1].rearrange("p h t -> p (h t)")
                                src = ps[:, i, 256:512]
                            ins = nc.vector.tensor_tensor(v, v, src, ALU.subtract)
                        ins.then_inc(tru.sem, 1)
                for i in range(NT):
                    dve.wait_ge(gmm.sem, gmm.n(layer, base + i + 1))
                    for par in range(2):
                        c = 2 * i + par
                        for pair in range(2):
                            for hb in range(2):
                                h = 2 * pair + hb
                                ins = nc.vector.scalar_tensor_tensor(
                                    G[HB[hb], c, pair, :], cst("ident64")[HB[hb], :],
                                    sc[HB[hb], 48 + 4 * c + h:49 + 4 * c + h],
                                    ps[HB[hb], 2 * (i % 2) + par, 128 + 64 * pair:192 + 64 * pair],
                                    ALU.mult, ALU.subtract)
                    ins.then_inc(gev_v.sem, 1)
                seq = order(d)
                nc.vector.memset(S[:, seq[0], :, :], 0.0).then_inc(stepv.sem, 1)
                dve.wait_ge(gev_a.sem, gev_a.n(layer, base + 6))
                for n in range(NCH - 1):
                    dve.wait_ge(step.sem, step.n(layer, 11 * d + n + 1))
                    nc.vector.tensor_tensor(S[:, seq[n + 1], :, :],
                                            ps[:, 4 + n % 2, 0:128].rearrange("p (b v) -> p b v", b=2),
                                            Uc[:, seq[n], :, :], ALU.add).then_inc(stepv.sem, 1)
                def fresh_values(i):
                    dve.wait_ge(zmm.sem, zmm.n(layer, base + i + 1))
                    for hb in range(2):
                        bank = 2 * (i % 2) + hb
                        src = ps[:, bank, 0:256].rearrange("p (k b t) -> p k b t", k=2, b=2)
                        vn = vnew[:, i].rearrange("p (b h) t -> p b h t", h=2)[:, :, hb, :]
                        yv = ysol[:, i, :, 0:HD].rearrange("p (b h) t -> p b h t", h=2)[:, :, hb, :]
                        nc.vector.tensor_tensor(vn, yv, src[:, 0], ALU.subtract)
                        ecum = sc[:, 4 * i:4 * i + 4].rearrange("p (b h) -> p b h", h=2)[:, :, hb:hb + 1] \
                            .broadcast_to([P, 2, HD])
                        ot = otmp[:, i].rearrange("p (b h) t -> p b h t", h=2)[:, :, hb, :]
                        ins = nc.vector.tensor_tensor(ot, src[:, 1], ecum, ALU.mult)
                    link(ins)
                    nc.vector.tensor_tensor(vnew[:, i], vnew[:, i], head_bc(bt[:, i, 4 * d:4 * d + 4]), ALU.mult) \
                        .then_inc(vnw.sem, 1)

                def outputs(i):
                    dve.wait_ge(avm.sem, avm.n(layer, base + i + 1))
                    yd = ycat[:, i, 512:768]
                    ot = otmp[:, i].rearrange("p h t -> p (h t)")
                    src = ps[:, 4 + i % 2, 0:256]
                    if d == 0:
                        nc.vector.tensor_tensor(yd, ot, src, ALU.add).then_inc(outv.sem, 1)
                    else:
                        link(nc.vector.tensor_tensor(ot, ot, src, ALU.add))
                        nc.vector.tensor_tensor(yd, yd, ot, ALU.add).then_inc(outv.sem, 1)

                for i in range(NT):
                    fresh_values(i)
                    if i >= 1:
                        outputs(i - 1)
                outputs(NT - 1)
                dve.wait_ge(outv.sem, outv.n(layer, base + 6))
            dve_gated(dve, layer, 0, 512, dz[:, :, 0:256])

        def dve_gated(dve, layer, which, c0, z):
            o = ycat[:, :, c0:c0 + 256]
            link(nc.vector.tensor_tensor(sqg, o, o, ALU.mult))
            link(nc.vector.tensor_reduce(ss[:, 0:24], sqg.rearrange("p i (h d) -> p (i h) d", d=HD), AX, ALU.add))
            nc.vector.tensor_scalar(ss2[:, 0:24], ss[:, 0:24], 1.0 / HD, EPS, ALU.mult, ALU.add) \
                .then_inc(go_ss.sem, 1)
            dve.wait_ge(go_rs.sem, go_rs.n(layer, which + 1))
            w = small[:, layer, (2 + which) * HD:(3 + which) * HD]
            for i in range(NT):
                oh = ycat[:, i, c0:c0 + 256].rearrange("p (h d) -> p h d", d=HD)
                nc.vector.tensor_tensor(oh, oh, head_bc(rs[:, 4 * i:4 * i + 4]), ALU.mult)
                zh = z[:, i, :].rearrange("p (h d) -> p h d", d=HD)
                ins = nc.vector.tensor_tensor(zh, zh, mask_bc(w), ALU.mult)
            link(ins)
            link(nc.vector.tensor_tensor(o, o, z, ALU.mult))

        def act_gated(act, layer, which):
            act.wait_ge(go_ss.sem, go_ss.n(layer, which + 1))
            link_act(nc.scalar.activation(rs[:, 0:24], ss2[:, 0:24], ACT.Ln))
            nc.scalar.activation(rs[:, 0:24], rs[:, 0:24], ACT.Exp, scale=-0.5).then_inc(go_rs.sem, 1)

        def act_deltanet(act, layer):
            for j in range(6):
                act.wait_ge(conv.sem, conv.n(layer, 24 + j + 1))
                nc.scalar.activation(convout[:, j, :], convout[:, j, :], ACT.Silu).then_inc(convact.sem, 1)
            nc.scalar.activation(bt[:, :, :], dz[:, :, 256:264], ACT.Exp, scale=-1.0).then_inc(gate_a.sem, 1)
            nc.scalar.activation(ealog[:, :], small[:, layer, 256:264], ACT.Exp).then_inc(gate_a.sem, 1)
            act.wait_ge(gate_v.sem, gate_v.n(layer, 1))
            nc.scalar.activation(gb[:, :, :], gb[:, :, :], ACT.Exp).then_inc(gate_a.sem, 1)
            act.wait_ge(gate_a.sem, gate_a.n(layer, 3))
            nc.scalar.activation(gb[:, :, :], gb[:, :, :], ACT.Ln, bias=1.0).then_inc(gate_a.sem, 1)
            for i in range(NT):
                act.wait_ge(dtt.sem, dtt.n(layer, i + 1))
                b = 2 * (i % 3)
                nc.scalar.activation(dt[:, i, 0:512], ps[:, b, :], ACT.Copy)
                nc.scalar.activation(dt[:, i, 512:768], ps[:, b + 1, 0:256], ACT.Copy).then_inc(dtev.sem, 1)
            act.wait_ge(dn_ss.sem, dn_ss.n(layer, 1))
            link_act(nc.scalar.activation(rs[:, 0:48], ss2[:, 0:48], ACT.Ln))
            nc.scalar.activation(rs[:, 0:48], rs[:, 0:48], ACT.Exp, scale=-0.5).then_inc(dn_rs.sem, 1)
            for i in range(NT):
                act.wait_ge(kqt.sem, kqt.n(layer, i + 1))
                for kind in range(2):
                    ins = nc.scalar.activation(
                        kqT[:, :, 2 * i:2 * i + 2, kind, :],
                        ps[:, 2 * (i % 3), 256 * kind:256 * kind + 256].rearrange("p (b c t) -> p b c t", b=2, c=2),
                        ACT.Copy)
                ins.then_inc(kqtev.sem, 1)
            for d in range(2):
                base = 6 * d
                if d == 1:
                    act.wait_ge(outv.sem, outv.n(layer, 6))
                for i in range(NT):
                    act.wait_ge(decay.sem, decay.n(layer, base + i + 1))
                    nc.scalar.activation(Dm[:, i], ps[:, i, 0:256].rearrange("p (h t) -> p h t", h=4), ACT.Exp) \
                        .then_inc(dexp.sem, 1)
                nc.scalar.activation(sc[:, :], ps[:, 6, 0:96], ACT.Exp).then_inc(dexp.sem, 1)
                nc.scalar.activation(vke[:, :, :, 0:HD], dt[:, :, 512:768].rearrange("p i (h d) -> p i h d", d=HD),
                                     ACT.Copy).then_inc(vke_v.sem, 1)
                for level in range(1, LEVELS):
                    for i in range(NT):
                        act.wait_ge(umm.sem, umm.n(layer, 36 * d + 6 * level + i + 1))
                        if level == 1:
                            act.wait_ge(pairs.sem, pairs.n(layer, base + 6))
                        if level > 1:
                            act.wait_ge(trm.sem, trm.n(layer, 30 * d + 6 * (level - 2) + i + 1))
                        nc.scalar.activation(Um[:, i], ps[:, 6 + i % 2, 0:256].rearrange("p (h t) -> p h t", h=4),
                                             ACT.Copy).then_inc(uev.sem, 1)
                for i in range(NT):
                    act.wait_ge(ymm.sem, ymm.n(layer, base + i + 1))
                    nc.scalar.activation(ysol[:, i].rearrange("p h t -> p (h t)"), ps[:, i, :], ACT.Copy) \
                        .then_inc(yev.sem, 1)
                for i in range(NT):
                    act.wait_ge(gmm.sem, gmm.n(layer, base + i + 1))
                    act.wait_ge(gev_v.sem, gev_v.n(layer, base + i + 1))
                    for par in range(2):
                        bank = 2 * (i % 2) + par
                        nc.scalar.activation(ykT[:, i, :, par, :], ps[:, bank, 0:128].rearrange("p (b t) -> p b t", b=2),
                                             ACT.Copy)
                        ins = nc.scalar.activation(Uc[:, 2 * i + par, :, :],
                                                   ps[:, bank, 256:384].rearrange("p (b t) -> p b t", b=2), ACT.Copy)
                    ins.then_inc(gev_a.sem, 1)
            act_gated(act, layer, 0)

        def pe_deltanet(pe, layer):
            pe.wait_ge(attn_y.sem, attn_y.n(layer, 48))
            pe.wait_ge(convact.sem, convact.n(layer, 6))
            for i in range(NT):
                if i >= 3:
                    pe.wait_ge(dtev.sem, dtev.n(layer, i - 2))
                c0 = i * P if i < NT_CTX else i * P + 4
                for j in range(6):
                    ins = nc.tensor.transpose(ps[:, 2 * (i % 3) + j // 4, (j % 4) * P:(j % 4 + 1) * P],
                                              convout[:, j, c0:c0 + P], ident)
                ins.then_inc(dtt.sem, 1)
            pe.wait_ge(dtev.sem, dtev.n(layer, 6))
            for i in range(NT):
                pe.wait_ge(dn_norm.sem, dn_norm.n(layer, i + 1))
                if i >= 3:
                    pe.wait_ge(kqtev.sem, kqtev.n(layer, i - 2))
                for n, c0 in enumerate((256, 384, 0, 128)):
                    ins = nc.tensor.transpose(ps[:, 2 * (i % 3), n * P:(n + 1) * P], dt[:, i, c0:c0 + P], ident)
                ins.then_inc(kqt.sem, 1)
            pe.wait_ge(kqtev.sem, kqtev.n(layer, 6))
            for d in range(2):
                base = 6 * d
                if d == 1:
                    pe.wait_ge(outv.sem, outv.n(layer, 6))
                strict, incl = cst(f"strict{d}"), cst(f"incl{d}")
                ind = cst("chunkind").rearrange("p (c m) -> p c m", c=2)
                for i in range(NT):
                    pe.wait_ge(gbr.sem, gbr.n(layer, base + i + 1))
                    g = gg[:, i, 4 * d:4 * d + 4]
                    for out, lhs in ((ps[:, 6, 4 * i:4 * i + 4], incl), (ps[:, 6, 24 + 4 * i:28 + 4 * i], strict),
                                     (ps[:, 6, 48 + 8 * i:52 + 8 * i], ind[:, 0, :]),
                                     (ps[:, 6, 52 + 8 * i:56 + 8 * i], ind[:, 1, :])):
                        nc.tensor.matmul(out, lhsT=lhs, rhs=g, start=True, stop=True)
                    nc.tensor.matmul(ps[:, i, 0:256], lhsT=strict, rhs=NL[:, i].rearrange("p h t -> p (h t)"),
                                     start=True, stop=True).then_inc(decay.sem, 1)
                pe.wait_ge(dexp.sem, dexp.n(layer, 7 * d + 7))
                for i in range(NT):
                    if i >= 3:
                        pe.wait_ge(pairs.sem, pairs.n(layer, base + i - 2))
                    for hb in range(2):
                        for par in range(2):
                            c = 2 * i + par
                            for pair in range(2):
                                ins = nc.tensor.matmul(
                                    ps[HB[par], 2 * (i % 3) + hb, 128 * pair:128 * pair + 128],
                                    lhsT=kqT[HB[hb], pair, c, 0, :],
                                    rhs=kqT[HB[hb], pair, c, :, :].rearrange("p k t -> p (k t)"),
                                    start=True, stop=True)
                    ins.then_inc(gram.sem, 1)

                def small_products(bank, c0, lhs, rhs, i, width=64):
                    for par in range(2):
                        for h in range(DNH):
                            ins = nc.tensor.matmul(ps[HB[par], bank, c0 + width * h:c0 + width * (h + 1)],
                                                   lhsT=lhs[HB[par], i, h, :], rhs=rhs(par, h), start=True, stop=True)
                    return ins

                for level in range(LEVELS):
                    first = 36 * d + 6 * level

                    def products(i, level=level, first=first):
                        pe.wait_ge(uev.sem, uev.n(layer, 30 * d + 6 * (level - 1) + i + 1))
                        if level < LEVELS - 1:
                            small_products(i, 0, TR[:, :, 1], lambda par, h: Um[HB[par], i, h, :], i)
                        ins = small_products(i, 256, Um, lambda par, h: TR[HB[par], i, 1, h, :], i)
                        ins.then_inc(trm.sem, 1)

                    for i in range(NT):
                        pe.wait_ge(nl.sem, nl.n(layer, first + i + 1))
                        if level == 0:
                            if i == 0:
                                pe.wait_ge(pairs.sem, pairs.n(layer, base + 6))
                            if i >= 2:
                                pe.wait_ge(tru.sem, tru.n(layer, first + i - 1))
                            rhs = lambda par, h: cst("ident64")[HB[par], :]
                        else:
                            pe.wait_ge(tru.sem, tru.n(layer, first - 6 + i + 1))
                            if level == 1 and i < 2:
                                pe.wait_ge(tru.sem, tru.n(layer, first))
                            if 6 * (level - 1) + i >= 2:
                                pe.wait_ge(uev.sem, uev.n(layer, 30 * d + 6 * (level - 1) + i - 1))
                            rhs = lambda par, h, i=i: TR[HB[par], i, 0, h, :]
                        small_products(6 + i % 2, 0, NL, rhs, i).then_inc(umm.sem, 1)
                        if level >= 1 and i >= 1:
                            products(i - 1)
                    if level >= 1:
                        products(NT - 1)
                pe.wait_ge(vke_v.sem, vke_v.n(layer, d + 1))
                pe.wait_ge(kev.sem, kev.n(layer, d + 1))
                pe.wait_ge(tru.sem, tru.n(layer, 36 * d + 36))
                for i in range(NT):
                    small_products(i, 0, TR[:, :, 1], lambda par, h: vke[HB[par], i, h, :], i, width=128) \
                        .then_inc(ymm.sem, 1)
                pe.wait_ge(yev.sem, yev.n(layer, base + 6))
                for i in range(NT):
                    if i >= 2:
                        pe.wait_ge(gev_a.sem, gev_a.n(layer, base + i - 1))
                    for par in range(2):
                        for pair in range(2):
                            for hb in range(2):
                                h = 2 * pair + hb
                                out = ps[HB[hb], 2 * (i % 2) + par, :]
                                nc.tensor.matmul(out[:, 64 * pair:64 * pair + 64], lhsT=vke[HB[par], i, h, HD:2 * HD],
                                                 rhs=TR[HB[par], i, 1, h, :], start=True, stop=True)
                                nc.tensor.matmul(out[:, 128 + 64 * pair:192 + 64 * pair],
                                                 lhsT=ysol[HB[par], i, h, HD:2 * HD], rhs=kbe[HB[par], i, h, :],
                                                 start=True, stop=True)
                                ins = nc.tensor.matmul(out[:, 256 + 64 * pair:320 + 64 * pair],
                                                       lhsT=kbe[HB[par], i, h, :], rhs=ysol[HB[par], i, h, 0:HD],
                                                       start=True, stop=True)
                    ins.then_inc(gmm.sem, 1)
                pe.wait_ge(gev_a.sem, gev_a.n(layer, base + 6))
                seq = order(d)
                for n in range(NCH - 1):
                    pe.wait_ge(stepv.sem, stepv.n(layer, 12 * d + n + 1))
                    for pair in range(2):
                        for hb in range(2):
                            ins = nc.tensor.matmul(ps[HB[hb], 4 + n % 2, 64 * pair:64 * pair + 64],
                                                   lhsT=G[HB[hb], seq[n], pair, :], rhs=S[HB[hb], seq[n], pair, :],
                                                   start=True, stop=True)
                    ins.then_inc(step.sem, 1)
                pe.wait_ge(stepv.sem, stepv.n(layer, 12 * d + NCH))

                def apply_values(i):
                    pe.wait_ge(vnw.sem, vnw.n(layer, base + i + 1))
                    if i >= 2:
                        pe.wait_ge(outv.sem, outv.n(layer, base + i - 1))
                    small_products(4 + i % 2, 0, AT, lambda par, h: vnew[HB[par], i, h, :], i).then_inc(avm.sem, 1)

                for i in range(NT):
                    if i >= 2:
                        pe.wait_ge(vnw.sem, vnw.n(layer, base + i - 1))
                    for hb in range(2):
                        for par in range(2):
                            c = 2 * i + par
                            for pair in range(2):
                                out = ps[HB[par], 2 * (i % 2) + hb, :]
                                nc.tensor.matmul(out[:, 64 * pair:64 * pair + 64], lhsT=ykT[HB[hb], i, pair, par, :],
                                                 rhs=S[HB[hb], c, pair, :], start=True, stop=True)
                                ins = nc.tensor.matmul(out[:, 128 + 64 * pair:192 + 64 * pair],
                                                       lhsT=kqT[HB[hb], pair, c, 1, :], rhs=S[HB[hb], c, pair, :],
                                                       start=True, stop=True)
                    ins.then_inc(zmm.sem, 1)
                    if i >= 1:
                        apply_values(i - 1)
                apply_values(NT - 1)


        def dve_hgrn(dve, layer):
            V = hgt[:, :, 0:256]
            for d in range(2):
                f = hgc[:, 2 + 2 * d:4 + 2 * d, :]
                if d == 0:
                    link(nc.vector.memset(reset, 1.0))
                    link(nc.vector.memset(reset[:, :, 0:1], 0.0))
                nc.vector.memset(gpad[:, :, :, 0:1], 0.0)
                link(nc.vector.memset(Ah, 0.0))
                dve.wait_ge(f_a.sem, f_a.n(layer, d + 1))
                link(nc.vector.tensor_scalar(f, f, 1.0, None, ALU.add))
                link(nc.vector.reciprocal(f, f))
                for j in range(2):
                    n = 2 * d + j
                    ins = nc.vector.tensor_scalar(f[:, j, :], f[:, j, :], omlT[:, layer, n:n + 1],
                                                  lbT[:, layer, n:n + 1], ALU.mult, ALU.add)
                ins.then_inc(f_v.sem, 1)
                dve.wait_ge(f_v.sem, f_v.n(layer, d + 1))
                nc.vector.tensor_scalar(kk, f, -1.0, 1.0, ALU.mult, ALU.add)
                dve.wait_ge(g_a.sem, g_a.n(layer, d + 1))
                for j in range(2):
                    ins = nc.vector.tensor_tensor_scan(Cc[:, j].rearrange("p c t -> p (c t)"),
                                                       reset.rearrange("p c t -> p (c t)"),
                                                       gpad[:, j].rearrange("p c t -> p (c t)"), 0.0, ALU.mult, ALU.add)
                link(ins)
                off = 1 - d
                for j in range(2):
                    xs = Cc[:, j, :, off:off + CHUNK]
                    ins = nc.vector.tensor_tensor(ER[:, j].rearrange("p (c t) -> p c t", c=NCH),
                                                  Cc[:, j, :, CHUNK:CHUNK + 1].broadcast_to([P, NCH, CHUNK]), xs,
                                                  ALU.subtract)
                ins.then_inc(er_v.sem, 1)

                def halves(v, level, half):
                    h = 1 << level
                    return v.rearrange("p (a f h) -> p a f h", f=2, h=h)[:, :, half, :]

                def distance(n):
                    level, j = divmod(n, 2)
                    h = 1 << level
                    nb = CHUNK // (2 * h)
                    if n >= 4:
                        dve.wait_ge(hgram.sem, hgram.n(layer, 14 * d + n - 3))
                    xs = Cc[:, j, :, off:off + CHUNK].rearrange("p c (b f h) -> p c b f h", f=2, h=h)
                    mid = Cc[:, j, :, h:h + (nb - 1) * 2 * h + 1:2 * h].unsqueeze(3).broadcast_to([P, NCH, nb, h])
                    z = Z[n % 4].rearrange("p (c b f h) -> p c b f h", c=NCH, f=2, h=h)
                    nc.vector.tensor_tensor(z[:, :, :, 0, :], mid, xs[:, :, :, 0, :], ALU.subtract)
                    nc.vector.tensor_tensor(z[:, :, :, 1, :], xs[:, :, :, 1, :], mid, ALU.subtract) \
                        .then_inc(zsub.sem, 1)

                def weigh(n):
                    level, j = divmod(n, 2)
                    dve.wait_ge(zexp.sem, zexp.n(layer, 12 * d + n + 1))
                    z = Z[n % 4]
                    for half in range(2):
                        other = kk[:, j, :] if half == d else hgc[:, j, :]
                        ins = nc.vector.tensor_tensor(halves(z, level, half), halves(z, level, half),
                                                      halves(other, level, half), ALU.mult)
                    ins.then_inc(zmul.sem, 1)

                def place(n):
                    level, j = divmod(n, 2)
                    dve.wait_ge(hgram.sem, hgram.n(layer, 14 * d + n + 1))
                    m = lvl_i[d][:, level, :].unsqueeze(1).broadcast_to([P, NT, HD])
                    if n >= 2:
                        dve.wait_ge(hpred.sem, hpred.n(layer, 14 * d + n - 1))
                    for hb in range(2):
                        ins = nc.vector.copy_predicated(
                            Ah[:, 2 * j + hb], m,
                            ps[:, 2 * (n % 3) + hb, 0:384].rearrange("p (i t) -> p i t", i=NT))
                    ins.then_inc(hpred.sem, 1)

                distance(0)
                for n in range(14):
                    if n + 1 < 12:
                        distance(n + 1)
                    if n < 12:
                        weigh(n)
                    if n == 2:
                        dve.wait_ge(er_a.sem, er_a.n(layer, d + 1))
                        qd, kd = (ED, ER) if d == 0 else (ER, ED)
                        nc.vector.tensor_tensor(qd, qd, hgc[:, 0:2, :], ALU.mult)
                        nc.vector.tensor_tensor(kd, kd, kk, ALU.mult).then_inc(qe_v.sem, 1)
                    if n >= 1:
                        place(n - 1)
                place(13)
                seq = order(d)
                link(nc.vector.memset(Sh[:, seq[0], :, :], 0.0))
                dve.wait_ge(uhev.sem, uhev.n(layer, 6 * d + 6))
                for n in range(NCH - 1):
                    for pair in range(2):
                        ins = nc.vector.scalar_tensor_tensor(Sh[:, seq[n + 1], pair, :], Sh[:, seq[n], pair, :],
                                                             ec[:, pair, seq[n]:seq[n] + 1], Uh[:, seq[n], pair, :],
                                                             ALU.mult, ALU.add)
                    if n < NCH - 2:
                        link(ins)
                ins.then_inc(hstate.sem, 1)
                for i in range(NT):
                    dve.wait_ge(hout.sem, hout.n(layer, 6 * d + i + 1))
                    y = ycat[:, i, 768:1024]
                    for hb in range(2):
                        dst = y.rearrange("p (b h t) -> p b h t", b=2, h=2)[:, :, hb, :]
                        src = ps[:, 2 * (i % 2) + hb, 0:128].rearrange("p (b t) -> p b t", b=2)
                        if d == 0:
                            ins = nc.vector.tensor_copy(dst, src)
                        else:
                            ins = nc.vector.tensor_tensor(dst, dst, src, ALU.add)
                    link(ins)
                    nc.vector.tensor_tensor(y, y, ps[:, 4 + i % 2, 0:256], ALU.add).then_inc(houtv.sem, 1)
                dve.wait_ge(houtv.sem, houtv.n(layer, 6 * d + 6))
            dve_gated(dve, layer, 1, 768, hgt[:, :, 256:512])
            nc.vector.memset(ss[:, 60:61], 0.0).then_inc(mixed.sem, 1)

        def act_hgrn(act, layer):
            for d in range(2):
                f = hgc[:, 2 + 2 * d:4 + 2 * d, :]
                if d == 1:
                    act.wait_ge(houtv.sem, houtv.n(layer, 6))
                else:
                    act.wait_ge(outv.sem, outv.n(layer, 12))
                nc.scalar.activation(f, f, ACT.Exp, scale=-1.0).then_inc(f_a.sem, 1)
                act.wait_ge(f_v.sem, f_v.n(layer, d + 1))
                for j in range(2):
                    ins = nc.scalar.activation(gpad[:, j, :, 1:CHUNK + 1],
                                               f[:, j, :].rearrange("p (c t) -> p c t", c=NCH), ACT.Ln)
                ins.then_inc(g_a.sem, 1)
                off = 1 - d

                def exps(n):
                    act.wait_ge(zsub.sem, zsub.n(layer, 12 * d + n + 1))
                    nc.scalar.activation(Z[n % 4], Z[n % 4], ACT.Exp).then_inc(zexp.sem, 1)

                act.wait_ge(er_v.sem, er_v.n(layer, d + 1))
                exps(0)
                for j in range(2):
                    nc.scalar.activation(ED[:, j].rearrange("p (c t) -> p c t", c=NCH), Cc[:, j, :, off:off + CHUNK],
                                         ACT.Exp)
                nc.scalar.activation(ec[:, :, :], Cc[:, :, :, CHUNK:CHUNK + 1].rearrange("p j c o -> p j (c o)"), ACT.Exp)
                nc.scalar.activation(ER, ER, ACT.Exp).then_inc(er_a.sem, 1)
                for n in range(1, 12):
                    exps(n)
                for i in range(NT):
                    act.wait_ge(kett.sem, kett.n(layer, 6 * d + i + 1))
                    nc.scalar.activation(ket[:, i, :], ps[:, 6 + i % 2, 0:256], ACT.Copy).then_inc(ketev.sem, 1)
                for i in range(NT):
                    act.wait_ge(umh.sem, umh.n(layer, 6 * d + i + 1))
                    for par in range(2):
                        ins = nc.scalar.activation(Uh[:, 2 * i + par, :, :],
                                                   ps[:, 2 * (i % 2) + par, 0:128].rearrange("p (b t) -> p b t", b=2),
                                                   ACT.Copy)
                    ins.then_inc(uhev.sem, 1)
            act_gated(act, layer, 1)

        def pe_hgrn(pe, layer):
            pe.wait_ge(outv.sem, outv.n(layer, 12))
            for d in range(2):
                for n in range(14):
                    level, j = divmod(n, 2)
                    if n < 12:
                        pe.wait_ge(zmul.sem, zmul.n(layer, 12 * d + n + 1))
                    if n >= 3:
                        pe.wait_ge(hpred.sem, hpred.n(layer, 14 * d + n - 2))
                    for hb in range(2):
                        for c in range(NCH):
                            sl = slice(c * CHUNK, (c + 1) * CHUNK)
                            if n < 12:
                                a = b = Z[n % 4][HB[hb], sl]
                            else:
                                a, b = kk[HB[hb], j, sl], hgc[HB[hb], j, sl]
                            ins = nc.tensor.matmul(ps[HB[c % 2], 2 * (n % 3) + hb, c // 2 * HD:c // 2 * HD + HD],
                                                   lhsT=a, rhs=b, start=True, stop=True)
                    ins.then_inc(hgram.sem, 1)
                pe.wait_ge(qe_v.sem, qe_v.n(layer, d + 1))
                kd = ER if d == 0 else ED
                qd = ED if d == 0 else ER
                for i in range(NT):
                    if i >= 2:
                        pe.wait_ge(ketev.sem, ketev.n(layer, 6 * d + i - 1))
                    for j in range(2):
                        ins = nc.tensor.transpose(ps[:, 6 + i % 2, j * P:(j + 1) * P], kd[:, j, i * P:(i + 1) * P], ident)
                    ins.then_inc(kett.sem, 1)
                pe.wait_ge(hpred.sem, hpred.n(layer, 14 * d + 14))
                for i in range(NT):
                    pe.wait_ge(ketev.sem, ketev.n(layer, 6 * d + i + 1))
                    if i >= 2:
                        pe.wait_ge(uhev.sem, uhev.n(layer, 6 * d + i - 1))
                    for par in range(2):
                        for h in range(DNH):
                            hb, pair = h % 2, h // 2
                            ins = nc.tensor.matmul(ps[HB[hb], 2 * (i % 2) + par, HD * pair:HD * pair + HD],
                                                   lhsT=ket[HB[par], i, h * HD:(h + 1) * HD],
                                                   rhs=hgt[HB[par], i, h * HD:(h + 1) * HD], start=True, stop=True)
                    ins.then_inc(umh.sem, 1)
                pe.wait_ge(hstate.sem, hstate.n(layer, d + 1))
                for i in range(NT):
                    if i >= 2:
                        pe.wait_ge(houtv.sem, houtv.n(layer, 6 * d + i - 1))
                    for par in range(2):
                        c = 2 * i + par
                        for h in range(DNH):
                            hb, pair = h % 2, h // 2
                            nc.tensor.matmul(ps[HB[par], 2 * (i % 2) + hb, HD * pair:HD * pair + HD],
                                             lhsT=qd[HB[hb], pair, c * CHUNK:(c + 1) * CHUNK],
                                             rhs=Sh[HB[hb], c, pair, :], start=True, stop=True)
                            ins = nc.tensor.matmul(ps[HB[par], 4 + i % 2, HD * h:HD * h + HD],
                                                   lhsT=Ah[HB[par], h, i, :], rhs=hgt[HB[par], i, h * HD:(h + 1) * HD],
                                                   start=True, stop=True)
                    ins.then_inc(hout.sem, 1)
                pe.wait_ge(houtv.sem, houtv.n(layer, 6 * d + 6))

        def pe_out(pe, layer):
            pe.wait_ge(mixed.sem, mixed.n(layer, 1))
            for f in range(KT):
                if f >= 3:
                    evacuated = (yt_a, yt_v)[(f - 3) % 2]
                    pe.wait_ge(evacuated.sem, evacuated.n(layer, (f - 3) // 2 + 1))
                for i in range(NT):
                    ins = nc.tensor.transpose(ps[:, 2 * (f % 3) + i // 4, (i % 4) * P:(i % 4 + 1) * P],
                                              ycat[:, i, f * P:(f + 1) * P], ident)
                ins.then_inc(yt.sem, 1)
            for n in range(4):
                v, half = divmod(n, 2)
                if n >= 2:
                    pe.wait_ge(gbev.sem, gbev.n(layer, n - 1))
                nc.tensor.matmul(ps[:, 6 + n % 2, :], lhsT=sel2[:, v, :], rhs=gates[:, 0, half * 512:half * 512 + 512],
                                 start=True, stop=True).then_inc(gbmm.sem, 1)
            pe.wait_ge(yt_a.sem, yt_a.n(layer, 4))
            pe.wait_ge(yt_v.sem, yt_v.n(layer, 4))
            for g in range(2):
                w = staged(pe, layer, N_MOD + len(GROUPS) + g)
                for i in range(NT):
                    u = 6 * g + i
                    if u >= 6:
                        pe.wait_ge(wov.sem, wov.n(layer, u - 5))
                    for f in range(KT):
                        ins = nc.tensor.matmul(ps[:, u % 6, :], lhsT=yT[:, f, i * P:(i + 1) * P], rhs=w[:, f, :],
                                               start=(f == 0), stop=(f == KT - 1))
                    ins.then_inc(wo.sem, 1)
                pe.wait_ge(wo.sem, wo.n(layer, 6 * g + 6))
                pe.sem_inc(wfree.sem, 1)

        def act_out(act, layer):
            for f in range(0, KT, 2):
                act.wait_ge(yt.sem, yt.n(layer, f + 1))
                b = 2 * (f % 3)
                nc.scalar.activation(yT[:, f, 0:512], ps[:, b, :], ACT.Copy)
                nc.scalar.activation(yT[:, f, 512:768], ps[:, b + 1, 0:256], ACT.Copy).then_inc(yt_a.sem, 1)
            for n in range(4):
                v, half = divmod(n, 2)
                act.wait_ge(gbmm.sem, gbmm.n(layer, n + 1))
                nc.scalar.activation(gbc[:, v, half * 512:half * 512 + 512], ps[:, 6 + n % 2, :], ACT.Copy) \
                    .then_inc(gbev.sem, 1)

        def dve_out(dve, layer):
            for f in range(1, KT, 2):
                dve.wait_ge(yt.sem, yt.n(layer, f + 1))
                b = 2 * (f % 3)
                nc.vector.tensor_copy(yT[:, f, 0:512], ps[:, b, :])
                nc.vector.tensor_copy(yT[:, f, 512:768], ps[:, b + 1, 0:256]).then_inc(yt_v.sem, 1)
            dve.wait_ge(gbev.sem, gbev.n(layer, 4))
            for u in range(12):
                g, i = divmod(u, 6)
                v = 1 if i < NT_CTX else 0
                dve.wait_ge(wo.sem, wo.n(layer, u + 1))
                if u >= 2:
                    dve.wait_ge(wov.sem, wov.n(layer, u - 1))
                link(nc.vector.tensor_tensor(otmp2[u % 2], ps[:, u % 6, :], gbc[:, v, g * 512:g * 512 + 512], ALU.mult))
                xs = x[:, i, g * 512:g * 512 + 512]
                nc.vector.tensor_tensor(xs, xs, otmp2[u % 2], ALU.add).then_inc(wov.sem, 1)

        def sp_experts(sp, layer):
            wg, wu, wd = t["moe_w_gate"], t["moe_w_up"], t["moe_w_down"]

            def gate_up(e, k):
                if k >= 4 or not isinstance(e, int) or e > 0:
                    sp.wait_ge(gufree.sem, e * 8 + (layer * 128 + k - 3))
                for m, w in enumerate((wg, wu)):
                    src = w[layer, bass.ds(e, 1), k * P:(k + 1) * P, :].rearrange("e p n -> p (e n)")
                    sp.dma_start(gu[k % 4][:, m, :], src).then_inc(guld[k % 4].sem, 16)

            def downs(e, n):
                if not isinstance(e, int) or e > 0:
                    sp.wait_ge(dfree.sem, e * 3 + (layer * 48 + n - 2))
                r0, r1 = 4 * n, min(4 * n + 4, FT)
                src = wd[layer, bass.ds(e, 1), r0 * P:r1 * P, :].rearrange("e (r p) n -> p (e r) n", p=P)
                sp.dma_start(down[:, r0:r1, :], src).then_inc(dld[n].sem, 16)

            sp.wait_ge(wov.sem, wov.n(layer, 12))
            for k in range(8):
                gate_up(0, k)
            sp.wait_ge(logit.sem, logit.n(layer, 1))
            for n in range(3):
                downs(0, n)
            with sp.Fori(1, NE) as e:
                for k in range(8):
                    gate_up(e, k)
                for n in range(3):
                    downs(e, n)

        def pe_experts(pe, layer):
            pe.wait_ge(hT_a.sem, hT_a.n(layer, 8))
            pe.wait_ge(hT_v.sem, hT_v.n(layer, 8))
            for i in range(NT):
                for f in range(KT):
                    ins = nc.tensor.matmul(ps[:, 6, i * NE:(i + 1) * NE], lhsT=hT2[:, f, i * P:(i + 1) * P],
                                           rhs=rw[:, layer, f, :], start=(f == 0), stop=(f == KT - 1))
            ins.then_inc(logit.sem, 1)
            for half in range(2):
                ins = nc.tensor.matmul(ps[0:CAP, half, :], lhsT=selM[:, :], rhs=gates[:, 1, half * 512:half * 512 + 512],
                                       start=True, stop=True)
            ins.then_inc(gm_mm.sem, 1)
            pe.wait_ge(affr.sem, affr.n(layer, 1))
            for i in range(NT):
                bank, c0 = (7, i * P) if i < NT_CTX else (5, (i - NT_CTX) * P)
                ins = nc.tensor.transpose(ps[0:NE, bank, c0:c0 + P], aff[:, i, 0:NE], ident)
            ins.then_inc(affTm.sem, 1)
            pe.wait_ge(gm_v.sem, gm_v.n(layer, 1))

            def spread(e):
                pe.wait_ge(affm_v.sem, e + (affm_v.n(layer, 1)))
                nc.tensor.matmul(ps[:, 6, :], lhsT=ones16[:, :], rhs=affm[0:NE, CTX:TOK], start=True, stop=True)
                nc.tensor.matmul(ps[:, 7, 0:CTX], lhsT=ones16[:, :], rhs=affm[0:NE, 0:CTX], start=True, stop=True) \
                    .then_inc(bc_mm.sem, 1)

            def gather(e):
                pe.wait_ge(picked.sem, e + picked.n(layer, 1))
                for f in range(KT):
                    bank, c0 = 6 + f // 4, (f % 4) * P
                    for (i0, i1), cap, off in (((NT_CTX, NT), CAP_L, 0), ((0, NT_CTX), CAP_C, CAP_L)):
                        for i in range(i0, i1):
                            ins = nc.tensor.matmul(ps[:, bank, c0 + off:c0 + off + cap],
                                                   lhsT=xn2[:, i, f * P:(f + 1) * P], rhs=Gm[:, i, 0:cap],
                                                   start=(i == i0), stop=(i == i1 - 1))
                ins.then_inc(gath.sem, 1)

            def turn_weights(e):
                pe.wait_ge(xe_a.sem, e + xe_a.n(layer, 1))
                pe.wait_ge(xe_v.sem, e + xe_v.n(layer, 1))
                for i in range(NT):
                    ins = nc.tensor.transpose(ps[0:CAP, 6 + i // 4, (i % 4) * P:(i % 4 + 1) * P], Wm[:, i, :], ident)
                ins.then_inc(wtm.sem, 1)

            spread(0)
            gather(0)
            turn_weights(0)
            with pe.Fori(0, NE) as e:
                pe.wait_ge(wta.sem, e + wta.n(layer, 1))
                spread(e + 1)
                for k in range(KT):
                    pe.wait_ge(guld[k % 4].sem, e * 64 + (layer * 1024 + 32 * (k // 4 + 1)))
                    for m in range(2):
                        for b in range(3):
                            n = min(512, FF - 512 * b)
                            ins = nc.tensor.matmul(ps[0:CAP, 3 * m + b, 0:n], lhsT=xeT[:, k, :],
                                                   rhs=gu[k % 4][:, m, 512 * b:512 * b + n], start=(k == 0),
                                                   stop=(k == KT - 1))
                    ins.then_inc(gufree.sem, 1)
                gather(e + 1)
                for b in range(3):
                    pe.wait_ge(h_v.sem, e * 3 + (layer * 48 + b + 1))
                    for ft in range(4 * b, min(4 * b + 4, FT)):
                        ins = nc.tensor.transpose(ps[:, b, (ft % 4) * CAP:(ft % 4 + 1) * CAP],
                                                  hh[0:CAP, ft * P:(ft + 1) * P], ident[0:CAP, 0:CAP])
                    ins.then_inc(htm.sem, 1)
                for n in range(3):
                    pe.wait_ge(hta.sem, e * 3 + (layer * 48 + n + 1))
                    pe.wait_ge(dld[n].sem, e * 16 + (layer * 256 + 16))
                    for ft in range(4 * n, min(4 * n + 4, FT)):
                        for half in range(2):
                            ins = nc.tensor.matmul(ps[0:CAP, 3 + half, :], lhsT=hTm[:, ft, :],
                                                   rhs=down[:, ft, half * 512:half * 512 + 512], start=(ft == 0),
                                                   stop=(ft == FT - 1))
                    ins.then_inc(dfree.sem, 1)
                for u in range(12):
                    half, i = divmod(u, NT)
                    if u % 6 == 0:
                        pe.wait_ge(ye_v.sem, e * 2 + (layer * 32 + half + 1))
                    if u >= 4:
                        pe.wait_ge(scv.sem, e * 12 + (layer * 192 + u - 3))
                    nc.tensor.matmul(ps[:, (0, 1, 2, 5)[u % 4], :], lhsT=WT[0:CAP, i, :],
                                     rhs=ye[0:CAP, half * 512:half * 512 + 512], start=True, stop=True) \
                        .then_inc(scm.sem, 1)
                turn_weights(e + 1)
                pe.wait_ge(scv.sem, e * 12 + (layer * 192 + 12))

        def act_experts(act, layer):
            act.wait_ge(aff_v.sem, aff_v.n(layer, 1))
            nc.scalar.activation(aff[:, :, 0:NE], aff[:, :, 0:NE], ACT.Exp).then_inc(aff_a.sem, 1)

            def gathered(e):
                act.wait_ge(gath.sem, e + gath.n(layer, 1))
                for f in range(4):
                    for v, (c0, n) in enumerate(((0, CAP_L), (CAP_L, CAP_C))):
                        ins = nc.scalar.activation(xeT[:, f, c0:c0 + n], ps[:, 6, f * P + c0:f * P + c0 + n],
                                                   ACT.Identity, scale=modC[:, 3, f, v:v + 1],
                                                   bias=modC[:, 2, f, v:v + 1])
                ins.then_inc(xe_a.sem, 1)

            def turned(e):
                act.wait_ge(wtm.sem, e + wtm.n(layer, 1))
                nc.scalar.activation(WT[0:CAP, 0:4, :].rearrange("p i t -> p (i t)"), ps[0:CAP, 6, :], ACT.Copy)
                nc.scalar.activation(WT[0:CAP, 4:6, :].rearrange("p i t -> p (i t)"), ps[0:CAP, 7, 0:256], ACT.Copy) \
                    .then_inc(wta.sem, 1)

            gathered(0)
            turned(0)
            with act.Fori(0, NE) as e:
                act.wait_ge(gufree.sem, e * 8 + (layer * 128 + 8))
                for b in range(3):
                    n = min(512, FF - 512 * b)
                    nc.scalar.activation(sg[0:CAP, 512 * b:512 * b + n], ps[0:CAP, b, 0:n], ACT.Silu) \
                        .then_inc(h_a.sem, 1)
                gathered(e + 1)
                for b in range(3):
                    act.wait_ge(htm.sem, e * 3 + (layer * 48 + b + 1))
                    nt = min(4, FT - 4 * b)
                    nc.scalar.activation(hTm[:, 4 * b:4 * b + nt, :].rearrange("p f c -> p (f c)"),
                                         ps[:, b, 0:nt * CAP], ACT.Copy).then_inc(hta.sem, 1)
                turned(e + 1)

        def dve_experts(dve, layer):
            nc.vector.memset(aff[:, :, NE:NE + 1], 0.0)
            nc.vector.memset(rk[:, :, :], 0.0)
            link(nc.vector.memset(Wm, 0.0))
            dve.wait_ge(logit.sem, logit.n(layer, 1))
            lg = ps[:, 6, 0:NT * NE].rearrange("p (i e) -> p i e", e=NE)
            link(nc.vector.tensor_reduce(lmax[:, :], lg, AX, ALU.max))
            nc.vector.tensor_tensor(aff[:, :, 0:NE], lg, lmax[:, :].unsqueeze(2).broadcast_to([P, NT, NE]),
                                    ALU.subtract).then_inc(aff_v.sem, 1)
            dve.wait_ge(gm_mm.sem, gm_mm.n(layer, 1))
            nc.vector.tensor_copy(gateM[0:CAP, 0:512], ps[0:CAP, 0, :])
            nc.vector.tensor_copy(gateM[0:CAP, 512:1024], ps[0:CAP, 1, :])
            dve.wait_ge(aff_a.sem, aff_a.n(layer, 1))
            link(nc.vector.tensor_reduce(lmax[:, :], aff[:, :, 0:NE], AX, ALU.add))
            link(nc.vector.reciprocal(lmax[:, :], lmax[:, :]))
            nc.vector.tensor_tensor(aff[:, :, 0:NE], aff[:, :, 0:NE], lmax[:, :].unsqueeze(2).broadcast_to([P, NT, NE]),
                                    ALU.mult).then_inc(affr.sem, 1)
            dve.wait_ge(affTm.sem, affTm.n(layer, 1))
            nc.vector.tensor_copy(affT[0:NE, 0:CTX], ps[0:NE, 7, 0:CTX])
            link(nc.vector.tensor_copy(affT[0:NE, CTX:TOK], ps[0:NE, 5, :]))
            nc.vector.memset(ss[:, 61:62], 0.0).then_inc(gm_v.sem, 1)

            def choose(e):
                if not isinstance(e, int):
                    dve.wait_ge(bc_mm.sem, e + (bc_mm.n(layer, 0)))
                nc.vector.tensor_scalar(affm[0:NE, :], affT[0:NE, :], ident[0:NE, bass.ds(e, 1)], None, ALU.mult) \
                    .then_inc(affm_v.sem, 1)
                link2(nc.vector.tensor_copy(affe[:, :], aff[:, :, bass.ds(e, 1)].rearrange("p i e -> p (i e)")))
                dve.wait_ge(bc_mm.sem, e + bc_mm.n(layer, 1))
                for i in range(NT):
                    bank, lo, hi, me = (7, 0, NT_CTX, i) if i < NT_CTX else (6, 0, NT_LAT, i - NT_CTX)
                    own = affe[:, i:i + 1]
                    if me > lo:
                        link2(nc.vector.tensor_scalar(rjunk[:, 0:me * P], ps[:, bank, 0:me * P], own, None, ALU.is_ge,
                                                      ALU.add, accum_out=rk[:, i, 0:1]))
                    if me < hi - 1:
                        link2(nc.vector.tensor_scalar(rjunk[:, 0:(hi - 1 - me) * P], ps[:, bank, (me + 1) * P:hi * P],
                                                      own, None, ALU.is_gt, ALU.add, accum_out=rk[:, i, 1:2]))
                    for n, (op, m) in enumerate(((ALU.is_ge, "before"), (ALU.is_gt, "after"))):
                        link2(nc.vector.scalar_tensor_tensor(rjunk[:, 0:P], ps[:, bank, me * P:(me + 1) * P], own,
                                                             cst(m), op, ALU.mult, accum_out=rk[:, i, 2 + n:3 + n]))
                link2(nc.vector.tensor_reduce(rank[:, :], rk[:, :, :], AX, ALU.add))
                if not isinstance(e, int):
                    dve.wait_ge(wtm.sem, e + wtm.n(layer, 0))
                for i in range(NT):
                    cap, off = (CAP_C, CAP_L) if i < NT_CTX else (CAP_L, 0)
                    nc.vector.tensor_scalar(Gm[:, i, 0:cap], cst("iota")[:, 0:cap], rank[:, i:i + 1], None, ALU.is_equal)
                    ins = nc.vector.tensor_scalar(Wm[:, i, off:off + cap], cst("iota")[:, 0:cap], rank[:, i:i + 1],
                                                  affe[:, i:i + 1], ALU.is_equal, ALU.mult)
                ins.then_inc(picked.sem, 1)

            def gathered(e):
                dve.wait_ge(gath.sem, e + gath.n(layer, 1))
                for f in range(4, 8):
                    for v, (c0, n) in enumerate(((0, CAP_L), (CAP_L, CAP_C))):
                        ins = nc.vector.tensor_scalar(xeT[:, f, c0:c0 + n], ps[:, 7, (f - 4) * P + c0:(f - 4) * P + c0 + n],
                                                      modC[:, 3, f, v:v + 1], modC[:, 2, f, v:v + 1], ALU.mult, ALU.add)
                ins.then_inc(xe_v.sem, 1)

            per = CHOOSE_STEPS
            state = {}

            def link2(ins):
                state["n"] += 1
                ins.then_inc(cstep.sem, 1)
                dve.wait_ge(cstep.sem, state["e"] * per + (layer * per * (NE + 1) + state["n"]))

            def run_choose(e):
                state["n"], state["e"] = 0, e
                choose(e)
                assert state["n"] == per, state["n"]

            run_choose(0)
            gathered(0)
            with dve.Fori(0, NE) as e:
                run_choose(e + 1)
                for b in range(3):
                    n = min(512, FF - 512 * b)
                    dve.wait_ge(h_a.sem, e * 3 + (layer * 48 + b + 1))
                    nc.vector.tensor_tensor(hh[0:CAP, 512 * b:512 * b + n], sg[0:CAP, 512 * b:512 * b + n],
                                            ps[0:CAP, 3 + b, 0:n], ALU.mult).then_inc(h_v.sem, 1)
                gathered(e + 1)
                dve.wait_ge(dfree.sem, e * 3 + (layer * 48 + 3))
                for half in range(2):
                    nc.vector.tensor_tensor(ye[0:CAP, half * 512:half * 512 + 512], ps[0:CAP, 3 + half, :],
                                            gateM[0:CAP, half * 512:half * 512 + 512], ALU.mult).then_inc(ye_v.sem, 1)
                for u in range(12):
                    half, i = divmod(u, NT)
                    dve.wait_ge(scm.sem, e * 12 + (layer * 192 + u + 1))
                    xs = x[:, i, half * 512:half * 512 + 512]
                    nc.vector.tensor_tensor(xs, xs, ps[:, (0, 1, 2, 5)[u % 4], :], ALU.add).then_inc(scv.sem, 1)

        block = ctx.enter_context(nc.Block())
        block.sync(sync_program)
        block.scalar(scalar_program)
        block.tensor(tensor_program)
        block.vector(vector_program)


INPUTS = ["x", "c", "ctx", "c_ctx", "w_mod", "b_mod", "w_in", "w_out", "attn_q_norm", "attn_k_norm", "dn_conv",
          "dn_a_log", "dn_dt_bias", "dn_norm", "hg_lower_bounds", "hg_norm", "moe_router", "moe_w_gate", "moe_w_up",
          "moe_w_down"]


def kernel(**inputs):
    import concourse.bacc as bacc
    from concourse.bass_utils import run_bass_kernel_spmd

    nc = bacc.Bacc("TRN2", target_bir_lowering=False, num_devices=1, dynamic_dma_scratch_size=1024)
    arrays, t = {}, {}
    for name in INPUTS + ["consts"]:
        a = constants() if name == "consts" else np.ascontiguousarray(inputs[name])
        arrays[f"in_{name}"] = a
        t[name] = nc.dram_tensor(f"in_{name}", a.shape, mybir.dt.from_np(a.dtype), kind="ExternalInput").ap()
    t["out"] = nc.dram_tensor("out_0", (1, LAT, D), F32, kind="ExternalOutput").ap()
    trunk_program(nc, t)
    r = run_bass_kernel_spmd(nc, [arrays], core_ids=[0])
    return r.results[0]["out_0"]
```

```python
from contextlib import ExitStack

import concourse.bass as bass
from concourse import mybir
import numpy as np

F32 = mybir.dt.float32
F32R = mybir.dt.float32r
I32 = mybir.dt.int32
ACT = mybir.ActivationFunctionType
ALU = mybir.AluOpType
AX = mybir.AxisListType.X

P = 128
DEPTH, D = 2, 1024
CTX, LAT = 256, 512
TOK = CTX + LAT
NT, NT_CTX, NT_LAT = TOK // P, CTX // P, LAT // P
KT = D // P
HD = 64
NQ, NKV = 8, 2
DNH = 4
CHUNK = 64
NCH = TOK // CHUNK
NCH_CTX = CTX // CHUNK
LEVELS = 6
CONV_K = 5
IN_COLS = 3088
NE, FF = 16, 1408
FT = FF // P
CAP_L, CAP_C = 2 * LAT // NE, 2 * CTX // NE
CAP = CAP_L + CAP_C
EPS = 1e-6
GRID_W = 64
ROPE_THETA = 10000.0

GROUPS = [(0, 512, "T"), (512, 256, "T"), (768, 384, "C"), (1152, 384, "C"),
          (1536, 272, "T"), (1808, 512, "C"), (2320, 256, "C"), (2576, 512, "T")]
N_MOD = 6 * D // 512
N_IN = 7 + 7 * DEPTH
N_FIRST = 5
LOADS = N_MOD + len(GROUPS) + 2
WRING = 2
POOL_ITEMS = (0, 1, 4, 7, 10, 13)
POOL_DOWN = (1, 4, 7, 10)
SCATTER_BANKS = {12: (0, 1, 2, 0, 1, 2, 5, 6, 7, 5, 6, 7), 8: (0, 1, 2, 0, 5, 6, 7, 5)}
ARENA = 43616


def out_tiles(layer):
    return range(NT_CTX if layer == DEPTH - 1 else 0, NT)


def choose_steps(layer):
    return 1 + sum(2 * n + 2 * (n - 1) for n in ((NT_LAT,) if layer == DEPTH - 1 else (NT_LAT, NT_CTX))) + 1


CONST = {}


def _layout():
    at = 0
    for name, n in (("ident", 128), ("lvl0", 7 * 64), ("lvl1", 7 * 64), ("strict0", 128), ("strict1", 128),
                    ("incl0", 128), ("incl1", 128), ("chunkind", 256), ("causal0", 64), ("causal1", 64),
                    ("iota", 64), ("before", 128), ("after", 128), ("ident64", 64), ("cc", 256), ("ss", 256)):
        CONST[name] = (at, n)
        at += n
    return at


N_CONST = _layout()


def constants():
    p = np.arange(P)[:, None]
    c = np.arange(P)[None, :]
    t64 = np.arange(64)[None, :]
    s64 = p % 64
    same = (p // 64) == (c // 64)
    out = np.zeros((P, N_CONST), np.float32)

    def put(name, a):
        at, n = CONST[name]
        out[:, at:at + n] = np.broadcast_to(a, (P, n))

    put("ident", p == c)
    lv = []
    for level in range(LEVELS):
        h = 1 << level
        lv.append((s64 // (2 * h) == t64 // (2 * h)) & (s64 % (2 * h) < h) & (t64 % (2 * h) >= h))
    lv.append(s64 == t64)
    put("lvl0", np.concatenate(lv, 1))
    lv = []
    for level in range(LEVELS):
        h = 1 << level
        lv.append((s64 // (2 * h) == t64 // (2 * h)) & (s64 % (2 * h) >= h) & (t64 % (2 * h) < h))
    lv.append(s64 == t64)
    put("lvl1", np.concatenate(lv, 1))
    put("strict0", same & (p > c))
    put("strict1", same & (p < c))
    put("incl0", same & (p <= c))
    put("incl1", same & (p >= c))
    put("chunkind", np.concatenate([np.broadcast_to(p // 64 == h, (P, P)) for h in range(2)], 1))
    put("causal0", s64 <= t64)
    put("causal1", s64 >= t64)
    put("iota", t64)
    put("before", c < p)
    put("after", c > p)
    put("ident64", s64 == t64)
    n_freq = HD // 4
    inv = (np.float32(ROPE_THETA) ** (-np.arange(n_freq, dtype=np.float32) / np.float32(n_freq))).astype(np.float32)
    t = np.arange(LAT)
    row, col = (t // GRID_W).astype(np.float32), (t % GRID_W).astype(np.float32)
    ar, ac = row[:, None] * inv, col[:, None] * inv
    cc = np.concatenate([np.cos(ar), np.cos(ar), np.cos(ac), np.cos(ac)], 1)
    ss = np.concatenate([-np.sin(ar), np.sin(ar), -np.sin(ac), np.sin(ac)], 1)
    put("cc", cc.reshape(NT_LAT, P, HD).transpose(1, 0, 2).reshape(P, -1))
    put("ss", ss.reshape(NT_LAT, P, HD).transpose(1, 0, 2).reshape(P, -1))
    return out


class Signal:

    def __init__(self, sem, per_layer):
        self.sem, self.per_layer = sem, per_layer

    def n(self, layer, count):
        return layer * self.per_layer + count


def trunk_program(nc, t):
    ctx = ExitStack()
    with ctx:
        def sb(name, shape, dt=F32):
            return ctx.enter_context(nc.sbuf_tensor(name, shape, dt))

        def sem(name, per_layer=0):
            return Signal(ctx.enter_context(nc.semaphore(name)), per_layer)

        x = sb("x", [P, NT, D])
        const = sb("const", [P, N_CONST])
        rowsT = sb("rowsT", [P, 84])
        condT = sb("condT", [P, 2 * KT])
        small = sb("small", [P, DEPTH, 4 * HD + 16])
        modC = sb("modC", [P, 4, KT, 2])
        gates = sb("gates", [2, 2, D])
        lbT = sb("lbT", [P, DEPTH, 4])
        omlT = sb("omlT", [P, DEPTH, 4])
        lbw = sb("lbw", [P, 6, 4])
        sel2 = sb("sel2", [2, 2, P])
        ones16 = sb("ones16", [16, P])
        ss = sb("ss", [P, 64])
        ss2 = sb("ss2", [P, 64])
        rs = sb("rs", [P, 64])
        nmax = sb("nmax", [P, 48])
        rsum = sb("rsum", [P, 48])
        rinv = sb("rinv", [P, 48])
        bt = sb("bt", [P, NT, 8])
        gg = sb("gg", [P, NT, 8])
        ga = sb("ga", [P, NT, 8])
        gb = sb("gb", [P, NT, 8])
        ealog = sb("ealog", [P, 8])
        sc = sb("sc", [P, 96])
        eb = sb("eb", [P, NT, DNH])
        ec = sb("ec", [P, 2, NCH])
        rw = sb("rw", [P, DEPTH, KT, NE])
        aff = sb("aff", [P, NT, NE + 1])
        affe = sb("affe", [P, NT])
        rk = sb("rk", [P, NT, 4])
        rank = sb("rank", [P, NT])
        lmax = sb("lmax", [P, NT])
        selM = sb("selM", [2, CAP])
        arena_at = -(-nc.sbuf_base // 64) * 64
        arena = nc.alloc_sbuf_tensor_at("arena", [P, ARENA], F32, offset=arena_at)

        def share(name, at, *dims, dt=F32R):
            n = int(np.prod(dims))
            assert at + n <= ARENA
            v = nc.alloc_sbuf_tensor_at(name, [P, n], dt, offset=arena_at + 4 * at)[:, :]
            if len(dims) == 1:
                return v
            names = "abcde"[:len(dims)]
            return v.rearrange(f"p ({' '.join(names)}) -> p {' '.join(names)}", **dict(zip(names, dims)))

        ps = ctx.enter_context(nc.psum_tensor("ps", [P, 8, 512], F32))

        def view(at, *dims):
            n = int(np.prod(dims))
            assert at + n <= ARENA
            v = arena[:, at:at + n]
            if len(dims) == 1:
                return v
            names = "abcde"[:len(dims)]
            return v.rearrange(f"p ({' '.join(names)}) -> p {' '.join(names)}", **dict(zip(names, dims)))

        def cst(name):
            at, n = CONST[name]
            return const[:, at:at + n]

        rows = view(42000, P)[0:84, :]
        ident = cst("ident")
        lvl = [cst(f"lvl{d}").rearrange("p (l t) -> p l t", l=7) for d in range(2)]
        lvl_i = [cst(f"lvl{d}").bitcast(I32).rearrange("p (l t) -> p l t", l=7) for d in range(2)]
        hT = view(0, KT, TOK)
        wst = [view(6144 + 4096 * i, KT, 512) for i in range(WRING)]
        qk = view(14336, NT, 640)
        vtok = view(18176, NT, 128)
        convin = view(18944, 6, 776)
        dz = view(23600, NT, 272)
        hgc = view(25232, 6, TOK)
        hgt = view(29840, NT, 512)
        ycat = view(32912, NT, D)
        modrow = view(18944, 6144)
        xn = ycat
        extra = 39056
        sq = view(32912, 3840)
        qn = view(32912, NT, 640)
        rope2 = view(extra, 640)
        qkT = view(0, 5, TOK)
        prob = [view(3840 + TOK * i, TOK) for i in range(2)]
        probT = [view(5376 + TOK * i, TOK) for i in range(2)]
        convout = view(10752, 6, 772)
        dt = view(0, NT, 768)
        sq_dn = view(extra, NT, 512)
        kqT = view(4608, 2, NCH, 2, HD)
        Uc = view(7680, NCH, 2, HD)
        vnew = view(7680, NT, DNH, HD)
        S = view(9216, NCH, 2, HD)
        AT = view(10752, NT, DNH, HD)
        TR = view(12288, NT, 2, DNH, HD)
        vke = view(15360, NT, DNH, 2 * HD)
        NTm = view(18944, NT, DNH, HD)
        NL = view(20480, NT, DNH, HD)
        ysol = view(18944, NT, DNH, 2 * HD)
        kbe = view(22016, NT, DNH, HD)
        Dm = view(extra, NT, DNH, HD)
        Um = view(extra, NT, DNH, HD)
        G = view(extra, NCH, 2, HD)
        otmp = view(extra, NT, DNH, HD)
        sqg = view(extra, NT, 256)
        ykT = dt[:, :, 0:256].rearrange("p i (b c t) -> p i b c t", b=2, c=2)

        gpad = view(0, 2, NCH, CHUNK + 1)
        Cc = view(1560, 2, NCH, CHUNK + 1)
        kk = view(3120, 2, TOK)
        Z = [view(4656 + TOK * i, TOK) for i in range(4)]
        Ah = view(7728, DNH, NT, HD)
        ED = view(9264, 2, TOK)
        ER = view(10800, 2, TOK)
        ket = view(12336, NT, 256)
        Uh = view(13872, NCH, 2, HD)
        Sh = view(15408, NCH, 2, HD)
        reset = view(16944, NCH, CHUNK + 1)
        yT = view(0, KT, TOK)
        gbc = view(14336, 2, D)
        otmp2 = [view(extra + 512 * i, 512) for i in range(2)]
        gu = [share(f"gu{i}", 2 * FF * i, 2, FF, dt=F32) for i in range(4)]
        down = share("down", 11264, FT, D, dt=F32)
        down_lo = share("down_lo", 11264, FT, D)
        hT2 = view(11264, KT, TOK)
        xn2 = view(22528, NT, D)
        gu_lo = [share(f"gu_lo{i}", 2 * FF * i, 2, FF) for i in range(4)]
        gu_hi = [share(f"gu_hi{i}", 31616 + FF * i, FF) for i in range(4)]
        xsplit = share("xsplit", 28672, KT, 2, CAP)
        sg = view(30208, FF)
        xe = view(30208, KT, CAP)
        hTm = share("hTm", 37248, FT, CAP)
        hTm_lo = share("hTm_lo", 38304, FT, CAP)
        ye = view(38304, D)
        rjunk = view(38816, 512)
        ye_lo = share("ye_lo", 38304, D)
        ye_hi = share("ye_hi", 37248, D)
        WT = share("WT", 39360, NT, P)
        Gm = view(40128, NT, CAP)
        w_slot = view(40704, 1)
        affm = view(41056, TOK)
        affT = view(41824, TOK)
        gateM = view(42592, D)

        s_first = sem("s_first")
        s_in = sem("s_in")
        s_rowsT = sem("s_rowsT")
        s_cond = sem("s_cond")
        s_setup = sem("s_setup")
        wload = [sem(f"wload{i}") for i in range(WRING)]
        wfree = sem("wfree", LOADS)
        bmod = sem("bmod", 32)
        modmm = sem("modmm", N_MOD)
        modadd = sem("modadd", N_MOD)
        modT = sem("modT", 1)
        modcol = sem("modcol", 1)
        sumsq = sem("sumsq", 12)
        rstd = sem("rstd", 2)
        act_rs = sem("act_rs", 2)
        normed = sem("normed", 12)
        normT = sem("normT", 16)
        hT_a = sem("hT_a", 8)
        hT_v = sem("hT_v", 8)
        proj = sem("proj", 48)
        projev = sem("projev", 48)
        qk_ss = sem("qk_ss", 1)
        qk_rs = sem("qk_rs", 1)
        qk_ready = sem("qk_ready", 1)
        qkt = sem("qkt", 5)
        qktev = sem("qktev", 5)
        score = sem("score", 48)
        smax = sem("smax", 48)
        expd = sem("expd", 48)
        ptt = sem("ptt", 48)
        pt_a = sem("pt_a", 48)
        pt_v = sem("pt_v", 48)
        pv = sem("pv", 48)
        attn_y = sem("attn_y", 48)
        conv = sem("conv", 30)
        convact = sem("convact", 6)
        dtt = sem("dtt", 6)
        dtev = sem("dtev", 6)
        dn_ss = sem("dn_ss", 1)
        dn_rs = sem("dn_rs", 1)
        dn_norm = sem("dn_norm", 6)
        kqt = sem("kqt", 6)
        kqtev = sem("kqtev", 6)
        gate_v = sem("gate_v", 1)
        gate_a = sem("gate_a", 4)
        gbr = sem("gbr", 12)
        decay = sem("decay", 12)
        dexp = sem("dexp", 14)
        gram = sem("gram", 12)
        pairs = sem("pairs", 12)
        vke_v = sem("vke_v", 2)
        kev = sem("kev", 2)
        nl = sem("nl", 72)
        umm = sem("umm", 72)
        uev = sem("uev", 60)
        trm = sem("trm", 60)
        tru = sem("tru", 72)
        ymm = sem("ymm", 12)
        yev = sem("yev", 12)
        gmm = sem("gmm", 12)
        gev_a = sem("gev_a", 12)
        gev_v = sem("gev_v", 12)
        step = sem("step", 22)
        stepv = sem("stepv", 24)
        zmm = sem("zmm", 12)
        vnw = sem("vnw", 12)
        avm = sem("avm", 12)
        outv = sem("outv", 12)
        go_ss = sem("go_ss", 2)
        go_rs = sem("go_rs", 2)
        f_v = sem("f_v", 4)
        g_a = sem("g_a", 2)
        zsub = sem("zsub", 24)
        zexp = sem("zexp", 24)
        zmul = sem("zmul", 24)
        hgram = sem("hgram", 28)
        hpred = sem("hpred", 28)
        er_v = sem("er_v", 2)
        er_a = sem("er_a", 2)
        qe_v = sem("qe_v", 2)
        kett = sem("kett", 12)
        ketev = sem("ketev", 12)
        umh = sem("umh", 12)
        uhev = sem("uhev", 12)
        hstate = sem("hstate", 2)
        hout = sem("hout", 12)
        houtv = sem("houtv", 12)
        mixed = sem("mixed", 1)
        yt = sem("yt", 8)
        yt_a = sem("yt_a", 6)
        yt_v = sem("yt_v", 2)
        gbmm = sem("gbmm", 4)
        gbev = sem("gbev", 4)
        wo = sem("wo", 12)
        wov = sem("wov", 12)
        logitT = sem("logitT", 1)
        logitT_v = sem("logitT_v", 1)
        logit = sem("logit", 1)
        aff_v = sem("aff_v", 1)
        aff_a = sem("aff_a", 1)
        affr = sem("affr", 1)
        affTm = sem("affTm", 1)
        gm_mm = sem("gm_mm", 1)
        gm_v = sem("gm_v", 1)
        affm_v = sem("affm_v", 17)
        bc_mm = sem("bc_mm", 17)
        picked = sem("picked", 17)
        gath = sem("gath", 34)
        xe_a = sem("xe_a", 34)
        xe_v = sem("xe_v", 16)
        wtm = sem("wtm", 17)
        wta = sem("wta", 16)
        guld = [sem(f"guld{i}", 64 * 16) for i in range(4)]
        dld = [sem(f"dld{i}", 16 * 16) for i in range(3)]
        gufree = sem("gufree", 256)
        hi_a = sem("hi_a", 256)
        lo_v = sem("lo_v", 16 * (2 * KT - len(POOL_ITEMS)))
        lo_p = sem("lo_p", 16 * len(POOL_ITEMS))
        xe_w = sem("xe_w", 34)
        dmm = sem("dmm", NE * FT)
        dhi_a = sem("dhi_a", NE * FT)
        dlo_v = sem("dlo_v", NE * (FT - len(POOL_DOWN)))
        dlo_p = sem("dlo_p", NE * len(POOL_DOWN))
        hTl = sem("hTl", 48)
        h_a = sem("h_a", 48)
        h_v = sem("h_v", 48)
        htm = sem("htm", 48)
        hta = sem("hta", 48)
        ye_v = sem("ye_v", 96)
        scm = sem("scm", 193)
        scv = sem("scv", 193)
        cstep = sem("cstep")
        act_step = sem("act_step")
        dve_step = sem("dve_step")
        s_out = sem("s_out")
        counts = {"act": 0, "dve": 0}

        def link_act(ins):
            counts["act"] += 1
            ins.then_inc(act_step.sem, 1)
            nc.scalar.wait_ge(act_step.sem, counts["act"])

        def link(ins):
            counts["dve"] += 1
            ins.then_inc(dve_step.sem, 1)
            nc.vector.wait_ge(dve_step.sem, counts["dve"])

        def loads(layer):
            w_mod, w_in, w_out = t["w_mod"], t["w_in"], t["w_out"]
            for g in range(N_MOD):
                yield w_mod[layer][:, g * 512:(g + 1) * 512], 512
            for c0, n, _ in GROUPS:
                yield w_in[layer][:, c0:c0 + n], n
            for g in range(2):
                yield w_out[layer][:, g * 512:(g + 1) * 512], 512

        def staged(eng, layer, g):
            n = layer * LOADS + g
            eng.wait_ge(wload[n % WRING].sem, 16 * (n // WRING + 1))
            return wst[n % WRING]

        def proj_units():
            for g, (c0, n, kind) in enumerate(GROUPS):
                if kind == "T":
                    for i in range(NT):
                        yield g, kind, i, 0, n
                else:
                    for c in range(n // P):
                        for seg in range(2):
                            yield g, kind, c, seg, (CTX, LAT)[seg]

        def sync_program(sp):
            for layer in range(DEPTH):
                for g, (src, n) in enumerate(loads(layer)):
                    k = layer * LOADS + g
                    if k >= WRING:
                        sp.wait_ge(wfree.sem, k - WRING + 1)
                    if g == N_MOD + len(GROUPS):
                        sp.wait_ge(houtv.sem, houtv.n(layer, 2 * len(out_tiles(layer))))
                    if layer and g < 2:
                        sp.wait_ge(gufree.sem, gufree.n(layer - 1, 256))
                        if g == 1:
                            sp.wait_ge(dmm.sem, dmm.n(layer - 1, NE * FT))
                    if g == 2:
                        if layer:
                            sp.wait_ge(scv.sem, scv.n(layer - 1, 193))
                        for r in range(2):
                            sp.dma_start(modrow[r:r + 1, :], t["b_mod"][layer:layer + 1, :]).then_inc(bmod.sem, 16)
                    sp.dma_start(wst[k % WRING][:, :, 0:n], src.rearrange("(f p) n -> p f n", p=P)) \
                        .then_inc(wload[k % WRING].sem, 16)
                sp_experts(sp, layer)
            sp.wait_ge(scv.sem, scv.n(DEPTH - 1, 1 + NE * 2 * len(out_tiles(DEPTH - 1))))
            sp.dma_start(t["out"][0].rearrange("(i p) d -> p i d", p=P), x[:, NT_CTX:NT, :]).then_inc(s_out.sem, 16)
            sp.wait_ge(s_out.sem, 16)

        def scalar_program(act):
            lat = t["x"][0].rearrange("(i p) d -> p i d", p=P)
            cx = t["ctx"][0].rearrange("(i p) d -> p i d", p=P)
            ins = [(const[:, :], t["consts"]),
                   (rows[0:60, :], t["dn_conv"].rearrange("l k (j p) -> (l k j) p", p=P)),
                   (rows[60:68, :], t["hg_lower_bounds"].rearrange("l r (j p) -> (l r j) p", p=P)),
                   (rows[68:76, :], t["c"].rearrange("b (f p) -> (b f) p", p=P)),
                   (rows[76:84, :], t["c_ctx"].rearrange("(f p) -> f p", p=P)),
                   (x[:, 0:NT_CTX, :], cx), (x[:, NT_CTX:NT, :], lat)]
            for layer in range(DEPTH):
                for j, name in enumerate(("attn_q_norm", "attn_k_norm", "dn_norm", "hg_norm")):
                    ins.append((small[:, layer, j * HD:(j + 1) * HD], t[name][layer].partition_broadcast(P)))
                for j, name in enumerate(("dn_a_log", "dn_dt_bias")):
                    ins.append((small[:, layer, 4 * HD + 8 * j:4 * HD + 8 * j + 8],
                                t[name][layer].rearrange("r h -> (r h)").partition_broadcast(P)))
                ins.append((rw[:, layer], t["moe_router"][layer].rearrange("(f p) e -> p f e", p=P)))
            assert len(ins) == N_IN
            for n, (dst, src) in enumerate(ins):
                act.dma_start(dst, src).then_inc((s_first if n < N_FIRST else s_in).sem, 16)
            act.wait_ge(s_rowsT.sem, 1)
            nc.scalar.activation(rowsT[:, :], ps[:, 7, 0:84], ACT.Copy).then_inc(s_cond.sem, 1)
            nc.scalar.activation(condT[:, :], ps[:, 7, 68:84], ACT.Silu).then_inc(s_cond.sem, 1)
            act.wait_ge(s_setup.sem, 1)
            nc.scalar.activation(lbw[:, 1:3, :], lbw[:, 1:3, :], ACT.Exp).then_inc(s_setup.sem, 1)
            for layer in range(DEPTH):
                act_norm(act, layer, 0)
                act_proj(act, layer)
                act_attention(act, layer)
                act_deltanet(act, layer)
                act_hgrn(act, layer)
                act_out(act, layer)
                act_norm(act, layer, 1)
                act_experts(act, layer)

        def act_norm(act, layer, which):
            act.wait_ge(s_in.sem, 16 * (N_IN - N_FIRST))
            if which == 0 and layer:
                act.wait_ge(scv.sem, scv.n(layer - 1, 193))
                act.wait_ge(wta.sem, wta.n(layer - 1, NE))
            outs = list(out_tiles(layer))
            for i in range(NT):
                if which == 1 and i in outs:
                    act.wait_ge(wov.sem, wov.n(layer, len(outs) + outs.index(i) + 1))
                nc.scalar.activation((xn if which == 0 else xn2)[:, i, :], x[:, i, :], ACT.Square, accum_out=ss[:, i:i + 1]) \
                    .then_inc(sumsq.sem, 1)
            act.wait_ge(rstd.sem, rstd.n(layer, which + 1))
            link_act(nc.scalar.activation(rs[:, 0:NT], ss2[:, 0:NT], ACT.Ln))
            nc.scalar.activation(rs[:, 0:NT], rs[:, 0:NT], ACT.Exp, scale=-0.5).then_inc(act_rs.sem, 1)
            for f in range(0, KT, 2):
                act.wait_ge(normT.sem, normT.n(layer, 8 * which + f + 1))
                if f == 0:
                    act.wait_ge(modcol.sem, modcol.n(layer, 1))
                b = 2 * (f % 3)
                for v, (bank, c0, n) in enumerate(((b + 1, CTX, LAT), (b, 0, CTX))):
                    ins = nc.scalar.activation((hT if which == 0 else hT2)[:, f, c0:c0 + n], ps[:, bank, 0:n], ACT.Identity,
                                               scale=modC[:, 2 * which + 1, f, v:v + 1],
                                               bias=modC[:, 2 * which, f, v:v + 1])
                ins.then_inc(hT_a.sem, 1)

        def act_proj(act, layer):
            for u, (g, kind, a, seg, n) in enumerate(proj_units()):
                if u == 20:
                    act.wait_ge(qk_ss.sem, qk_ss.n(layer, 1))
                    link_act(nc.scalar.activation(rs[:, 0:60], ss2[:, 0:60], ACT.Ln))
                    nc.scalar.activation(rs[:, 0:60], rs[:, 0:60], ACT.Exp, scale=-0.5).then_inc(qk_rs.sem, 1)
                act.wait_ge(proj.sem, proj.n(layer, u + 1))
                src = ps[:, u % 6, 0:n]
                c0 = GROUPS[g][0]
                if g == 0:
                    todo = [(qk[:, a, 0:512], src, ACT.Copy)]
                elif g == 1:
                    todo = [(qk[:, a, 512:640], src[:, 0:128], ACT.Copy), (vtok[:, a, :], src[:, 128:256], ACT.Copy)]
                elif g in (2, 3):
                    j = (c0 - 768) // P + a
                    todo = [(convin[:, j, (2, 262)[seg]:(2, 262)[seg] + n], src, ACT.Copy)]
                elif g == 4:
                    todo = [(dz[:, a, 0:256], src[:, 0:256], ACT.Silu), (dz[:, a, 256:272], src[:, 256:272], ACT.Copy)]
                elif g in (5, 6):
                    j = (c0 - 1808) // P + a
                    todo = [(hgc[:, j, (0, CTX)[seg]:(0, CTX)[seg] + n], src, ACT.Silu if j < 2 else ACT.Sigmoid)]
                else:
                    todo = [(hgt[:, a, 0:256], src[:, 0:256], ACT.Copy), (hgt[:, a, 256:512], src[:, 256:512], ACT.Silu)]
                for dst, s, fn in todo:
                    ins = nc.scalar.activation(dst, s, fn)
                ins.then_inc(projev.sem, 1)

        def tensor_program(pe):
            pe.wait_ge(s_first.sem, 16 * N_FIRST)
            nc.tensor.transpose(ps[:, 7, 0:84], rows[:, :], ident[0:84, 0:84]).then_inc(s_rowsT.sem, 1)
            pe.wait_ge(s_cond.sem, 2)
            for layer in range(DEPTH):
                pe_mod(pe, layer)
                pe_norm(pe, layer, 0)
                pe_proj(pe, layer)
                pe_attention(pe, layer)
                pe_deltanet(pe, layer)
                pe_hgrn(pe, layer)
                pe_out(pe, layer)
                pe_norm(pe, layer, 1)
                pe_experts(pe, layer)

        def pe_mod(pe, layer):
            cT = condT[:, :].rearrange("p (v f) -> p f v", v=2)
            if layer:
                pe.wait_ge(wta.sem, wta.n(layer - 1, NE))
                pe.wait_ge(scv.sem, scv.n(layer - 1, 193))
            for g in range(N_MOD):
                w = staged(pe, layer, g)
                if g >= 2:
                    pe.wait_ge(modadd.sem, modadd.n(layer, g - 1))
                for f in range(KT):
                    ins = nc.tensor.matmul(ps[0:2, g % 2, :], lhsT=cT[:, f, :], rhs=w[:, f, :],
                                           start=(f == 0), stop=(f == KT - 1))
                ins.then_inc(modmm.sem, 1)
                pe.wait_ge(modmm.sem, modmm.n(layer, g + 1))
                pe.sem_inc(wfree.sem, 1)
            pe.wait_ge(modadd.sem, modadd.n(layer, N_MOD))
            for m, part in enumerate((0, 1, 3, 4)):
                for f in range(KT):
                    c0 = part * D + f * P
                    at = 2 * (m * KT + f)
                    ins = nc.tensor.transpose(ps[:, 6, at:at + 2], modrow[0:2, c0:c0 + P], ident[0:2, 0:2])
            ins.then_inc(modT.sem, 1)

        def pe_norm(pe, layer, which):
            for f in range(KT):
                if f == 0:
                    pe.wait_ge(normed.sem, normed.n(layer, 6 * which + 6))
                if f >= 3:
                    evacuated = (hT_a, hT_v)[(f - 3) % 2]
                    pe.wait_ge(evacuated.sem, evacuated.n(layer, 4 * which + (f - 3) // 2 + 1))
                b = 2 * (f % 3)
                for i in range(NT):
                    bank, c0 = (b, i * P) if i < NT_CTX else (b + 1, (i - NT_CTX) * P)
                    src = (xn if which == 0 else xn2)[:, i, f * P:(f + 1) * P]
                    ins = nc.tensor.transpose(ps[:, bank, c0:c0 + P], src, ident)
                ins.then_inc(normT.sem, 1)

        def pe_proj(pe, layer):
            pe.wait_ge(hT_a.sem, hT_a.n(layer, 4))
            pe.wait_ge(hT_v.sem, hT_v.n(layer, 4))
            last_g, w = -1, None
            units = list(proj_units())
            for u, (g, kind, a, seg, n) in enumerate(units):
                if g != last_g:
                    w, last_g = staged(pe, layer, N_MOD + g), g
                if u >= 6:
                    pe.wait_ge(projev.sem, projev.n(layer, u - 5))
                for f in range(KT):
                    out = ps[:, u % 6, 0:n]
                    if kind == "T":
                        lhs, rhs = hT[:, f, a * P:(a + 1) * P], w[:, f, 0:n]
                    else:
                        c0 = (0, CTX)[seg]
                        lhs, rhs = w[:, f, a * P:(a + 1) * P], hT[:, f, c0:c0 + n]
                    ins = nc.tensor.matmul(out, lhsT=lhs, rhs=rhs, start=(f == 0), stop=(f == KT - 1))
                ins.then_inc(proj.sem, 1)
                if u + 1 == len(units) or units[u + 1][0] != g:
                    pe.wait_ge(proj.sem, proj.n(layer, u + 1))
                    pe.sem_inc(wfree.sem, 1)

        def vector_program(dve):
            nc.vector.memset(ones16[:, :], 1.0)
            dve.wait_ge(s_first.sem, 16 * N_FIRST)
            nc.vector.tensor_copy(sel2[:, :, :], ident[0:2, 0:2].unsqueeze(2).broadcast_to([2, 2, P]))
            nc.vector.tensor_copy(selM[:, 0:CAP_L], ident[0:2, 0:1].broadcast_to([2, CAP_L]))
            nc.vector.tensor_copy(selM[:, CAP_L:CAP], ident[0:2, 1:2].broadcast_to([2, CAP_C]))
            dve.wait_ge(s_cond.sem, 2)
            b0, b1 = rowsT[:, 60:64], rowsT[:, 64:68]
            link(nc.vector.tensor_tensor(lbw[:, 0, :], b0, b1, ALU.max))
            nc.vector.tensor_tensor(lbw[:, 1, :], b0, lbw[:, 0, :], ALU.subtract)
            nc.vector.tensor_tensor(lbw[:, 2, :], b1, lbw[:, 0, :], ALU.subtract).then_inc(s_setup.sem, 1)
            dve.wait_ge(s_setup.sem, 2)
            link(nc.vector.tensor_tensor(lbw[:, 3, :], lbw[:, 1, :], lbw[:, 2, :], ALU.add))
            link(nc.vector.reciprocal(lbw[:, 3, :], lbw[:, 3, :]))
            nc.vector.tensor_tensor(lbw[:, 4, :], lbw[:, 1, :], lbw[:, 3, :], ALU.mult)
            link(nc.vector.tensor_tensor(lbw[:, 5, :], lbw[:, 2, :], lbw[:, 3, :], ALU.mult))
            link(nc.vector.tensor_tensor(lbw[:, 5, :], lbw[:, 4, :], lbw[:, 5, :], ALU.add))
            nc.vector.tensor_tensor(lbT[:, 0, :], lbw[:, 4, :], lbw[:, 4, :], ALU.subtract)
            link(nc.vector.tensor_tensor(lbT[:, 1, :], lbw[:, 5, :], lbw[:, 4, :], ALU.subtract))
            nc.vector.tensor_scalar(omlT[:, :, :], lbT[:, :, :], -1.0, 1.0, ALU.mult, ALU.add)
            for layer in range(DEPTH):
                dve_mod(dve, layer)
                dve_norm(dve, layer, 0)
                dve_attention(dve, layer)
                dve_deltanet(dve, layer)
                dve_hgrn(dve, layer)
                dve_out(dve, layer)
                dve_norm(dve, layer, 1)
                dve_experts(dve, layer)

        def dve_mod(dve, layer):
            dve.wait_ge(bmod.sem, bmod.n(layer, 32))
            for g in range(N_MOD):
                dve.wait_ge(modmm.sem, modmm.n(layer, g + 1))
                row = modrow[0:2, g * 512:(g + 1) * 512]
                part = g // 2
                if part in (2, 5):
                    dst = gates[:, part // 3, (g % 2) * 512:(g % 2) * 512 + 512]
                else:
                    dst = row
                nc.vector.tensor_tensor(dst, ps[0:2, g % 2, :], row, ALU.add).then_inc(modadd.sem, 1)
            dve.wait_ge(modT.sem, modT.n(layer, 1))
            for m in range(4):
                src = ps[:, 6, 16 * m:16 * m + 16].rearrange("p (f v) -> p f v", v=2)
                ins = nc.vector.tensor_scalar(modC[:, m, :, :], src, float(m % 2), None, ALU.add)
            ins.then_inc(modcol.sem, 1)

        def dve_norm(dve, layer, which):
            dve.wait_ge(sumsq.sem, sumsq.n(layer, 6 * which + 6))
            nc.vector.tensor_scalar(ss2[:, 0:NT], ss[:, 0:NT], 1.0 / D, EPS, ALU.mult, ALU.add) \
                .then_inc(rstd.sem, 1)
            dve.wait_ge(act_rs.sem, act_rs.n(layer, which + 1))
            for i in range(NT):
                nc.vector.tensor_scalar((xn if which == 0 else xn2)[:, i, :], x[:, i, :], rs[:, i:i + 1], None,
                                        ALU.mult).then_inc(normed.sem, 1)
            dve.wait_ge(modcol.sem, modcol.n(layer, 1))
            for f in range(1, KT, 2):
                dve.wait_ge(normT.sem, normT.n(layer, 8 * which + f + 1))
                b = 2 * (f % 3)
                for v, (bank, c0, n) in enumerate(((b + 1, CTX, LAT), (b, 0, CTX))):
                    ins = nc.vector.tensor_scalar((hT if which == 0 else hT2)[:, f, c0:c0 + n], ps[:, bank, 0:n],
                                                  modC[:, 2 * which + 1, f, v:v + 1],
                                                  modC[:, 2 * which, f, v:v + 1], ALU.mult, ALU.add)
                ins.then_inc(hT_v.sem, 1)


        def attn_units(layer):
            return NQ * len(out_tiles(layer))

        def attn_unit(layer, u):
            qt, h = divmod(u + 48 - attn_units(layer), NQ)
            return qt, h, h // 4, h % 4, (NT_CTX if qt < NT_CTX else NT)

        def dve_attention(dve, layer):
            dve.wait_ge(projev.sem, projev.n(layer, 12))
            flat = qk.rearrange("p i c -> p (i c)")
            dve.wait_ge(normT.sem, normT.n(layer, 8))
            link(nc.vector.tensor_tensor(sq, flat, flat, ALU.mult))
            link(nc.vector.tensor_reduce(ss[:, 0:60], sq.rearrange("p (h d) -> p h d", d=HD), AX, ALU.add))
            nc.vector.tensor_scalar(ss2[:, 0:60], ss[:, 0:60], 1.0 / HD, EPS, ALU.mult, ALU.add) \
                .then_inc(qk_ss.sem, 1)
            dve.wait_ge(qk_rs.sem, qk_rs.n(layer, 1))
            rq = rs[:, 0:60].rearrange("p (i h) -> p i h", h=10)[:, :, 0:NQ]
            link(nc.vector.tensor_scalar(rq, rq, HD ** -0.5, None, ALU.mult))
            qh = qk.rearrange("p i (h d) -> p (i h) d", d=HD)
            link(nc.vector.tensor_tensor(qh, qh, rs[:, 0:60].unsqueeze(2).broadcast_to([P, 60, HD]), ALU.mult))
            for i in range(NT):
                src = qk[:, i, 0:512].rearrange("p (k j d) -> p k j d", k=2, d=HD)
                dst = qn[:, i, 0:512].rearrange("p (j k d) -> p k j d", k=2, d=HD)
                w = small[:, layer, 0:HD].unsqueeze(1).unsqueeze(1).broadcast_to([P, 2, 4, HD])
                nc.vector.tensor_tensor(dst, src, w, ALU.mult)
                src = qk[:, i, 512:640].rearrange("p (k d) -> p k d", d=HD)
                dst = qn[:, i, 512:640].rearrange("p (k d) -> p k d", d=HD)
                w = small[:, layer, HD:2 * HD].unsqueeze(1).broadcast_to([P, 2, HD])
                ins = nc.vector.tensor_tensor(dst, src, w, ALU.mult)
            link(ins)
            cc = cst("cc").rearrange("p (i d) -> p i d", d=HD)
            s_ = cst("ss").rearrange("p (i b h d) -> p i b h d", b=2, h=2, d=16)
            for i in range(NT_LAT):
                q = qn[:, NT_CTX + i, :]
                t1 = qk[:, NT_CTX + i, :]
                nc.vector.tensor_tensor(t1.rearrange("p (h d) -> p h d", d=HD), q.rearrange("p (h d) -> p h d", d=HD),
                                        cc[:, i, :].unsqueeze(1).broadcast_to([P, 10, HD]), ALU.mult)
                for half in range(2):
                    src = q.rearrange("p (a b h d) -> p a b h d", b=2, h=2, d=16)[:, :, :, 1 - half, :]
                    dst = rope2.rearrange("p (a b h d) -> p a b h d", b=2, h=2, d=16)[:, :, :, half, :]
                    tab = s_[:, i, :, half, :].unsqueeze(1).broadcast_to([P, 10, 2, 16])
                    ins = nc.vector.tensor_tensor(dst, src, tab, ALU.mult)
                link(ins)
                link(nc.vector.tensor_tensor(q, t1, rope2, ALU.add))
            nc.vector.memset(ss[:, 60:61], 0.0).then_inc(qk_ready.sem, 1)

            def row_max(u):
                nk = attn_unit(layer, u)[4]
                dve.wait_ge(score.sem, score.n(layer, u + 1))
                b = 2 * (u % 2)
                nc.vector.tensor_reduce(nmax[:, u:u + 1], ps[:, b:b + 2, :].rearrange("p b n -> p (b n)")[:, 0:nk * P],
                                        AX, ALU.max, negate=True).then_inc(smax.sem, 1)

            def evacuate(u):
                nk = attn_unit(layer, u)[4]
                na = 2 * nk // 3
                dve.wait_ge(ptt.sem, ptt.n(layer, u + 1))
                if u >= 2:
                    dve.wait_ge(pv.sem, pv.n(layer, u - 1))
                nc.vector.tensor_copy(probT[u % 2][:, na * P:nk * P], ps[:, 5, 0:(nk - na) * P]).then_inc(pt_v.sem, 1)

            def finish(u):
                qt, h, _, _, _ = attn_unit(layer, u)
                dve.wait_ge(expd.sem, expd.n(layer, u + 1))
                link(nc.vector.reciprocal(rinv[:, u:u + 1], rsum[:, u:u + 1]))
                dve.wait_ge(pv.sem, pv.n(layer, u + 1))
                nc.vector.tensor_scalar(ycat[:, qt, h * HD:(h + 1) * HD], ps[:, 6 + u % 2, 0:HD], rinv[:, u:u + 1],
                                        None, ALU.mult).then_inc(attn_y.sem, 1)

            nc.vector.memset(convin[:, :, 0:2], 0.0)
            nc.vector.memset(convin[:, :, 258:262], 0.0)
            link(nc.vector.memset(convin[:, :, 774:776], 0.0))
            dve.wait_ge(projev.sem, projev.n(layer, 48))

            def conv_step(n):
                k, j = divmod(n, 6)
                w = rowsT[:, layer * 30 + n:layer * 30 + n + 1]
                if k == 0:
                    ins = nc.vector.tensor_scalar(convout[:, j, :], convin[:, j, 0:772], w, None, ALU.mult)
                else:
                    dve.wait_ge(conv.sem, conv.n(layer, n - 5))
                    ins = nc.vector.scalar_tensor_tensor(convout[:, j, :], convin[:, j, k:k + 772], w,
                                                         convout[:, j, :], ALU.mult, ALU.add)
                ins.then_inc(conv.sem, 1)

            row_max(0)
            for u in range(attn_units(layer)):
                if u < 30:
                    conv_step(u)
                if u < 4:
                    f = hgc[:, 2 + u, :]
                    nc.vector.tensor_scalar(f, f, omlT[:, layer, u:u + 1], lbT[:, layer, u:u + 1], ALU.mult, ALU.add) \
                        .then_inc(f_v.sem, 1)
                if u + 1 < attn_units(layer):
                    row_max(u + 1)
                evacuate(u)
                if u >= 1:
                    finish(u - 1)
            finish(attn_units(layer) - 1)

        def act_attention(act, layer):
            for p in range(5):
                act.wait_ge(qkt.sem, qkt.n(layer, p + 1))
                b = 2 * (p % 3)
                nc.scalar.activation(qkT[:, p, 0:512], ps[:, b, :], ACT.Copy)
                nc.scalar.activation(qkT[:, p, 512:768], ps[:, b + 1, 0:256], ACT.Copy).then_inc(qktev.sem, 1)

            def exps(u):
                nk = attn_unit(layer, u)[4]
                act.wait_ge(smax.sem, smax.n(layer, u + 1))
                if u >= 2:
                    act.wait_ge(ptt.sem, ptt.n(layer, u - 1))
                b = 2 * (u % 2)
                nc.scalar.activation(prob[u % 2][:, 0:nk * P],
                                     ps[:, b:b + 2, :].rearrange("p b n -> p (b n)")[:, 0:nk * P], ACT.Exp,
                                     bias=nmax[:, u:u + 1], accum_out=rsum[:, u:u + 1]).then_inc(expd.sem, 1)

            exps(0)
            for u in range(attn_units(layer)):
                if u + 1 < attn_units(layer):
                    exps(u + 1)
                nk = attn_unit(layer, u)[4]
                na = 2 * nk // 3
                act.wait_ge(ptt.sem, ptt.n(layer, u + 1))
                if u >= 2:
                    act.wait_ge(pv.sem, pv.n(layer, u - 1))
                nc.scalar.activation(probT[u % 2][:, 0:na * P], ps[:, 4, 0:na * P], ACT.Copy).then_inc(pt_a.sem, 1)

        def pe_attention(pe, layer):
            pe.wait_ge(qk_ready.sem, qk_ready.n(layer, 1))
            pe.wait_ge(projev.sem, projev.n(layer, 48))
            for p in range(5):
                if p >= 3:
                    pe.wait_ge(qktev.sem, qktev.n(layer, p - 2))
                b = 2 * (p % 3)
                for i in range(NT):
                    ins = nc.tensor.transpose(ps[:, b + i // 4, (i % 4) * P:(i % 4 + 1) * P],
                                              qn[:, i, p * P:(p + 1) * P], ident)
                ins.then_inc(qkt.sem, 1)
            pe.wait_ge(qktev.sem, qktev.n(layer, 5))

            def scores(u):
                qt, h, kv, j, nk = attn_unit(layer, u)
                if u >= 2:
                    pe.wait_ge(expd.sem, expd.n(layer, u - 1))
                b = 2 * (u % 2)
                part = slice(kv * HD, (kv + 1) * HD)
                for n0 in range(0, nk * P, 512):
                    n = min(512, nk * P - n0)
                    ins = nc.tensor.matmul(ps[:, b + n0 // 512, 0:n], lhsT=qkT[part, j, qt * P:(qt + 1) * P],
                                           rhs=qkT[part, 4, n0:n0 + n], start=True, stop=True)
                ins.then_inc(score.sem, 1)

            def turn(u):
                nk = attn_unit(layer, u)[4]
                na = 2 * nk // 3
                pe.wait_ge(expd.sem, expd.n(layer, u + 1))
                if u >= 1:
                    pe.wait_ge(pt_a.sem, pt_a.n(layer, u))
                    pe.wait_ge(pt_v.sem, pt_v.n(layer, u))
                for kt in range(nk):
                    out = ps[:, 4, kt * P:(kt + 1) * P] if kt < na else ps[:, 5, (kt - na) * P:(kt - na + 1) * P]
                    ins = nc.tensor.transpose(out, prob[u % 2][:, kt * P:(kt + 1) * P], ident)
                ins.then_inc(ptt.sem, 1)

            def values(u):
                qt, h, kv, j, nk = attn_unit(layer, u)
                pe.wait_ge(pt_a.sem, pt_a.n(layer, u + 1))
                pe.wait_ge(pt_v.sem, pt_v.n(layer, u + 1))
                if u >= 2:
                    pe.wait_ge(attn_y.sem, attn_y.n(layer, u - 1))
                for kt in range(nk):
                    ins = nc.tensor.matmul(ps[:, 6 + u % 2, 0:HD], lhsT=probT[u % 2][:, kt * P:(kt + 1) * P],
                                           rhs=vtok[:, kt, kv * HD:(kv + 1) * HD], start=(kt == 0), stop=(kt == nk - 1))
                ins.then_inc(pv.sem, 1)

            scores(0)
            for u in range(attn_units(layer)):
                if u + 1 < attn_units(layer):
                    scores(u + 1)
                if u >= 1:
                    values(u - 1)
                turn(u)
            values(attn_units(layer) - 1)

        def order(d):
            c, l = list(range(NCH_CTX)), list(range(NCH_CTX, NCH))
            return c + l if d == 0 else c[::-1] + l[::-1]

        HB = [slice(0, 64), slice(64, 128)]

        def head_bc(v):
            return v.unsqueeze(2).broadcast_to([P, DNH, HD])

        def mask_bc(v):
            return v.unsqueeze(1).broadcast_to([P, DNH, HD])

        def dve_deltanet(dve, layer):
            dve.wait_ge(attn_y.sem, attn_y.n(layer, attn_units(layer)))
            alog, dtb = small[:, layer, 256:264], small[:, layer, 264:272]
            link(nc.vector.tensor_tensor(ga[:, :, :], dz[:, :, 264:272], dtb.unsqueeze(1).broadcast_to([P, NT, 8]),
                                         ALU.add))
            link(nc.vector.tensor_scalar(gb[:, :, :], ga[:, :, :], -1.0, None, ALU.mult))
            nc.vector.tensor_tensor(gb[:, :, :], gb[:, :, :], ga[:, :, :], ALU.min).then_inc(gate_v.sem, 1)
            dve.wait_ge(gate_a.sem, gate_a.n(layer, 4))
            link(nc.vector.tensor_scalar(bt[:, :, :], bt[:, :, :], 1.0, None, ALU.add))
            nc.vector.reciprocal(bt[:, :, :], bt[:, :, :])
            link(nc.vector.scalar_tensor_tensor(gg[:, :, :], ga[:, :, :], 0.0, gb[:, :, :], ALU.max, ALU.add))
            link(nc.vector.scalar_tensor_tensor(gg[:, :, :], gg[:, :, :], -1.0,
                                                ealog[:, :].unsqueeze(1).broadcast_to([P, NT, 8]), ALU.mult, ALU.mult))
            for i in range(NT):
                dve.wait_ge(dtev.sem, dtev.n(layer, i + 1))
                link(nc.vector.tensor_tensor(sq_dn[:, i], dt[:, i, 0:512], dt[:, i, 0:512], ALU.mult))
                ins = nc.vector.tensor_reduce(ss[:, 8 * i:8 * i + 8], sq_dn[:, i].rearrange("p (h d) -> p h d", d=HD),
                                              AX, ALU.add)
            link(ins)
            nc.vector.tensor_scalar(ss2[:, 0:48], ss[:, 0:48], EPS, None, ALU.add).then_inc(dn_ss.sem, 1)
            dve.wait_ge(dn_rs.sem, dn_rs.n(layer, 1))
            rq = rs[:, 0:48].rearrange("p (i h) -> p i h", h=8)[:, :, 0:DNH]
            link(nc.vector.tensor_scalar(rq, rq, HD ** -0.5, None, ALU.mult))
            for i in range(NT):
                v = dt[:, i, 0:512].rearrange("p (h d) -> p h d", d=HD)
                nc.vector.tensor_tensor(v, v, rs[:, 8 * i:8 * i + 8].unsqueeze(2).broadcast_to([P, 8, HD]),
                                        ALU.mult).then_inc(dn_norm.sem, 1)
            dve.wait_ge(kqtev.sem, kqtev.n(layer, 6))
            for d in range(2):
                base = 6 * d
                causal = cst(f"causal{d}")
                for i in range(NT):
                    nc.vector.tensor_tensor(NL[:, i], mask_bc(causal), head_bc(gg[:, i, 4 * d:4 * d + 4]),
                                            ALU.mult).then_inc(gbr.sem, 1)
                dve.wait_ge(dexp.sem, dexp.n(layer, 7 * d + 7))
                link(nc.vector.tensor_tensor(eb[:, :, :], sc[:, 24:48].rearrange("p (i h) -> p i h", h=4),
                                             bt[:, :, 4 * d:4 * d + 4], ALU.mult))
                for i in range(NT):
                    k_ = dt[:, i, 256:512].rearrange("p (h d) -> p h d", d=HD)
                    nc.vector.tensor_tensor(vke[:, i, :, HD:2 * HD], k_, head_bc(sc[:, 4 * i:4 * i + 4]), ALU.mult)
                    ins = nc.vector.tensor_tensor(kbe[:, i], k_, head_bc(eb[:, i, :]), ALU.mult)
                ins.then_inc(kev.sem, 1)
                for i in range(NT):
                    link(nc.vector.tensor_tensor(Dm[:, i], Dm[:, i], mask_bc(causal), ALU.mult))
                    dve.wait_ge(gram.sem, gram.n(layer, base + i + 1))
                    for hb in range(2):
                        bank = 2 * (i % 3) + hb
                        src = ps[:, bank, 0:256].rearrange("p (b k t) -> p b k t", b=2, k=2)
                        hs = Dm[:, i].rearrange("p (b h) t -> p b h t", h=2)[:, :, hb, :]
                        nc.vector.tensor_tensor(AT[:, i].rearrange("p (b h) t -> p b h t", h=2)[:, :, hb, :], hs,
                                                src[:, :, 1, :], ALU.mult)
                        ins = nc.vector.tensor_tensor(NTm[:, i].rearrange("p (b h) t -> p b h t", h=2)[:, :, hb, :], hs,
                                                      src[:, :, 0, :], ALU.mult)
                    link(ins)
                    nc.vector.tensor_tensor(NTm[:, i], NTm[:, i], head_bc(bt[:, i, 4 * d:4 * d + 4]), ALU.mult) \
                        .then_inc(pairs.sem, 1)
                for level in range(LEVELS):
                    m = mask_bc(lvl[d][:, level, :])
                    first = 36 * d + 6 * level
                    for i in range(NT):
                        if level == 0:
                            dve.wait_ge(pairs.sem, pairs.n(layer, base + i + 1))
                        else:
                            dve.wait_ge(umm.sem, umm.n(layer, first - 6 + i + 1))
                            if level == 1:
                                dve.wait_ge(tru.sem, tru.n(layer, first - 6 + i + 1))
                        ins = nc.vector.tensor_tensor(NL[:, i], NTm[:, i], m, ALU.mult)
                        ins.then_inc(nl.sem, 1)
                    for i in range(NT):
                        i64 = mask_bc(cst("ident64"))
                        if level == 0:
                            dve.wait_ge(nl.sem, nl.n(layer, first + i + 1))
                            nc.vector.tensor_tensor(TR[:, i, 1], i64, NL[:, i], ALU.subtract)
                            dve.wait_ge(umm.sem, umm.n(layer, first + i + 1))
                            ins = nc.vector.tensor_tensor(TR[:, i, 0], i64,
                                                          ps[:, 6 + i % 2, 0:256].rearrange("p (h t) -> p h t", h=4),
                                                          ALU.subtract)
                        else:
                            dve.wait_ge(trm.sem, trm.n(layer, 30 * d + 6 * (level - 1) + i + 1))
                            if level < LEVELS - 1:
                                v = TR[:, i].rearrange("p a h t -> p (a h t)")
                                src = ps[:, i, :]
                            else:
                                v = TR[:, i, 1].rearrange("p h t -> p (h t)")
                                src = ps[:, i, 256:512]
                            ins = nc.vector.tensor_tensor(v, v, src, ALU.subtract)
                        ins.then_inc(tru.sem, 1)
                for i in range(NT):
                    dve.wait_ge(gmm.sem, gmm.n(layer, base + i + 1))
                    for par in range(2):
                        c = 2 * i + par
                        for pair in range(2):
                            for hb in range(2):
                                h = 2 * pair + hb
                                ins = nc.vector.scalar_tensor_tensor(
                                    G[HB[hb], c, pair, :], cst("ident64")[HB[hb], :],
                                    sc[HB[hb], 48 + 4 * c + h:49 + 4 * c + h],
                                    ps[HB[hb], 2 * (i % 2) + par, 128 + 64 * pair:192 + 64 * pair],
                                    ALU.mult, ALU.subtract)
                    ins.then_inc(gev_v.sem, 1)
                seq = order(d)
                nc.vector.memset(S[:, seq[0], :, :], 0.0).then_inc(stepv.sem, 1)
                dve.wait_ge(gev_a.sem, gev_a.n(layer, base + 6))
                for n in range(NCH - 1):
                    dve.wait_ge(step.sem, step.n(layer, 11 * d + n + 1))
                    nc.vector.tensor_tensor(S[:, seq[n + 1], :, :],
                                            ps[:, 4 + n % 2, 0:128].rearrange("p (b v) -> p b v", b=2),
                                            Uc[:, seq[n], :, :], ALU.add).then_inc(stepv.sem, 1)
                outs = list(out_tiles(layer))
                base_o = len(outs) * d

                def fresh_values(i):
                    dve.wait_ge(zmm.sem, zmm.n(layer, base_o + outs.index(i) + 1))
                    for hb in range(2):
                        bank = 2 * (i % 2) + hb
                        src = ps[:, bank, 0:256].rearrange("p (k b t) -> p k b t", k=2, b=2)
                        vn = vnew[:, i].rearrange("p (b h) t -> p b h t", h=2)[:, :, hb, :]
                        yv = ysol[:, i, :, 0:HD].rearrange("p (b h) t -> p b h t", h=2)[:, :, hb, :]
                        nc.vector.tensor_tensor(vn, yv, src[:, 0], ALU.subtract)
                        ecum = sc[:, 4 * i:4 * i + 4].rearrange("p (b h) -> p b h", h=2)[:, :, hb:hb + 1] \
                            .broadcast_to([P, 2, HD])
                        ot = otmp[:, i].rearrange("p (b h) t -> p b h t", h=2)[:, :, hb, :]
                        ins = nc.vector.tensor_tensor(ot, src[:, 1], ecum, ALU.mult)
                    link(ins)
                    nc.vector.tensor_tensor(vnew[:, i], vnew[:, i], head_bc(bt[:, i, 4 * d:4 * d + 4]), ALU.mult) \
                        .then_inc(vnw.sem, 1)

                def outputs(i):
                    dve.wait_ge(avm.sem, avm.n(layer, base_o + outs.index(i) + 1))
                    yd = ycat[:, i, 512:768]
                    ot = otmp[:, i].rearrange("p h t -> p (h t)")
                    src = ps[:, 4 + i % 2, 0:256]
                    if d == 0:
                        nc.vector.tensor_tensor(yd, ot, src, ALU.add).then_inc(outv.sem, 1)
                    else:
                        link(nc.vector.tensor_tensor(ot, ot, src, ALU.add))
                        nc.vector.tensor_tensor(yd, yd, ot, ALU.add).then_inc(outv.sem, 1)

                for i in outs:
                    fresh_values(i)
                    if i > outs[0]:
                        outputs(i - 1)
                outputs(NT - 1)
                dve.wait_ge(outv.sem, outv.n(layer, base_o + len(outs)))

        def dve_squares(dve, layer, which, c0):
            o = ycat[:, :, c0:c0 + 256]
            link(nc.vector.tensor_tensor(sqg, o, o, ALU.mult))
            link(nc.vector.tensor_reduce(ss[:, 0:24], sqg.rearrange("p i (h d) -> p (i h) d", d=HD), AX, ALU.add))
            nc.vector.tensor_scalar(ss2[:, 0:24], ss[:, 0:24], 1.0 / HD, EPS, ALU.mult, ALU.add) \
                .then_inc(go_ss.sem, 1)

        def dve_gated(dve, layer, which, c0, z):
            o = ycat[:, :, c0:c0 + 256]
            dve.wait_ge(go_rs.sem, go_rs.n(layer, which + 1))
            w = small[:, layer, (2 + which) * HD:(3 + which) * HD]
            for i in range(NT):
                oh = ycat[:, i, c0:c0 + 256].rearrange("p (h d) -> p h d", d=HD)
                nc.vector.tensor_tensor(oh, oh, head_bc(rs[:, 4 * i:4 * i + 4]), ALU.mult)
                zh = z[:, i, :].rearrange("p (h d) -> p h d", d=HD)
                ins = nc.vector.tensor_tensor(zh, zh, mask_bc(w), ALU.mult)
            link(ins)
            link(nc.vector.tensor_tensor(o, o, z, ALU.mult))

        def act_gated(act, layer, which):
            act.wait_ge(go_ss.sem, go_ss.n(layer, which + 1))
            link_act(nc.scalar.activation(rs[:, 0:24], ss2[:, 0:24], ACT.Ln))
            nc.scalar.activation(rs[:, 0:24], rs[:, 0:24], ACT.Exp, scale=-0.5).then_inc(go_rs.sem, 1)

        def act_deltanet(act, layer):
            for j in range(6):
                act.wait_ge(conv.sem, conv.n(layer, 24 + j + 1))
                nc.scalar.activation(convout[:, j, :], convout[:, j, :], ACT.Silu).then_inc(convact.sem, 1)
            nc.scalar.activation(bt[:, :, :], dz[:, :, 256:264], ACT.Exp, scale=-1.0).then_inc(gate_a.sem, 1)
            nc.scalar.activation(ealog[:, :], small[:, layer, 256:264], ACT.Exp).then_inc(gate_a.sem, 1)
            act.wait_ge(gate_v.sem, gate_v.n(layer, 1))
            nc.scalar.activation(gb[:, :, :], gb[:, :, :], ACT.Exp).then_inc(gate_a.sem, 1)
            act.wait_ge(gate_a.sem, gate_a.n(layer, 3))
            nc.scalar.activation(gb[:, :, :], gb[:, :, :], ACT.Ln, bias=1.0).then_inc(gate_a.sem, 1)
            for i in range(NT):
                act.wait_ge(dtt.sem, dtt.n(layer, i + 1))
                b = 2 * (i % 3)
                nc.scalar.activation(dt[:, i, 0:512], ps[:, b, :], ACT.Copy)
                nc.scalar.activation(dt[:, i, 512:768], ps[:, b + 1, 0:256], ACT.Copy).then_inc(dtev.sem, 1)
            act.wait_ge(dn_ss.sem, dn_ss.n(layer, 1))
            link_act(nc.scalar.activation(rs[:, 0:48], ss2[:, 0:48], ACT.Ln))
            nc.scalar.activation(rs[:, 0:48], rs[:, 0:48], ACT.Exp, scale=-0.5).then_inc(dn_rs.sem, 1)
            for i in range(NT):
                act.wait_ge(kqt.sem, kqt.n(layer, i + 1))
                for kind in range(2):
                    ins = nc.scalar.activation(
                        kqT[:, :, 2 * i:2 * i + 2, kind, :],
                        ps[:, 2 * (i % 3), 256 * kind:256 * kind + 256].rearrange("p (b c t) -> p b c t", b=2, c=2),
                        ACT.Copy)
                ins.then_inc(kqtev.sem, 1)
            for d in range(2):
                base = 6 * d
                if d == 1:
                    act.wait_ge(outv.sem, outv.n(layer, len(out_tiles(layer))))
                for i in range(NT):
                    act.wait_ge(decay.sem, decay.n(layer, base + i + 1))
                    nc.scalar.activation(Dm[:, i], ps[:, i, 0:256].rearrange("p (h t) -> p h t", h=4), ACT.Exp) \
                        .then_inc(dexp.sem, 1)
                nc.scalar.activation(sc[:, :], ps[:, 6, 0:96], ACT.Exp).then_inc(dexp.sem, 1)
                nc.scalar.activation(vke[:, :, :, 0:HD], dt[:, :, 512:768].rearrange("p i (h d) -> p i h d", d=HD),
                                     ACT.Copy).then_inc(vke_v.sem, 1)
                for level in range(1, LEVELS):
                    for i in range(NT):
                        act.wait_ge(umm.sem, umm.n(layer, 36 * d + 6 * level + i + 1))
                        if level == 1:
                            act.wait_ge(pairs.sem, pairs.n(layer, base + 6))
                        if level > 1:
                            act.wait_ge(trm.sem, trm.n(layer, 30 * d + 6 * (level - 2) + i + 1))
                        nc.scalar.activation(Um[:, i], ps[:, 6 + i % 2, 0:256].rearrange("p (h t) -> p h t", h=4),
                                             ACT.Copy).then_inc(uev.sem, 1)
                for i in range(NT):
                    act.wait_ge(ymm.sem, ymm.n(layer, base + i + 1))
                    nc.scalar.activation(ysol[:, i].rearrange("p h t -> p (h t)"), ps[:, i, :], ACT.Copy) \
                        .then_inc(yev.sem, 1)
                for i in range(NT):
                    act.wait_ge(gmm.sem, gmm.n(layer, base + i + 1))
                    act.wait_ge(gev_v.sem, gev_v.n(layer, base + i + 1))
                    for par in range(2):
                        bank = 2 * (i % 2) + par
                        nc.scalar.activation(ykT[:, i, :, par, :], ps[:, bank, 0:128].rearrange("p (b t) -> p b t", b=2),
                                             ACT.Copy)
                        ins = nc.scalar.activation(Uc[:, 2 * i + par, :, :],
                                                   ps[:, bank, 256:384].rearrange("p (b t) -> p b t", b=2), ACT.Copy)
                    ins.then_inc(gev_a.sem, 1)

        def pe_deltanet(pe, layer):
            pe.wait_ge(attn_y.sem, attn_y.n(layer, attn_units(layer)))
            pe.wait_ge(convact.sem, convact.n(layer, 6))
            for i in range(NT):
                if i >= 3:
                    pe.wait_ge(dtev.sem, dtev.n(layer, i - 2))
                c0 = i * P if i < NT_CTX else i * P + 4
                for j in range(6):
                    ins = nc.tensor.transpose(ps[:, 2 * (i % 3) + j // 4, (j % 4) * P:(j % 4 + 1) * P],
                                              convout[:, j, c0:c0 + P], ident)
                ins.then_inc(dtt.sem, 1)
            pe.wait_ge(dtev.sem, dtev.n(layer, 6))
            for i in range(NT):
                pe.wait_ge(dn_norm.sem, dn_norm.n(layer, i + 1))
                if i >= 3:
                    pe.wait_ge(kqtev.sem, kqtev.n(layer, i - 2))
                for n, c0 in enumerate((256, 384, 0, 128)):
                    ins = nc.tensor.transpose(ps[:, 2 * (i % 3), n * P:(n + 1) * P], dt[:, i, c0:c0 + P], ident)
                ins.then_inc(kqt.sem, 1)
            pe.wait_ge(kqtev.sem, kqtev.n(layer, 6))
            for d in range(2):
                base = 6 * d
                if d == 1:
                    pe.wait_ge(outv.sem, outv.n(layer, len(out_tiles(layer))))
                strict, incl = cst(f"strict{d}"), cst(f"incl{d}")
                ind = cst("chunkind").rearrange("p (c m) -> p c m", c=2)
                for i in range(NT):
                    pe.wait_ge(gbr.sem, gbr.n(layer, base + i + 1))
                    g = gg[:, i, 4 * d:4 * d + 4]
                    for out, lhs in ((ps[:, 6, 4 * i:4 * i + 4], incl), (ps[:, 6, 24 + 4 * i:28 + 4 * i], strict),
                                     (ps[:, 6, 48 + 8 * i:52 + 8 * i], ind[:, 0, :]),
                                     (ps[:, 6, 52 + 8 * i:56 + 8 * i], ind[:, 1, :])):
                        nc.tensor.matmul(out, lhsT=lhs, rhs=g, start=True, stop=True)
                    nc.tensor.matmul(ps[:, i, 0:256], lhsT=strict, rhs=NL[:, i].rearrange("p h t -> p (h t)"),
                                     start=True, stop=True).then_inc(decay.sem, 1)
                pe.wait_ge(dexp.sem, dexp.n(layer, 7 * d + 7))
                for i in range(NT):
                    if i >= 3:
                        pe.wait_ge(pairs.sem, pairs.n(layer, base + i - 2))
                    for hb in range(2):
                        for par in range(2):
                            c = 2 * i + par
                            for pair in range(2):
                                ins = nc.tensor.matmul(
                                    ps[HB[par], 2 * (i % 3) + hb, 128 * pair:128 * pair + 128],
                                    lhsT=kqT[HB[hb], pair, c, 0, :],
                                    rhs=kqT[HB[hb], pair, c, :, :].rearrange("p k t -> p (k t)"),
                                    start=True, stop=True)
                    ins.then_inc(gram.sem, 1)

                def small_products(bank, c0, lhs, rhs, i, width=64):
                    for par in range(2):
                        for h in range(DNH):
                            ins = nc.tensor.matmul(ps[HB[par], bank, c0 + width * h:c0 + width * (h + 1)],
                                                   lhsT=lhs[HB[par], i, h, :], rhs=rhs(par, h), start=True, stop=True)
                    return ins

                for level in range(LEVELS):
                    first = 36 * d + 6 * level

                    def products(i, level=level, first=first):
                        pe.wait_ge(uev.sem, uev.n(layer, 30 * d + 6 * (level - 1) + i + 1))
                        if level < LEVELS - 1:
                            small_products(i, 0, TR[:, :, 1], lambda par, h: Um[HB[par], i, h, :], i)
                        ins = small_products(i, 256, Um, lambda par, h: TR[HB[par], i, 1, h, :], i)
                        ins.then_inc(trm.sem, 1)

                    for i in range(NT):
                        pe.wait_ge(nl.sem, nl.n(layer, first + i + 1))
                        if level == 0:
                            if i == 0:
                                pe.wait_ge(pairs.sem, pairs.n(layer, base + 6))
                            if i >= 2:
                                pe.wait_ge(tru.sem, tru.n(layer, first + i - 1))
                            rhs = lambda par, h: cst("ident64")[HB[par], :]
                        else:
                            pe.wait_ge(tru.sem, tru.n(layer, first - 6 + i + 1))
                            if level == 1 and i < 2:
                                pe.wait_ge(tru.sem, tru.n(layer, first))
                            if 6 * (level - 1) + i >= 2:
                                pe.wait_ge(uev.sem, uev.n(layer, 30 * d + 6 * (level - 1) + i - 1))
                            rhs = lambda par, h, i=i: TR[HB[par], i, 0, h, :]
                        small_products(6 + i % 2, 0, NL, rhs, i).then_inc(umm.sem, 1)
                        if level >= 1 and i >= 1:
                            products(i - 1)
                    if level >= 1:
                        products(NT - 1)
                pe.wait_ge(vke_v.sem, vke_v.n(layer, d + 1))
                pe.wait_ge(kev.sem, kev.n(layer, d + 1))
                pe.wait_ge(tru.sem, tru.n(layer, 36 * d + 36))
                for i in range(NT):
                    small_products(i, 0, TR[:, :, 1], lambda par, h: vke[HB[par], i, h, :], i, width=128) \
                        .then_inc(ymm.sem, 1)
                pe.wait_ge(yev.sem, yev.n(layer, base + 6))
                for i in range(NT):
                    if i >= 2:
                        pe.wait_ge(gev_a.sem, gev_a.n(layer, base + i - 1))
                    for par in range(2):
                        for pair in range(2):
                            for hb in range(2):
                                h = 2 * pair + hb
                                out = ps[HB[hb], 2 * (i % 2) + par, :]
                                nc.tensor.matmul(out[:, 64 * pair:64 * pair + 64], lhsT=vke[HB[par], i, h, HD:2 * HD],
                                                 rhs=TR[HB[par], i, 1, h, :], start=True, stop=True)
                                nc.tensor.matmul(out[:, 128 + 64 * pair:192 + 64 * pair],
                                                 lhsT=ysol[HB[par], i, h, HD:2 * HD], rhs=kbe[HB[par], i, h, :],
                                                 start=True, stop=True)
                                ins = nc.tensor.matmul(out[:, 256 + 64 * pair:320 + 64 * pair],
                                                       lhsT=kbe[HB[par], i, h, :], rhs=ysol[HB[par], i, h, 0:HD],
                                                       start=True, stop=True)
                    ins.then_inc(gmm.sem, 1)
                pe.wait_ge(gev_a.sem, gev_a.n(layer, base + 6))
                seq = order(d)
                for n in range(NCH - 1):
                    pe.wait_ge(stepv.sem, stepv.n(layer, 12 * d + n + 1))
                    for pair in range(2):
                        for hb in range(2):
                            ins = nc.tensor.matmul(ps[HB[hb], 4 + n % 2, 64 * pair:64 * pair + 64],
                                                   lhsT=G[HB[hb], seq[n], pair, :], rhs=S[HB[hb], seq[n], pair, :],
                                                   start=True, stop=True)
                    ins.then_inc(step.sem, 1)
                pe.wait_ge(stepv.sem, stepv.n(layer, 12 * d + NCH))

                outs = list(out_tiles(layer))
                base_o = len(outs) * d

                def apply_values(i):
                    n = outs.index(i)
                    pe.wait_ge(vnw.sem, vnw.n(layer, base_o + n + 1))
                    if n >= 2:
                        pe.wait_ge(outv.sem, outv.n(layer, base_o + n - 1))
                    small_products(4 + i % 2, 0, AT, lambda par, h: vnew[HB[par], i, h, :], i).then_inc(avm.sem, 1)

                for n, i in enumerate(outs):
                    if n >= 2:
                        pe.wait_ge(vnw.sem, vnw.n(layer, base_o + n - 1))
                    for hb in range(2):
                        for par in range(2):
                            c = 2 * i + par
                            for pair in range(2):
                                out = ps[HB[par], 2 * (i % 2) + hb, :]
                                nc.tensor.matmul(out[:, 64 * pair:64 * pair + 64], lhsT=ykT[HB[hb], i, pair, par, :],
                                                 rhs=S[HB[hb], c, pair, :], start=True, stop=True)
                                ins = nc.tensor.matmul(out[:, 128 + 64 * pair:192 + 64 * pair],
                                                       lhsT=kqT[HB[hb], pair, c, 1, :], rhs=S[HB[hb], c, pair, :],
                                                       start=True, stop=True)
                    ins.then_inc(zmm.sem, 1)
                    if n >= 1:
                        apply_values(i - 1)
                apply_values(NT - 1)


        def dve_hgrn(dve, layer):
            V = hgt[:, :, 0:256]
            for d in range(2):
                f = hgc[:, 2 + 2 * d:4 + 2 * d, :]
                if d == 0:
                    link(nc.vector.memset(reset, 1.0))
                    link(nc.vector.memset(reset[:, :, 0:1], 0.0))
                nc.vector.memset(gpad[:, :, :, 0:1], 0.0)
                link(nc.vector.memset(Ah, 0.0))
                dve.wait_ge(f_v.sem, f_v.n(layer, 4))
                nc.vector.tensor_scalar(kk, f, -1.0, 1.0, ALU.mult, ALU.add)
                dve.wait_ge(g_a.sem, g_a.n(layer, d + 1))
                for j in range(2):
                    ins = nc.vector.tensor_tensor_scan(Cc[:, j].rearrange("p c t -> p (c t)"),
                                                       reset.rearrange("p c t -> p (c t)"),
                                                       gpad[:, j].rearrange("p c t -> p (c t)"), 0.0, ALU.mult, ALU.add)
                link(ins)
                off = 1 - d
                for j in range(2):
                    xs = Cc[:, j, :, off:off + CHUNK]
                    ins = nc.vector.tensor_tensor(ER[:, j].rearrange("p (c t) -> p c t", c=NCH),
                                                  Cc[:, j, :, CHUNK:CHUNK + 1].broadcast_to([P, NCH, CHUNK]), xs,
                                                  ALU.subtract)
                ins.then_inc(er_v.sem, 1)

                def halves(v, level, half):
                    h = 1 << level
                    return v.rearrange("p (a f h) -> p a f h", f=2, h=h)[:, :, half, :]

                def distance(n):
                    level, j = divmod(n, 2)
                    h = 1 << level
                    nb = CHUNK // (2 * h)
                    if n >= 4:
                        dve.wait_ge(hgram.sem, hgram.n(layer, 14 * d + n - 3))
                    xs = Cc[:, j, :, off:off + CHUNK].rearrange("p c (b f h) -> p c b f h", f=2, h=h)
                    mid = Cc[:, j, :, h:h + (nb - 1) * 2 * h + 1:2 * h].unsqueeze(3).broadcast_to([P, NCH, nb, h])
                    z = Z[n % 4].rearrange("p (c b f h) -> p c b f h", c=NCH, f=2, h=h)
                    nc.vector.tensor_tensor(z[:, :, :, 0, :], mid, xs[:, :, :, 0, :], ALU.subtract)
                    nc.vector.tensor_tensor(z[:, :, :, 1, :], xs[:, :, :, 1, :], mid, ALU.subtract) \
                        .then_inc(zsub.sem, 1)

                def weigh(n):
                    level, j = divmod(n, 2)
                    dve.wait_ge(zexp.sem, zexp.n(layer, 12 * d + n + 1))
                    z = Z[n % 4]
                    for half in range(2):
                        other = kk[:, j, :] if half == d else hgc[:, j, :]
                        ins = nc.vector.tensor_tensor(halves(z, level, half), halves(z, level, half),
                                                      halves(other, level, half), ALU.mult)
                    ins.then_inc(zmul.sem, 1)

                def place(n):
                    level, j = divmod(n, 2)
                    dve.wait_ge(hgram.sem, hgram.n(layer, 14 * d + n + 1))
                    m = lvl_i[d][:, level, :].unsqueeze(1).broadcast_to([P, NT, HD])
                    if n >= 2:
                        dve.wait_ge(hpred.sem, hpred.n(layer, 14 * d + n - 1))
                    for hb in range(2):
                        ins = nc.vector.copy_predicated(
                            Ah[:, 2 * j + hb], m,
                            ps[:, 2 * (n % 3) + hb, 0:384].rearrange("p (i t) -> p i t", i=NT))
                    ins.then_inc(hpred.sem, 1)

                distance(0)
                for n in range(14):
                    if n + 1 < 12:
                        distance(n + 1)
                    if n < 12:
                        weigh(n)
                    if n == 2:
                        dve.wait_ge(er_a.sem, er_a.n(layer, d + 1))
                        qd, kd = (ED, ER) if d == 0 else (ER, ED)
                        nc.vector.tensor_tensor(qd, qd, hgc[:, 0:2, :], ALU.mult)
                        nc.vector.tensor_tensor(kd, kd, kk, ALU.mult).then_inc(qe_v.sem, 1)
                    if n >= 1:
                        place(n - 1)
                place(13)
                if d == 0:
                    dve_squares(dve, layer, 0, 512)
                else:
                    dve_gated(dve, layer, 0, 512, dz[:, :, 0:256])
                seq = order(d)
                link(nc.vector.memset(Sh[:, seq[0], :, :], 0.0))
                dve.wait_ge(uhev.sem, uhev.n(layer, 6 * d + 6))
                for n in range(NCH - 1):
                    for pair in range(2):
                        ins = nc.vector.scalar_tensor_tensor(Sh[:, seq[n + 1], pair, :], Sh[:, seq[n], pair, :],
                                                             ec[:, pair, seq[n]:seq[n] + 1], Uh[:, seq[n], pair, :],
                                                             ALU.mult, ALU.add)
                    if n < NCH - 2:
                        link(ins)
                ins.then_inc(hstate.sem, 1)
                outs = list(out_tiles(layer))
                for n, i in enumerate(outs):
                    dve.wait_ge(hout.sem, hout.n(layer, len(outs) * d + n + 1))
                    y = ycat[:, i, 768:1024]
                    for hb in range(2):
                        dst = y.rearrange("p (b h t) -> p b h t", b=2, h=2)[:, :, hb, :]
                        src = ps[:, 2 * (i % 2) + hb, 0:128].rearrange("p (b t) -> p b t", b=2)
                        if d == 0:
                            ins = nc.vector.tensor_copy(dst, src)
                        else:
                            ins = nc.vector.tensor_tensor(dst, dst, src, ALU.add)
                    link(ins)
                    nc.vector.tensor_tensor(y, y, ps[:, 4 + i % 2, 0:256], ALU.add).then_inc(houtv.sem, 1)
                dve.wait_ge(houtv.sem, houtv.n(layer, len(outs) * (d + 1)))
            dve_squares(dve, layer, 1, 768)
            dve_gated(dve, layer, 1, 768, hgt[:, :, 256:512])
            nc.vector.memset(ss[:, 60:61], 0.0).then_inc(mixed.sem, 1)

        def act_hgrn(act, layer):
            for d in range(2):
                f = hgc[:, 2 + 2 * d:4 + 2 * d, :]
                if d == 1:
                    act.wait_ge(houtv.sem, houtv.n(layer, len(out_tiles(layer))))
                else:
                    act.wait_ge(outv.sem, outv.n(layer, 2 * len(out_tiles(layer))))
                act.wait_ge(f_v.sem, f_v.n(layer, 4))
                for j in range(2):
                    ins = nc.scalar.activation(gpad[:, j, :, 1:CHUNK + 1],
                                               f[:, j, :].rearrange("p (c t) -> p c t", c=NCH), ACT.Ln)
                ins.then_inc(g_a.sem, 1)
                off = 1 - d

                def exps(n):
                    act.wait_ge(zsub.sem, zsub.n(layer, 12 * d + n + 1))
                    nc.scalar.activation(Z[n % 4], Z[n % 4], ACT.Exp).then_inc(zexp.sem, 1)

                act.wait_ge(er_v.sem, er_v.n(layer, d + 1))
                exps(0)
                for j in range(2):
                    nc.scalar.activation(ED[:, j].rearrange("p (c t) -> p c t", c=NCH), Cc[:, j, :, off:off + CHUNK],
                                         ACT.Exp)
                nc.scalar.activation(ec[:, :, :], Cc[:, :, :, CHUNK:CHUNK + 1].rearrange("p j c o -> p j (c o)"), ACT.Exp)
                nc.scalar.activation(ER, ER, ACT.Exp).then_inc(er_a.sem, 1)
                for n in range(1, 12):
                    exps(n)
                for i in range(NT):
                    act.wait_ge(kett.sem, kett.n(layer, 6 * d + i + 1))
                    nc.scalar.activation(ket[:, i, :], ps[:, 6 + i % 2, 0:256], ACT.Copy).then_inc(ketev.sem, 1)
                for i in range(NT):
                    act.wait_ge(umh.sem, umh.n(layer, 6 * d + i + 1))
                    for par in range(2):
                        ins = nc.scalar.activation(Uh[:, 2 * i + par, :, :],
                                                   ps[:, 2 * (i % 2) + par, 0:128].rearrange("p (b t) -> p b t", b=2),
                                                   ACT.Copy)
                    ins.then_inc(uhev.sem, 1)
                act_gated(act, layer, d)

        def pe_hgrn(pe, layer):
            pe.wait_ge(outv.sem, outv.n(layer, 2 * len(out_tiles(layer))))
            for d in range(2):
                for n in range(14):
                    level, j = divmod(n, 2)
                    if n < 12:
                        pe.wait_ge(zmul.sem, zmul.n(layer, 12 * d + n + 1))
                    if n >= 3:
                        pe.wait_ge(hpred.sem, hpred.n(layer, 14 * d + n - 2))
                    for hb in range(2):
                        for c in range(NCH):
                            sl = slice(c * CHUNK, (c + 1) * CHUNK)
                            if n < 12:
                                a = b = Z[n % 4][HB[hb], sl]
                            else:
                                a, b = kk[HB[hb], j, sl], hgc[HB[hb], j, sl]
                            ins = nc.tensor.matmul(ps[HB[c % 2], 2 * (n % 3) + hb, c // 2 * HD:c // 2 * HD + HD],
                                                   lhsT=a, rhs=b, start=True, stop=True)
                    ins.then_inc(hgram.sem, 1)
                pe.wait_ge(qe_v.sem, qe_v.n(layer, d + 1))
                kd = ER if d == 0 else ED
                qd = ED if d == 0 else ER
                for i in range(NT):
                    if i >= 2:
                        pe.wait_ge(ketev.sem, ketev.n(layer, 6 * d + i - 1))
                    for j in range(2):
                        ins = nc.tensor.transpose(ps[:, 6 + i % 2, j * P:(j + 1) * P], kd[:, j, i * P:(i + 1) * P], ident)
                    ins.then_inc(kett.sem, 1)
                pe.wait_ge(hpred.sem, hpred.n(layer, 14 * d + 14))
                for i in range(NT):
                    pe.wait_ge(ketev.sem, ketev.n(layer, 6 * d + i + 1))
                    if i >= 2:
                        pe.wait_ge(uhev.sem, uhev.n(layer, 6 * d + i - 1))
                    for par in range(2):
                        for h in range(DNH):
                            hb, pair = h % 2, h // 2
                            ins = nc.tensor.matmul(ps[HB[hb], 2 * (i % 2) + par, HD * pair:HD * pair + HD],
                                                   lhsT=ket[HB[par], i, h * HD:(h + 1) * HD],
                                                   rhs=hgt[HB[par], i, h * HD:(h + 1) * HD], start=True, stop=True)
                    ins.then_inc(umh.sem, 1)
                pe.wait_ge(hstate.sem, hstate.n(layer, d + 1))
                outs = list(out_tiles(layer))
                for n, i in enumerate(outs):
                    if n >= 2:
                        pe.wait_ge(houtv.sem, houtv.n(layer, len(outs) * d + n - 1))
                    for par in range(2):
                        c = 2 * i + par
                        for h in range(DNH):
                            hb, pair = h % 2, h // 2
                            nc.tensor.matmul(ps[HB[par], 2 * (i % 2) + hb, HD * pair:HD * pair + HD],
                                             lhsT=qd[HB[hb], pair, c * CHUNK:(c + 1) * CHUNK],
                                             rhs=Sh[HB[hb], c, pair, :], start=True, stop=True)
                            ins = nc.tensor.matmul(ps[HB[par], 4 + i % 2, HD * h:HD * h + HD],
                                                   lhsT=Ah[HB[par], h, i, :], rhs=hgt[HB[par], i, h * HD:(h + 1) * HD],
                                                   start=True, stop=True)
                    ins.then_inc(hout.sem, 1)
                pe.wait_ge(houtv.sem, houtv.n(layer, len(outs) * (d + 1)))

        def pe_out(pe, layer):
            outs = list(out_tiles(layer))
            for f in range(KT):
                if f == 6:
                    pe.wait_ge(mixed.sem, mixed.n(layer, 1))
                if f >= 3:
                    pe.wait_ge(yt_a.sem, yt_a.n(layer, f - 2))
                for i in outs:
                    ins = nc.tensor.transpose(ps[:, 2 * (f % 3) + i // 4, (i % 4) * P:(i % 4 + 1) * P],
                                              ycat[:, i, f * P:(f + 1) * P], ident)
                ins.then_inc(yt.sem, 1)
            for n in range(4):
                v, half = divmod(n, 2)
                if n >= 2:
                    pe.wait_ge(gbev.sem, gbev.n(layer, n - 1))
                nc.tensor.matmul(ps[:, 6 + n % 2, :], lhsT=sel2[:, v, :], rhs=gates[:, 0, half * 512:half * 512 + 512],
                                 start=True, stop=True).then_inc(gbmm.sem, 1)
            pe.wait_ge(yt_a.sem, yt_a.n(layer, 6))
            pe.wait_ge(yt_v.sem, yt_v.n(layer, 2))
            for g in range(2):
                w = staged(pe, layer, N_MOD + len(GROUPS) + g)
                for n, i in enumerate(outs):
                    u = len(outs) * g + n
                    if u >= 6:
                        pe.wait_ge(wov.sem, wov.n(layer, u - 5))
                    for f in range(KT):
                        ins = nc.tensor.matmul(ps[:, u % 6, :], lhsT=yT[:, f, i * P:(i + 1) * P], rhs=w[:, f, :],
                                               start=(f == 0), stop=(f == KT - 1))
                    ins.then_inc(wo.sem, 1)
                pe.wait_ge(wo.sem, wo.n(layer, len(outs) * (g + 1)))
                pe.sem_inc(wfree.sem, 1)

        def act_out(act, layer):
            for f in range(6):
                act.wait_ge(yt.sem, yt.n(layer, f + 1))
                b = 2 * (f % 3)
                c0 = out_tiles(layer)[0] * P
                nc.scalar.activation(yT[:, f, c0:512], ps[:, b, c0:512], ACT.Copy)
                nc.scalar.activation(yT[:, f, 512:768], ps[:, b + 1, 0:256], ACT.Copy).then_inc(yt_a.sem, 1)
            for n in range(4):
                v, half = divmod(n, 2)
                act.wait_ge(gbmm.sem, gbmm.n(layer, n + 1))
                nc.scalar.activation(gbc[:, v, half * 512:half * 512 + 512], ps[:, 6 + n % 2, :], ACT.Copy) \
                    .then_inc(gbev.sem, 1)

        def dve_out(dve, layer):
            for f in range(6, KT):
                dve.wait_ge(yt.sem, yt.n(layer, f + 1))
                b = 2 * (f % 3)
                c0 = out_tiles(layer)[0] * P
                nc.vector.tensor_copy(yT[:, f, c0:512], ps[:, b, c0:512])
                nc.vector.tensor_copy(yT[:, f, 512:768], ps[:, b + 1, 0:256]).then_inc(yt_v.sem, 1)
            dve.wait_ge(gbev.sem, gbev.n(layer, 4))
            outs = list(out_tiles(layer))
            for u in range(2 * len(outs)):
                g, i = u // len(outs), outs[u % len(outs)]
                v = 1 if i < NT_CTX else 0
                dve.wait_ge(wo.sem, wo.n(layer, u + 1))
                if u >= 2:
                    dve.wait_ge(wov.sem, wov.n(layer, u - 1))
                link(nc.vector.tensor_tensor(otmp2[u % 2], ps[:, u % 6, :], gbc[:, v, g * 512:g * 512 + 512], ALU.mult))
                xs = x[:, i, g * 512:g * 512 + 512]
                nc.vector.tensor_tensor(xs, xs, otmp2[u % 2], ALU.add).then_inc(wov.sem, 1)

        def sp_experts(sp, layer):
            wg, wu, wd = t["moe_w_gate"], t["moe_w_up"], t["moe_w_down"]

            def gate_up(e, k):
                if k >= 4 or not isinstance(e, int) or e > 0:
                    sp.wait_ge(gufree.sem, e * 16 + (layer * 256 + 2 * k - 6))
                for part in range(2):
                    m, row = divmod(2 * k + part, KT)
                    src = (wg, wu)[m][layer, bass.ds(e, 1), row * P:(row + 1) * P, :].rearrange("e p n -> p (e n)")
                    sp.dma_start(gu[k % 4][:, part, :], src).then_inc(guld[k % 4].sem, 16)

            def downs(e, n):
                r0, r1 = 4 * n, min(4 * n + 4, FT)
                if not isinstance(e, int) or e > 0:
                    sp.wait_ge(dmm.sem, e * FT + (layer * NE * FT + r1 - FT))
                src = wd[layer, bass.ds(e, 1), r0 * P:r1 * P, :].rearrange("e (r p) n -> p (e r) n", p=P)
                sp.dma_start(down[:, r0:r1, :], src).then_inc(dld[n].sem, 16)

            sp.wait_ge(wov.sem, wov.n(layer, 2 * len(out_tiles(layer))))
            for k in range(8):
                gate_up(0, k)
            sp.wait_ge(logit.sem, logit.n(layer, 1))
            for n in range(3):
                downs(0, n)
            with sp.Fori(1, NE) as e:
                for k in range(4):
                    gate_up(e, k)
                for n in range(3):
                    downs(e, n)
                for k in range(4, 8):
                    gate_up(e, k)

        def expert_shape(layer):
            tiles = list(out_tiles(layer))
            seqs = [((NT_CTX, NT), CAP_L, 0), ((0, NT_CTX), CAP_C, CAP_L)][:1 if layer == DEPTH - 1 else 2]
            return tiles, seqs, sum(cap for _, cap, _ in seqs)

        def pe_experts(pe, layer):
            tiles, seqs, rows_e = expert_shape(layer)
            banks = SCATTER_BANKS[2 * len(tiles)]
            pe.wait_ge(hT_a.sem, hT_a.n(layer, 8))
            pe.wait_ge(hT_v.sem, hT_v.n(layer, 8))
            for bank, c0, n in ((6, CTX, LAT), (7, 0, CTX))[:2 if tiles[0] == 0 else 1]:
                for f in range(KT):
                    ins = nc.tensor.matmul(ps[0:NE, bank, 0:n], lhsT=rw[:, layer, f, :], rhs=hT2[:, f, c0:c0 + n],
                                           start=(f == 0), stop=(f == KT - 1))
            ins.then_inc(logitT.sem, 1)
            for half in range(2):
                ins = nc.tensor.matmul(ps[0:CAP, half, :], lhsT=selM[:, :], rhs=gates[:, 1, half * 512:half * 512 + 512],
                                       start=True, stop=True)
            ins.then_inc(gm_mm.sem, 1)
            pe.wait_ge(logitT_v.sem, logitT_v.n(layer, 1))
            for i in tiles:
                ins = nc.tensor.transpose(ps[:, 4, i * NE:(i + 1) * NE], affT[0:NE, i * P:(i + 1) * P],
                                          ident[0:NE, 0:NE])
            ins.then_inc(logit.sem, 1)
            pe.wait_ge(affr.sem, affr.n(layer, 1))
            for i in range(NT):
                bank, c0 = (7, i * P) if i < NT_CTX else (5, (i - NT_CTX) * P)
                ins = nc.tensor.transpose(ps[0:NE, bank, c0:c0 + P], aff[:, i, 0:NE], ident)
            ins.then_inc(affTm.sem, 1)
            pe.wait_ge(gm_v.sem, gm_v.n(layer, 1))

            def spread(e):
                pe.wait_ge(affm_v.sem, e + (affm_v.n(layer, 1)))
                ins = nc.tensor.matmul(ps[:, 6, :], lhsT=ones16[:, :], rhs=affm[0:NE, CTX:TOK], start=True, stop=True)
                if tiles[0] == 0:
                    ins = nc.tensor.matmul(ps[:, 7, 0:CTX], lhsT=ones16[:, :], rhs=affm[0:NE, 0:CTX], start=True,
                                           stop=True)
                ins.then_inc(bc_mm.sem, 1)

            def gather(e):
                pe.wait_ge(picked.sem, e + picked.n(layer, 1))
                for f in range(KT):
                    bank, c0 = 6 + f // 4, (f % 4) * P
                    for (i0, i1), cap, off in seqs:
                        for i in range(i0, i1):
                            ins = nc.tensor.matmul(ps[:, bank, c0 + off:c0 + off + cap],
                                                   lhsT=xn2[:, i, f * P:(f + 1) * P], rhs=Gm[:, i, off:off + cap],
                                                   start=(i == i0), stop=(i == i1 - 1))
                    if f % 4 == 3:
                        ins.then_inc(gath.sem, 1)

            def turn_choice(e):
                for i in tiles:
                    nc.tensor.transpose(ps[0:CAP, 3 + i // 4, (i % 4) * P:(i % 4 + 1) * P], Gm[:, i, :], ident)
                for i in tiles:
                    ins = nc.tensor.matmul(ps[0:rows_e, 4, 256:257], lhsT=Gm[:, i, 0:rows_e], rhs=affe[:, i:i + 1],
                                           start=(i == tiles[0]), stop=(i == tiles[-1]))
                ins.then_inc(wtm.sem, 1)

            def lo_ready(e, item):
                if item in POOL_ITEMS:
                    n = len(POOL_ITEMS)
                    pe.wait_ge(lo_p.sem, e * n + (layer * 16 * n + POOL_ITEMS.index(item) + 1))
                else:
                    n = 2 * KT - len(POOL_ITEMS)
                    pe.wait_ge(lo_v.sem, e * n + (layer * 16 * n + item + 1 - sum(p < item for p in POOL_ITEMS)))

            pe.sem_inc(scm.sem, 1)
            spread(0)
            gather(0)
            turn_choice(0)
            with pe.Fori(0, NE) as e:
                for item in range(2 * KT):
                    m, row = divmod(item, KT)
                    slot, part = item // 2 % 4, item % 2
                    if item == 0:
                        pe.wait_ge(xe_v.sem, e + xe_v.n(layer, 1))
                    if item == 4:
                        pe.wait_ge(scv.sem, e * len(banks) + scv.n(layer, 1))
                        spread(e + 1)
                    if item == KT:
                        pe.wait_ge(wta.sem, e + wta.n(layer, 1))
                    pe.wait_ge(hi_a.sem, e * 16 + (layer * 256 + item + 1))
                    hi, lo = gu_hi[item % 4], gu_lo[slot][:, part, :]
                    x_hi, x_lo = (xsplit[:, row, part_x, 0:rows_e] for part_x in range(2))
                    passes = [(x_hi, hi), (x_lo, hi), (x_hi, lo)]
                    for n_pass, (lhs, w_part) in enumerate(passes):
                        if n_pass == len(passes) - 1:
                            lo_ready(e, item)
                        for b in range(3):
                            n = min(512, FF - 512 * b)
                            ins = nc.tensor.matmul(ps[0:rows_e, 3 * m + b, 0:n], lhsT=lhs,
                                                   rhs=w_part[:, 512 * b:512 * b + n],
                                                   start=(row == 0 and n_pass == 0),
                                                   stop=(row == KT - 1 and n_pass == len(passes) - 1))
                    ins.then_inc(gufree.sem, 1)
                for b in range(3):
                    pe.wait_ge(h_v.sem, e * 3 + (layer * 48 + b + 1))
                    for ft in range(4 * b, min(4 * b + 4, FT)):
                        ins = nc.tensor.transpose(ps[:, b, (ft % 4) * CAP:(ft % 4 + 1) * CAP],
                                                  sg[0:CAP, ft * P:(ft + 1) * P], ident[0:CAP, 0:CAP])
                    ins.then_inc(htm.sem, 1)
                for ft in range(FT):
                    if ft % 4 == 0:
                        pe.wait_ge(hta.sem, e * 3 + (layer * 48 + ft // 4 + 1))
                    pe.wait_ge(dhi_a.sem, e * FT + (layer * NE * FT + ft + 1))
                    h_hi, h_lo = hTm[:, ft, 0:rows_e], hTm_lo[:, ft, 0:rows_e]
                    hi, lo = gu_hi[ft % 4][:, 0:D], down_lo[:, ft, :]
                    for n_pass, (lhs, w_part) in enumerate(((h_hi, hi), (h_lo, hi), (h_hi, lo))):
                        if n_pass == 1 and ft % 4 == 0:
                            pe.wait_ge(hTl.sem, e * 3 + (layer * 48 + ft // 4 + 1))
                        if n_pass == 2:
                            if ft in POOL_DOWN:
                                n = len(POOL_DOWN)
                                pe.wait_ge(dlo_p.sem, e * n + (layer * NE * n + POOL_DOWN.index(ft) + 1))
                            else:
                                n = FT - len(POOL_DOWN)
                                pe.wait_ge(dlo_v.sem, e * n + (layer * NE * n + ft + 1 - sum(q < ft for q in POOL_DOWN)))
                        for half in range(2):
                            ins = nc.tensor.matmul(ps[0:rows_e, 3 + half, :], lhsT=lhs,
                                                   rhs=w_part[:, half * 512:half * 512 + 512],
                                                   start=(ft == 0 and n_pass == 0), stop=(ft == FT - 1 and n_pass == 2))
                    ins.then_inc(dmm.sem, 1)
                gather(e + 1)
                pe.wait_ge(ye_v.sem, e * 6 + (layer * 96 + 2))
                turn_choice(e + 1)
                for u in range(2 * len(tiles)):
                    half, i = divmod(u, len(tiles))
                    if i == 0:
                        pe.wait_ge(ye_v.sem, e * 6 + (layer * 96 + half + 5))
                    if banks[u] in banks[:u]:
                        last = u - 1 - banks[:u][::-1].index(banks[u])
                        pe.wait_ge(scv.sem, e * len(banks) + scv.n(layer, last + 2))
                    if banks[u] == 6:
                        pe.wait_ge(xe_a.sem, e * 2 + xe_a.n(layer, 4))
                    for part, y in enumerate((ye_hi, ye_lo)):
                        ins = nc.tensor.matmul(ps[:, banks[u], :], lhsT=WT[0:rows_e, tiles[i], :],
                                               rhs=y[0:rows_e, half * 512:half * 512 + 512], start=(part == 0),
                                               stop=(part == 1))
                    ins.then_inc(scm.sem, 1)
                pe.wait_ge(scv.sem, e * len(banks) + scv.n(layer, 1 + banks.index(5)))

        def act_experts(act, layer):
            tiles, seqs, rows_e = expert_shape(layer)
            act.wait_ge(aff_v.sem, aff_v.n(layer, 1))
            nc.scalar.activation(aff[:, :, 0:NE], aff[:, :, 0:NE], ACT.Exp).then_inc(aff_a.sem, 1)

            def gathered(e):
                for half in range(2):
                    act.wait_ge(gath.sem, e * 2 + gath.n(layer, half + 1))
                    for f in range(4 * half, 4 * half + 4):
                        for v, (_, n, c0) in enumerate(seqs):
                            ins = nc.scalar.activation(xe[:, f, c0:c0 + n],
                                                       ps[:, 6 + half, (f % 4) * P + c0:(f % 4) * P + c0 + n],
                                                       ACT.Identity, scale=modC[:, 3, f, v:v + 1],
                                                       bias=modC[:, 2, f, v:v + 1])
                    ins.then_inc(xe_w.sem, 1)
                for half in range(2):
                    act.wait_ge(xe_w.sem, e * 2 + xe_w.n(layer, half + 1))
                    fs = slice(4 * half, 4 * half + 4)
                    nc.scalar.activation(xsplit[:, fs, 0, 0:rows_e], xe[:, fs, 0:rows_e], ACT.Copy).then_inc(xe_a.sem, 1)

            def turned(e):
                act.wait_ge(wtm.sem, e + wtm.n(layer, 1))
                act.wait_ge(scm.sem, e * (2 * len(tiles)) + scm.n(layer, 1))
                i0 = tiles[0]
                nc.scalar.activation(WT[0:rows_e, i0:4, :].rearrange("p i t -> p (i t)"),
                                     ps[0:rows_e, 3, i0 * P:4 * P], ACT.Copy)
                nc.scalar.activation(WT[0:rows_e, 4:6, :].rearrange("p i t -> p (i t)"), ps[0:rows_e, 4, 0:256], ACT.Copy)
                nc.scalar.activation(w_slot[0:rows_e, :], ps[0:rows_e, 4, 256:257], ACT.Copy).then_inc(wta.sem, 1)

            def hi_parts(e, items):
                for item in items:
                    k, part = divmod(item, 2)
                    if part == 0:
                        act.wait_ge(guld[k % 4].sem, e * 64 + (layer * 1024 + 32 * (k // 4 + 1)))
                    if item > 3:
                        act.wait_ge(gufree.sem, e * 16 + (layer * 256 + item - 3))
                    elif not isinstance(e, int):
                        act.wait_ge(dmm.sem, e * FT + (layer * NE * FT - (3 if item == 3 else 2 - item)))
                    nc.scalar.activation(gu_hi[item % 4], gu[k % 4][:, part, :], ACT.Copy).then_inc(hi_a.sem, 1)

            def down_hi(e, items):
                for ft in items:
                    if ft % 4 == 0:
                        act.wait_ge(dld[ft // 4].sem, e * 16 + (layer * 256 + 16))
                    if ft < 4:
                        act.wait_ge(gufree.sem, e * 16 + (layer * 256 + 13 + ft))
                    else:
                        act.wait_ge(dmm.sem, e * FT + (layer * NE * FT + ft - 3))
                    nc.scalar.activation(gu_hi[ft % 4][:, 0:D], down[:, ft, :], ACT.Copy).then_inc(dhi_a.sem, 1)

            def expert(e, is_last):
                turned(e)
                hi_parts(e, range(4, 12))
                act.wait_ge(gufree.sem, e * 16 + (layer * 256 + KT))
                cols = [slice(512 * b, min(512 * b + 512, FF)) for b in range(3)]
                for b in range(3):
                    n = cols[b].stop - cols[b].start
                    nc.scalar.activation(sg[0:rows_e, cols[b]], ps[0:rows_e, b, 0:n], ACT.Silu).then_inc(h_a.sem, 1)
                hi_parts(e, range(12, 16))
                down_hi(e, range(2))
                for b in range(3):
                    act.wait_ge(htm.sem, e * 3 + (layer * 48 + b + 1))
                    nt = min(4, FT - 4 * b)
                    nc.scalar.activation(hTm[:, 4 * b:4 * b + nt, 0:rows_e],
                                         ps[:, b, 0:nt * CAP].rearrange("p (f c) -> p f c", c=CAP)[:, :, 0:rows_e],
                                         ACT.Copy).then_inc(hta.sem, 1)
                down_hi(e, range(2, FT))
                if not is_last:
                    hi_parts(e + 1, range(4))
                gathered(e + 1)

            gathered(0)
            hi_parts(0, range(4))
            with act.Fori(0, NE - 1) as e:
                expert(e, False)
            expert(NE - 1, True)

        def dve_experts(dve, layer):
            tiles, seqs, rows_e = expert_shape(layer)
            banks = SCATTER_BANKS[2 * len(tiles)]
            nc.vector.memset(aff[:, :, NE:NE + 1], 0.0)
            nc.vector.memset(rk[:, :, :], 0.0)
            link(nc.vector.memset(Gm, 0.0))
            dve.sem_inc(scv.sem, 1)
            dve.wait_ge(logitT.sem, logitT.n(layer, 1))
            if tiles[0] == 0:
                nc.vector.tensor_copy(affT[0:NE, 0:CTX], ps[0:NE, 7, 0:CTX])
            nc.vector.tensor_copy(affT[0:NE, CTX:TOK], ps[0:NE, 6, :]).then_inc(logitT_v.sem, 1)
            t0, nt = tiles[0], len(tiles)
            dve.wait_ge(logit.sem, logit.n(layer, 1))
            lg = ps[:, 4, t0 * NE:NT * NE].rearrange("p (i e) -> p i e", e=NE)
            link(nc.vector.tensor_reduce(lmax[:, t0:NT], lg, AX, ALU.max))
            nc.vector.tensor_tensor(aff[:, t0:NT, 0:NE], lg, lmax[:, t0:NT].unsqueeze(2).broadcast_to([P, nt, NE]),
                                    ALU.subtract).then_inc(aff_v.sem, 1)
            dve.wait_ge(gm_mm.sem, gm_mm.n(layer, 1))
            nc.vector.tensor_copy(gateM[0:CAP, 0:512], ps[0:CAP, 0, :])
            nc.vector.tensor_copy(gateM[0:CAP, 512:1024], ps[0:CAP, 1, :])
            dve.wait_ge(aff_a.sem, aff_a.n(layer, 1))
            link(nc.vector.tensor_reduce(lmax[:, :], aff[:, :, 0:NE], AX, ALU.add))
            link(nc.vector.reciprocal(lmax[:, :], lmax[:, :]))
            nc.vector.tensor_tensor(aff[:, :, 0:NE], aff[:, :, 0:NE], lmax[:, :].unsqueeze(2).broadcast_to([P, NT, NE]),
                                    ALU.mult).then_inc(affr.sem, 1)
            dve.wait_ge(affTm.sem, affTm.n(layer, 1))
            nc.vector.tensor_copy(affT[0:NE, 0:CTX], ps[0:NE, 7, 0:CTX])
            link(nc.vector.tensor_copy(affT[0:NE, CTX:TOK], ps[0:NE, 5, :]))
            nc.vector.memset(ss[:, 61:62], 0.0).then_inc(gm_v.sem, 1)

            state = {}

            def link2(ins):
                state["n"] += 1
                ins.then_inc(cstep.sem, 1)
                dve.wait_ge(cstep.sem, state["e"] * choose_steps(layer)
                            + (layer * choose_steps(0) * (NE + 1) + state["n"]))

            def own_affinity(e):
                state["n"], state["e"] = 0, e
                if not isinstance(e, int):
                    dve.wait_ge(bc_mm.sem, e + (bc_mm.n(layer, 0)))
                    dve.wait_ge(wtm.sem, e + wtm.n(layer, 0))
                nc.vector.tensor_scalar(affm[0:NE, :], affT[0:NE, :], ident[0:NE, bass.ds(e, 1)], None, ALU.mult) \
                    .then_inc(affm_v.sem, 1)
                link2(nc.vector.tensor_copy(affe[:, :], aff[:, :, bass.ds(e, 1)].rearrange("p i e -> p (i e)")))

            def rank_tile(e, i):
                if i == tiles[0]:
                    dve.wait_ge(bc_mm.sem, e + bc_mm.n(layer, 1))
                bank, hi, me = (7, NT_CTX, i) if i < NT_CTX else (6, NT_LAT, i - NT_CTX)
                own = affe[:, i:i + 1]
                if me > 0:
                    link2(nc.vector.tensor_scalar(rjunk[:, 0:me * P], ps[:, bank, 0:me * P], own, None, ALU.is_ge,
                                                  ALU.add, accum_out=rk[:, i, 0:1]))
                if me < hi - 1:
                    link2(nc.vector.tensor_scalar(rjunk[:, 0:(hi - 1 - me) * P], ps[:, bank, (me + 1) * P:hi * P],
                                                  own, None, ALU.is_gt, ALU.add, accum_out=rk[:, i, 1:2]))
                for n, (op, m) in enumerate(((ALU.is_ge, "before"), (ALU.is_gt, "after"))):
                    link2(nc.vector.scalar_tensor_tensor(rjunk[:, 0:P], ps[:, bank, me * P:(me + 1) * P], own,
                                                         cst(m), op, ALU.mult, accum_out=rk[:, i, 2 + n:3 + n]))

            def pick(e):
                link2(nc.vector.tensor_reduce(rank[:, :], rk[:, :, :], AX, ALU.add))
                assert state["n"] == choose_steps(layer), state["n"]
                for i in tiles:
                    cap, off = (CAP_C, CAP_L) if i < NT_CTX else (CAP_L, 0)
                    ins = nc.vector.tensor_scalar(Gm[:, i, off:off + cap], cst("iota")[:, 0:cap], rank[:, i:i + 1], None,
                                                  ALU.is_equal)
                ins.then_inc(picked.sem, 1)

            own_affinity(0)
            for i in tiles:
                rank_tile(0, i)
            pick(0)
            with dve.Fori(0, NE) as e:
                own_affinity(e + 1)
                cols = [slice(512 * b, min(512 * b + 512, FF)) for b in range(3)]
                n_own = 0
                for item in range(2 * KT):
                    if item in POOL_ITEMS:
                        continue
                    k, part = divmod(item, 2)
                    dve.wait_ge(hi_a.sem, e * 16 + (layer * 256 + item + 1))
                    nc.vector.tensor_tensor(gu_lo[k % 4][:, part, :], gu[k % 4][:, part, :],
                                            gu_hi[item % 4].bitcast(F32), ALU.subtract).then_inc(lo_v.sem, 1)
                    if 3 <= n_own < 3 + len(tiles):
                        rank_tile(e + 1, tiles[n_own - 3])
                    if n_own == 3 + len(tiles):
                        pick(e + 1)
                    n_own += 1
                dve.wait_ge(gufree.sem, e * 16 + (layer * 256 + 16))
                for b in range(3):
                    n = cols[b].stop - cols[b].start
                    dve.wait_ge(h_a.sem, e * 3 + (layer * 48 + b + 1))
                    nc.vector.tensor_tensor(sg[0:rows_e, cols[b]], sg[0:rows_e, cols[b]], ps[0:rows_e, 3 + b, 0:n],
                                            ALU.mult).then_inc(h_v.sem, 1)
                for ft in range(FT):
                    if ft not in POOL_DOWN:
                        dve.wait_ge(dhi_a.sem, e * FT + (layer * NE * FT + ft + 1))
                        nc.vector.tensor_tensor(down_lo[:, ft, :], down[:, ft, :], gu_hi[ft % 4][:, 0:D].bitcast(F32),
                                                ALU.subtract).then_inc(dlo_v.sem, 1)
                    if ft == 0:
                        for b in range(3):
                            dve.wait_ge(hta.sem, e * 3 + (layer * 48 + b + 1))
                            nt = min(4, FT - 4 * b)
                            src = ps[:, b, 0:nt * CAP].rearrange("p (f c) -> p f c", c=CAP)[:, :, 0:rows_e]
                            nc.vector.tensor_tensor(hTm_lo[:, 4 * b:4 * b + nt, 0:rows_e], src,
                                                    hTm[:, 4 * b:4 * b + nt, 0:rows_e].bitcast(F32), ALU.subtract) \
                                .then_inc(hTl.sem, 1)
                dve.wait_ge(dmm.sem, e * FT + (layer * NE * FT + FT))
                halves_e = [slice(512 * half, 512 * half + 512) for half in range(2)]
                for half, cols in enumerate(halves_e):
                    nc.vector.scalar_tensor_tensor(ye[0:rows_e, cols], ps[0:rows_e, 3 + half, :], w_slot[0:rows_e, :],
                                                   gateM[0:rows_e, cols], ALU.mult, ALU.mult).then_inc(ye_v.sem, 1)
                for half, cols in enumerate(halves_e):
                    dve.wait_ge(ye_v.sem, e * 6 + (layer * 96 + half + 1))
                    nc.vector.tensor_copy(ye_hi[0:rows_e, cols], ye[0:rows_e, cols]).then_inc(ye_v.sem, 1)
                for half, cols in enumerate(halves_e):
                    dve.wait_ge(ye_v.sem, e * 6 + (layer * 96 + half + 3))
                    nc.vector.tensor_tensor(ye_lo[0:rows_e, cols], ye[0:rows_e, cols], ye_hi[0:rows_e, cols].bitcast(F32),
                                            ALU.subtract).then_inc(ye_v.sem, 1)
                for u in range(2 * len(tiles)):
                    half, i = divmod(u, len(tiles))
                    dve.wait_ge(scm.sem, e * len(banks) + scm.n(layer, u + 2))
                    xs = x[:, tiles[i], half * 512:half * 512 + 512]
                    nc.vector.tensor_tensor(xs, xs, ps[:, banks[u], :], ALU.add).then_inc(scv.sem, 1)

        def pool_program(pool):
            for layer in range(DEPTH):
                rows_e = expert_shape(layer)[2]
                with pool.Fori(0, NE) as e:
                    for item in POOL_ITEMS:
                        k, part = divmod(item, 2)
                        pool.wait_ge(hi_a.sem, e * 16 + (layer * 256 + item + 1))
                        nc.gpsimd.tensor_tensor(gu_lo[k % 4][:, part, :], gu[k % 4][:, part, :], gu_hi[item % 4].bitcast(F32),
                                                ALU.subtract).then_inc(lo_p.sem, 1)
                        if item == 1:
                            pool.wait_ge(xe_a.sem, e * 2 + xe_a.n(layer, 2))
                            nc.gpsimd.tensor_tensor(xsplit[:, :, 1, 0:rows_e], xe[:, :, 0:rows_e],
                                                    xsplit[:, :, 0, 0:rows_e].bitcast(F32), ALU.subtract) \
                                .then_inc(xe_v.sem, 1)
                    for ft in POOL_DOWN:
                        pool.wait_ge(dhi_a.sem, e * FT + (layer * NE * FT + ft + 1))
                        nc.gpsimd.tensor_tensor(down_lo[:, ft, :], down[:, ft, :], gu_hi[ft % 4][:, 0:D].bitcast(F32),
                                                ALU.subtract).then_inc(dlo_p.sem, 1)

        block = ctx.enter_context(nc.Block())
        block.sync(sync_program)
        block.scalar(scalar_program)
        block.tensor(tensor_program)
        block.vector(vector_program)
        block.gpsimd(pool_program)


INPUTS = ["x", "c", "ctx", "c_ctx", "w_mod", "b_mod", "w_in", "w_out", "attn_q_norm", "attn_k_norm", "dn_conv",
          "dn_a_log", "dn_dt_bias", "dn_norm", "hg_lower_bounds", "hg_norm", "moe_router", "moe_w_gate", "moe_w_up",
          "moe_w_down"]


def kernel(**inputs):
    import concourse.bacc as bacc
    from concourse.bass_utils import run_bass_kernel_spmd

    nc = bacc.Bacc("TRN2", target_bir_lowering=False, num_devices=1, dynamic_dma_scratch_size=1024)
    arrays, t = {}, {}
    for name in INPUTS + ["consts"]:
        a = constants() if name == "consts" else np.ascontiguousarray(inputs[name])
        arrays[f"in_{name}"] = a
        t[name] = nc.dram_tensor(f"in_{name}", a.shape, mybir.dt.from_np(a.dtype), kind="ExternalInput").ap()
    t["out"] = nc.dram_tensor("out_0", (1, LAT, D), F32, kind="ExternalOutput").ap()
    trunk_program(nc, t)
    r = run_bass_kernel_spmd(nc, [arrays], core_ids=[0])
    return r.results[0]["out_0"]
```
